# Optimizing a Trainium2 kernel written in Bass

```python
import math
import jax, jax.numpy as jnp
from jax import lax
import numpy as np

D_MODEL = 1024
BATCH = 1
SEQ = 256
DEPTH = 2

EPS = 1e-6
HEAD_DIM = 64
Q_BLOCK = 128
LRU_WIDTH = 512
LRU_BLOCKS = 8
LRU_BLOCK = LRU_WIDTH // LRU_BLOCKS
CONV_WIDTH = 4
LRU_C = 8.0
NSA_HEADS = 8
NSA_KV_GROUPS = 2
NSA_HPG = NSA_HEADS // NSA_KV_GROUPS
CMP_LEN = 32
CMP_STRIDE = 16
CMP_HIDDEN = 128
SLC_LEN = 64
SLC_TOPN = 8
WIN = 512
FORCE_SCORE = 1e4
DSA_HEADS = 16
DSA_KV_HEADS = 2
DSA_HPG = DSA_HEADS // DSA_KV_HEADS
IDX_HEADS = 8
IDX_DIM = 64
IDX_TOPK_MAX = 256
D_FF = -(-8 * D_MODEL // (3 * 256)) * 256
NSA_Q = NSA_HEADS * HEAD_DIM
NSA_KV = NSA_KV_GROUPS * HEAD_DIM
IN0_SIZES = (LRU_WIDTH, LRU_WIDTH, NSA_Q, NSA_KV, NSA_KV, NSA_KV, NSA_KV, NSA_KV, NSA_KV, NSA_HEADS * 3)
IN0 = sum(IN0_SIZES)
MIX0 = LRU_WIDTH + NSA_Q
IN1_SIZES = (DSA_HEADS * HEAD_DIM, DSA_KV_HEADS * HEAD_DIM, DSA_KV_HEADS * HEAD_DIM, IDX_HEADS * IDX_DIM, IDX_DIM, IDX_HEADS)
IN1 = sum(IN1_SIZES)
MIX1 = DSA_HEADS * HEAD_DIM


def _split(t, sizes):
    return jnp.split(t, np.cumsum(sizes)[:-1].tolist(), axis=-1)

def rmsnorm(x, g):
    xf = x.astype(jnp.float32)
    y = xf * lax.rsqrt(jnp.mean(xf * xf, axis=-1, keepdims=True) + EPS)
    return (y * g.astype(jnp.float32)).astype(x.dtype)

def modulate(x, g, shift, scale):
    return rmsnorm(x, g) * (1.0 + scale[:, None, :]) + shift[:, None, :]

def masked_softmax(s, mask):
    s = jnp.where(mask, s.astype(jnp.float32), -jnp.inf)
    m = jnp.max(s, axis=-1, keepdims=True)
    m = jnp.where(jnp.isfinite(m), m, 0.0)
    p = jnp.exp(s - m)
    return p / jnp.maximum(jnp.sum(p, axis=-1, keepdims=True), 1e-30)

def swiglu(h, wg, wu, wd):
    return (jax.nn.silu(h @ wg) * (h @ wu)) @ wd

def adaln(c, w_mod, b_mod):
    mod = jax.nn.silu(c) @ w_mod + b_mod
    return jnp.split(mod, 6, axis=-1)

def causal_conv(x, w, b):
    S = x.shape[1]
    xp = jnp.pad(x, ((0, 0), (CONV_WIDTH - 1, 0), (0, 0)))
    out = xp[:, 0:S] * w[0]
    for k in range(1, CONV_WIDTH):
        out = out + xp[:, k:k + S] * w[k]
    return out + b

def rg_lru(x, wa, ba, wx, bx, lam):
    B, S, _ = x.shape
    xf = x.astype(jnp.float32)
    xb = xf.reshape(B, S, LRU_BLOCKS, LRU_BLOCK)
    r = jax.nn.sigmoid(jnp.einsum('bshi,hij->bshj', xb, wa).reshape(B, S, LRU_WIDTH) + ba)
    i = jax.nn.sigmoid(jnp.einsum('bshi,hij->bshj', xb, wx).reshape(B, S, LRU_WIDTH) + bx)
    log_a = -LRU_C * r * jax.nn.softplus(-lam.astype(jnp.float32))
    a = jnp.exp(log_a)
    mult = jnp.sqrt(-jnp.expm1(2.0 * log_a))
    mult = jnp.where((jnp.arange(S) == 0)[None, :, None], 1.0, mult)
    u = mult * (i * xf)

    def combine(e1, e2):
        a1, b1 = e1
        a2, b2 = e2
        return a1 * a2, a2 * b1 + b2

    _, h = lax.associative_scan(combine, (a, u), axis=1)
    return h.astype(x.dtype)

def compress_blocks(kv, pe, w1, w2):
    B, S, G, D = kv.shape
    nc = (S - CMP_LEN) // CMP_STRIDE + 1
    idx = jnp.arange(nc)[:, None] * CMP_STRIDE + jnp.arange(CMP_LEN)[None, :]
    blk = kv[:, idx] + pe[:, None, :]
    flat = blk.transpose(0, 1, 3, 2, 4).reshape(B, nc, G, CMP_LEN * D)
    return jax.nn.gelu(flat @ w1) @ w2

def nsa_mixer(q, k_cmp, v_cmp, k_slc, v_slc, k_win, v_win, gates, pe_k, w1_k, w2_k, pe_v, w1_v, w2_v):
    B, S = q.shape[:2]
    G, R, D = NSA_KV_GROUPS, NSA_HPG, HEAD_DIM
    scale = D ** -0.5
    nc = (S - CMP_LEN) // CMP_STRIDE + 1
    nsel = S // SLC_LEN
    n_top = min(SLC_TOPN, nsel)
    rs = lambda t: t.reshape(B, S, G, D)
    kc = compress_blocks(rs(k_cmp), pe_k, w1_k, w2_k)
    vc = compress_blocks(rs(v_cmp), pe_v, w1_v, w2_v)
    ks = rs(k_slc).reshape(B, nsel, SLC_LEN, G, D).transpose(0, 3, 1, 2, 4)
    vs = rs(v_slc).reshape(B, nsel, SLC_LEN, G, D).transpose(0, 3, 1, 2, 4)
    pad = ((0, 0), (WIN, 0), (0, 0), (0, 0))
    kw_pad = jnp.pad(rs(k_win), pad)
    vw_pad = jnp.pad(rs(v_win), pad)
    c_start = jnp.arange(nc) * CMP_STRIDE
    c_end = c_start + CMP_LEN - 1
    j_start = jnp.arange(nsel) * SLC_LEN
    overlap = ((c_start[:, None] < j_start[None, :] + SLC_LEN)
               & (c_start[:, None] + CMP_LEN > j_start[None, :])).astype(jnp.float32)
    jj = jnp.arange(nsel)
    b_i = jnp.arange(B)[:, None, None, None]
    g_i = jnp.arange(G)[None, :, None, None]

    def block(ib):
        t0 = ib * Q_BLOCK
        tq = t0 + jnp.arange(Q_BLOCK)
        qc = lax.dynamic_slice_in_dim(q, t0, Q_BLOCK, axis=1).reshape(B, Q_BLOCK, G, R, D)
        gc = lax.dynamic_slice_in_dim(gates, t0, Q_BLOCK, axis=1).reshape(B, Q_BLOCK, G, R, 3)
        s = jnp.einsum('bqgrd,bcgd->bgrqc', qc, kc) * scale
        p_cmp = masked_softmax(s, c_end[None, :] <= tq[:, None])
        o_cmp = jnp.einsum('bgrqc,bcgd->bqgrd', p_cmp, vc)
        imp = jnp.einsum('bgrqc,cj->bgqj', p_cmp, overlap)
        cur = tq // SLC_LEN
        forced = (jj[None, :] == 0) | (jj[None, :] == cur[:, None]) | (jj[None, :] == cur[:, None] - 1)
        imp = jnp.where(forced, FORCE_SCORE, imp)
        imp = jnp.where(jj[None, :] <= cur[:, None], imp, -jnp.inf)
        _, sel = lax.top_k(imp, n_top)
        kg = ks[b_i, g_i, sel].reshape(B, G, Q_BLOCK, n_top * SLC_LEN, D)
        vg = vs[b_i, g_i, sel].reshape(B, G, Q_BLOCK, n_top * SLC_LEN, D)
        kpos = sel[..., None] * SLC_LEN + jnp.arange(SLC_LEN)
        smask = (kpos <= tq[:, None, None]).reshape(B, G, 1, Q_BLOCK, n_top * SLC_LEN)
        s = jnp.einsum('bqgrd,bgqkd->bgrqk', qc, kg) * scale
        o_slc = jnp.einsum('bgrqk,bgqkd->bqgrd', masked_softmax(s, smask), vg)
        kw = lax.dynamic_slice_in_dim(kw_pad, t0, WIN + Q_BLOCK, axis=1)
        vw = lax.dynamic_slice_in_dim(vw_pad, t0, WIN + Q_BLOCK, axis=1)
        kpw = t0 - WIN + jnp.arange(WIN + Q_BLOCK)
        wmask = (kpw[None, :] >= 0) & (kpw[None, :] <= tq[:, None]) & (kpw[None, :] > tq[:, None] - WIN)
        s = jnp.einsum('bqgrd,bkgd->bgrqk', qc, kw) * scale
        o_win = jnp.einsum('bgrqk,bkgd->bqgrd', masked_softmax(s, wmask), vw)
        o = gc[..., 0:1] * o_cmp + gc[..., 1:2] * o_slc + gc[..., 2:3] * o_win
        return o.reshape(B, Q_BLOCK, G * R * D).astype(q.dtype)

    out = lax.map(block, jnp.arange(S // Q_BLOCK))
    return out.transpose(1, 0, 2, 3).reshape(B, S, G * R * D)

def dsa_mixer(q, k, v, q_idx, k_idx, w_idx):
    B, S = q.shape[:2]
    G, R, D = DSA_KV_HEADS, DSA_HPG, HEAD_DIM
    scale = D ** -0.5
    n_keep = min(IDX_TOPK_MAX, S // 4)
    kk = k.reshape(B, S, G, D)
    vv = v.reshape(B, S, G, D)
    qi_all = q_idx.reshape(B, S, IDX_HEADS, IDX_DIM)
    kpos = jnp.arange(S)
    b_i = jnp.arange(B)[:, None, None]

    def block(ib):
        t0 = ib * Q_BLOCK
        tq = t0 + jnp.arange(Q_BLOCK)
        qi = lax.dynamic_slice_in_dim(qi_all, t0, Q_BLOCK, axis=1)
        wi = lax.dynamic_slice_in_dim(w_idx, t0, Q_BLOCK, axis=1)
        sc = jax.nn.relu(jnp.einsum('bqhd,bsd->bqhs', qi, k_idx) * IDX_DIM ** -0.5)
        idx_score = jnp.einsum('bqhs,bqh->bqs', sc.astype(jnp.float32), wi.astype(jnp.float32)) * IDX_HEADS ** -0.5
        idx_score = jnp.where(kpos[None, :] <= tq[:, None], idx_score, -jnp.inf)
        _, sel = lax.top_k(idx_score, n_keep)
        kg = kk[b_i, sel]
        vg = vv[b_i, sel]
        qc = lax.dynamic_slice_in_dim(q, t0, Q_BLOCK, axis=1).reshape(B, Q_BLOCK, G, R, D)
        s = jnp.einsum('bqgrd,bqkgd->bgrqk', qc, kg) * scale
        mask = (sel <= tq[None, :, None])[:, None, None]
        o = jnp.einsum('bgrqk,bqkgd->bqgrd', masked_softmax(s, mask), vg)
        return o.reshape(B, Q_BLOCK, G * R * D).astype(q.dtype)

    out = lax.map(block, jnp.arange(S // Q_BLOCK))
    return out.transpose(1, 0, 2, 3).reshape(B, S, G * R * D)

def layer_ab(x, c, norm_mix, norm_ffn, mod_w, mod_b, w_in, conv_w, conv_b, wa, ba, wx, bx, lam,
             pe_k, w1_k, w2_k, pe_v, w1_v, w2_v, w_out, wg, wu, wd):
    sh_m, sc_m, g_m, sh_f, sc_f, g_f = adaln(c, mod_w, mod_b)
    h = modulate(x, norm_mix, sh_m, sc_m)
    (a_gate, a_x, q, kc, vc, ks, vs, kw, vw, gts) = _split(h @ w_in, IN0_SIZES)
    y_a = rg_lru(causal_conv(a_x, conv_w, conv_b), wa, ba, wx, bx, lam) * jax.nn.gelu(a_gate)
    y_b = nsa_mixer(q, kc, vc, ks, vs, kw, vw, jax.nn.sigmoid(gts), pe_k, w1_k, w2_k, pe_v, w1_v, w2_v)
    x = x + g_m[:, None, :] * (jnp.concatenate([y_a, y_b], axis=-1) @ w_out)
    h = modulate(x, norm_ffn, sh_f, sc_f)
    return x + g_f[:, None, :] * swiglu(h, wg, wu, wd)

def layer_c(x, c, norm_mix, norm_ffn, mod_w, mod_b, w_in, w_out, wg, wu, wd):
    sh_m, sc_m, g_m, sh_f, sc_f, g_f = adaln(c, mod_w, mod_b)
    h = modulate(x, norm_mix, sh_m, sc_m)
    q, k, v, q_idx, k_idx, w_idx = _split(h @ w_in, IN1_SIZES)
    x = x + g_m[:, None, :] * (dsa_mixer(q, k, v, q_idx, k_idx, w_idx) @ w_out)
    h = modulate(x, norm_ffn, sh_f, sc_f)
    return x + g_f[:, None, :] * swiglu(h, wg, wu, wd)

def first_inputs(seed: int = 0) -> dict:
    key = jax.random.key(seed)
    keys = iter(jax.random.split(key, 64))

    def nrm(shape, s):
        return jax.random.normal(next(keys), shape, jnp.float32) * s

    def gain(n):
        return 1.0 + nrm((n,), 0.05)

    D = D_MODEL
    a0 = jax.random.uniform(next(keys), (LRU_WIDTH,), jnp.float32, minval=0.9, maxval=0.999)
    r0 = a0 ** (1.0 / LRU_C)
    lam = jnp.log(r0) - jnp.log1p(-r0)
    return {
        "x": nrm((BATCH, SEQ, D), 1.0),
        "c": nrm((BATCH, D), 1.0),
        "l0_norm_mix": gain(D),
        "l0_norm_ffn": gain(D),
        "l0_mod_w": nrm((D, 6 * D), 0.5 * D ** -0.5),
        "l0_mod_b": nrm((6 * D,), 0.01),
        "l0_w_in": nrm((D, IN0), D ** -0.5),
        "l0_conv_w": nrm((CONV_WIDTH, LRU_WIDTH), CONV_WIDTH ** -0.5),
        "l0_conv_b": nrm((LRU_WIDTH,), 0.01),
        "l0_lru_wa": nrm((LRU_BLOCKS, LRU_BLOCK, LRU_BLOCK), LRU_BLOCK ** -0.5),
        "l0_lru_ba": nrm((LRU_WIDTH,), 0.01),
        "l0_lru_wx": nrm((LRU_BLOCKS, LRU_BLOCK, LRU_BLOCK), LRU_BLOCK ** -0.5),
        "l0_lru_bx": nrm((LRU_WIDTH,), 0.01),
        "l0_lru_lambda": lam,
        "l0_cmp_pe_k": nrm((CMP_LEN, HEAD_DIM), 0.5),
        "l0_cmp_w1_k": nrm((CMP_LEN * HEAD_DIM, CMP_HIDDEN), (CMP_LEN * HEAD_DIM) ** -0.5),
        "l0_cmp_w2_k": nrm((CMP_HIDDEN, HEAD_DIM), CMP_HIDDEN ** -0.5),
        "l0_cmp_pe_v": nrm((CMP_LEN, HEAD_DIM), 0.5),
        "l0_cmp_w1_v": nrm((CMP_LEN * HEAD_DIM, CMP_HIDDEN), (CMP_LEN * HEAD_DIM) ** -0.5),
        "l0_cmp_w2_v": nrm((CMP_HIDDEN, HEAD_DIM), CMP_HIDDEN ** -0.5),
        "l0_w_out": nrm((MIX0, D), MIX0 ** -0.5),
        "l0_ffn_wg": nrm((D, D_FF), D ** -0.5),
        "l0_ffn_wu": nrm((D, D_FF), D ** -0.5),
        "l0_ffn_wd": nrm((D_FF, D), D_FF ** -0.5),
        "l1_norm_mix": gain(D),
        "l1_norm_ffn": gain(D),
        "l1_mod_w": nrm((D, 6 * D), 0.5 * D ** -0.5),
        "l1_mod_b": nrm((6 * D,), 0.01),
        "l1_w_in": nrm((D, IN1), D ** -0.5),
        "l1_w_out": nrm((MIX1, D), MIX1 ** -0.5),
        "l1_ffn_wg": nrm((D, D_FF), D ** -0.5),
        "l1_ffn_wu": nrm((D, D_FF), D ** -0.5),
        "l1_ffn_wd": nrm((D_FF, D), D_FF ** -0.5),
        "final_norm": gain(D),
    }

def first_block(x, c,
              l0_norm_mix, l0_norm_ffn, l0_mod_w, l0_mod_b, l0_w_in, l0_conv_w, l0_conv_b,
              l0_lru_wa, l0_lru_ba, l0_lru_wx, l0_lru_bx, l0_lru_lambda,
              l0_cmp_pe_k, l0_cmp_w1_k, l0_cmp_w2_k, l0_cmp_pe_v, l0_cmp_w1_v, l0_cmp_w2_v,
              l0_w_out, l0_ffn_wg, l0_ffn_wu, l0_ffn_wd,
              l1_norm_mix, l1_norm_ffn, l1_mod_w, l1_mod_b, l1_w_in, l1_w_out,
              l1_ffn_wg, l1_ffn_wu, l1_ffn_wd,
              final_norm):
    layer_params = [
        (l0_norm_mix, l0_norm_ffn, l0_mod_w, l0_mod_b, l0_w_in, l0_conv_w, l0_conv_b,
         l0_lru_wa, l0_lru_ba, l0_lru_wx, l0_lru_bx, l0_lru_lambda,
         l0_cmp_pe_k, l0_cmp_w1_k, l0_cmp_w2_k, l0_cmp_pe_v, l0_cmp_w1_v, l0_cmp_w2_v,
         l0_w_out, l0_ffn_wg, l0_ffn_wu, l0_ffn_wd),
        (l1_norm_mix, l1_norm_ffn, l1_mod_w, l1_mod_b, l1_w_in, l1_w_out,
         l1_ffn_wg, l1_ffn_wu, l1_ffn_wd),
    ]
    for layer in range(DEPTH):
        if layer % 2 == 0:
            x = layer_ab(x, c, *layer_params[layer])
        else:
            x = layer_c(x, c, *layer_params[layer])
    return rmsnorm(x, final_norm)


CTX_LEN = 256
GRID_W = 64

SGU_HEADS = 4
SGU_HEAD_DIM = 64
SGU_W = SGU_HEADS * SGU_HEAD_DIM
CHUNK = 128
FNET_GROUPS = 4
FNET_GROUP_DIM = 64
FNET_W = FNET_GROUPS * FNET_GROUP_DIM
MLA_HEADS = 4
QK_NOPE_DIM = 128
QK_ROPE_DIM = 64
QK_DIM = QK_NOPE_DIM + QK_ROPE_DIM
V_DIM = 128
Q_LORA = 256
KV_LORA = 128
MLA_W = MLA_HEADS * V_DIM
ROPE_THETA = 10000.0
OFF_U = 0
OFF_V = OFF_U + SGU_W
OFF_F = OFF_V + SGU_W
OFF_Q = OFF_F + FNET_W
OFF_KV = OFF_Q + Q_LORA
OFF_KR = OFF_KV + KV_LORA
IN_W = OFF_KR + QK_ROPE_DIM
MIX_W = SGU_W + FNET_W + MLA_W
N_EXPERTS = 16
EC_FACTOR = 2
D_EXPERT = 512


def rms_norm(x):
    xf = x.astype(jnp.float32)
    return (xf * lax.rsqrt(jnp.mean(xf * xf, axis=-1, keepdims=True) + EPS)).astype(x.dtype)

def ada_modulation(cond, w_ada, b_ada):
    m = (jax.nn.silu(cond) @ w_ada + b_ada)[:, None, :]
    return jnp.split(m, 6, axis=-1)

def modulate_2(x, shift, scale):
    return rms_norm(x) * (1 + scale) + shift

def rope_1d(x, pos):
    half = x.shape[-1] // 2
    freqs = ROPE_THETA ** (-jnp.arange(half, dtype=jnp.float32) / half)
    ang = pos.astype(jnp.float32)[:, None] * freqs
    cos = jnp.cos(ang)[:, None, :]
    sin = jnp.sin(ang)[:, None, :]
    xf = x.astype(jnp.float32)
    x1, x2 = xf[..., :half], xf[..., half:]
    return jnp.concatenate([x1 * cos - x2 * sin, x1 * sin + x2 * cos], axis=-1).astype(x.dtype)

def rope_2d(x, pos_row, pos_col):
    half = x.shape[-1] // 2
    return jnp.concatenate([rope_1d(x[..., :half], pos_row), rope_1d(x[..., half:], pos_col)], axis=-1)

def with_rope(t, pos_row, pos_col):
    return jnp.concatenate([t[..., :QK_NOPE_DIM], rope_2d(t[..., QK_NOPE_DIM:], pos_row, pos_col)], axis=-1)

def chunk_mlp(pu, pv, sgu_norm, w_sgu, b_sgu):
    b, n, _ = pu.shape
    u = jax.nn.gelu(pu)
    v = rms_norm(jax.nn.gelu(pv)) * sgu_norm
    v = v.reshape(b, n // CHUNK, CHUNK, SGU_HEADS, SGU_HEAD_DIM)
    z = jnp.einsum('hpq,bcqhd->bcphd', w_sgu, v) + b_sgu.T[:, :, None]
    return u * z.reshape(b, n, SGU_W)

def fourier_mix(pf):
    b, n, _ = pf.shape
    f = pf.reshape(b, n, FNET_GROUPS, FNET_GROUP_DIM).astype(jnp.float32)
    y = jnp.fft.fft2(f, axes=(1, 3), norm="ortho").real
    return y.reshape(b, n, FNET_W).astype(pf.dtype)

def mla_queries(pq, q_lora_norm, w_uq, q_norm):
    b, n, _ = pq.shape
    cq = rms_norm(pq) * q_lora_norm
    q = (cq @ w_uq).reshape(b, n, MLA_HEADS, QK_DIM)
    return rms_norm(q) * q_norm

def mla_keys_values(pkv, pkr, kv_lora_norm, w_ukv, k_norm):
    b, n, _ = pkv.shape
    ckv = rms_norm(pkv) * kv_lora_norm
    kv = (ckv @ w_ukv).reshape(b, n, MLA_HEADS, QK_NOPE_DIM + V_DIM)
    k_nope, v = kv[..., :QK_NOPE_DIM], kv[..., QK_NOPE_DIM:]
    k_rope = jnp.broadcast_to(pkr[:, :, None, :], (b, n, MLA_HEADS, QK_ROPE_DIM))
    k = rms_norm(jnp.concatenate([k_nope, k_rope], axis=-1)) * k_norm
    return k, v

def block_attention(q, k, v):
    b, n, h, _ = q.shape
    scale = QK_DIM ** -0.5
    qb = jnp.moveaxis(q.reshape(b, n // Q_BLOCK, Q_BLOCK, h, QK_DIM), 1, 0)

    def one_block(qblk):
        s = jnp.einsum('bqhd,bkhd->bhqk', qblk, k).astype(jnp.float32) * scale
        p = jax.nn.softmax(s, axis=-1).astype(v.dtype)
        return jnp.einsum('bhqk,bkhv->bqhv', p, v)

    o = lax.map(one_block, qb)
    return jnp.moveaxis(o, 0, 1).reshape(b, n, h * V_DIM)

def local_head_groups(p, sgu_norm, w_sgu, b_sgu, q_lora_norm, w_uq, q_norm):
    ya = chunk_mlp(p[..., OFF_U:OFF_V], p[..., OFF_V:OFF_F], sgu_norm, w_sgu, b_sgu)
    yb = fourier_mix(p[..., OFF_F:OFF_Q])
    q = mla_queries(p[..., OFF_Q:OFF_KV], q_lora_norm, w_uq, q_norm)
    return ya, yb, q

def expert_choice_moe(h, w_router, w_gate, w_up, w_down):
    b, n, d = h.shape
    cap = EC_FACTOR * n // N_EXPERTS
    aff = jax.nn.softmax(jnp.einsum('bnd,de->bne', h, w_router).astype(jnp.float32), axis=-1)
    g, idx = lax.top_k(jnp.swapaxes(aff, 1, 2), cap)
    xs = jax.vmap(lambda hb, ib: hb[ib])(h, idx)
    hid = jax.nn.silu(jnp.einsum('becd,edf->becf', xs, w_gate)) * jnp.einsum('becd,edf->becf', xs, w_up)
    y = jnp.einsum('becf,efd->becd', hid, w_down) * g[..., None].astype(h.dtype)
    return jax.vmap(lambda yb, ib: jnp.zeros((n, d), h.dtype).at[ib.reshape(-1)].add(yb.reshape(-1, d)))(y, idx)

def second_inputs(seed: int = 0) -> dict:
    key = jax.random.key(seed)
    ks = jax.random.split(key, 22)

    def nrm(k, shape, scale):
        return jax.random.normal(k, shape, jnp.float32) * scale

    return {
        "x": nrm(ks[0], (BATCH, SEQ, D_MODEL), 1.0),
        "c": nrm(ks[1], (BATCH, D_MODEL), 1.0),
        "ctx": nrm(ks[2], (BATCH, CTX_LEN, D_MODEL), 1.0),
        "c_ctx": nrm(ks[3], (D_MODEL,), 1.0),
        "w_ada": nrm(ks[4], (DEPTH, D_MODEL, 6 * D_MODEL), 0.5 * D_MODEL ** -0.5),
        "b_ada": nrm(ks[5], (DEPTH, 6 * D_MODEL), 0.01),
        "w_in": nrm(ks[6], (DEPTH, D_MODEL, IN_W), D_MODEL ** -0.5),
        "sgu_norm": 1.0 + nrm(ks[7], (DEPTH, SGU_W), 0.01),
        "w_sgu": nrm(ks[8], (DEPTH, SGU_HEADS, CHUNK, CHUNK), CHUNK ** -0.5),
        "b_sgu": 1.0 + nrm(ks[9], (DEPTH, SGU_HEADS, CHUNK), 0.01),
        "q_lora_norm": 1.0 + nrm(ks[10], (DEPTH, Q_LORA), 0.01),
        "w_uq": nrm(ks[11], (DEPTH, Q_LORA, MLA_HEADS * QK_DIM), Q_LORA ** -0.5),
        "kv_lora_norm": 1.0 + nrm(ks[12], (DEPTH, KV_LORA), 0.01),
        "w_ukv": nrm(ks[13], (DEPTH, KV_LORA, MLA_HEADS * (QK_NOPE_DIM + V_DIM)), KV_LORA ** -0.5),
        "q_norm": 1.0 + nrm(ks[14], (DEPTH, QK_DIM), 0.01),
        "k_norm": 1.0 + nrm(ks[15], (DEPTH, QK_DIM), 0.01),
        "w_out": nrm(ks[16], (DEPTH, MIX_W, D_MODEL), MIX_W ** -0.5),
        "w_router": nrm(ks[17], (DEPTH, D_MODEL, N_EXPERTS), D_MODEL ** -0.5),
        "w_gate": nrm(ks[18], (DEPTH, N_EXPERTS, D_MODEL, D_EXPERT), D_MODEL ** -0.5),
        "w_up": nrm(ks[19], (DEPTH, N_EXPERTS, D_MODEL, D_EXPERT), D_MODEL ** -0.5),
        "w_down": nrm(ks[20], (DEPTH, N_EXPERTS, D_EXPERT, D_MODEL), D_EXPERT ** -0.5),
    }

def second_block(x, c, ctx, c_ctx, w_ada, b_ada, w_in, sgu_norm, w_sgu, b_sgu, q_lora_norm, w_uq,
              kv_lora_norm, w_ukv, q_norm, k_norm, w_out, w_router, w_gate, w_up, w_down):
    n = x.shape[1]
    rows = n // GRID_W
    pos_row = jnp.repeat(jnp.arange(rows, dtype=jnp.int32), GRID_W)
    pos_col = jnp.tile(jnp.arange(GRID_W, dtype=jnp.int32), rows)
    xc = ctx
    for l in range(DEPTH):
        last = l == DEPTH - 1
        sh1, sc1, g1, sh2, sc2, g2 = ada_modulation(c, w_ada[l], b_ada[l])
        csh1, csc1, cg1, csh2, csc2, cg2 = ada_modulation(c_ctx[None], w_ada[l], b_ada[l])

        hx = modulate_2(x, sh1, sc1)
        hc = modulate_2(xc, csh1, csc1)
        col0 = OFF_KV if last else 0
        pc = hc @ w_in[l][:, col0:]
        k_ctx, v_ctx = mla_keys_values(pc[..., OFF_KV - col0:OFF_KR - col0], pc[..., OFF_KR - col0:],
                                       kv_lora_norm[l], w_ukv[l], k_norm[l])

        px = hx @ w_in[l]
        ya, yb, q = local_head_groups(px, sgu_norm[l], w_sgu[l], b_sgu[l], q_lora_norm[l], w_uq[l], q_norm[l])
        k, v = mla_keys_values(px[..., OFF_KV:OFF_KR], px[..., OFF_KR:], kv_lora_norm[l], w_ukv[l], k_norm[l])
        q = with_rope(q, pos_row, pos_col)
        k = with_rope(k, pos_row, pos_col)
        yc = block_attention(q, jnp.concatenate([k_ctx, k], axis=1), jnp.concatenate([v_ctx, v], axis=1))
        x = x + g1 * (jnp.concatenate([ya, yb, yc], axis=-1) @ w_out[l])

        if not last:
            ya_c, yb_c, q_c = local_head_groups(pc, sgu_norm[l], w_sgu[l], b_sgu[l], q_lora_norm[l], w_uq[l], q_norm[l])
            yc_c = block_attention(q_c, k_ctx, v_ctx)
            xc = xc + cg1 * (jnp.concatenate([ya_c, yb_c, yc_c], axis=-1) @ w_out[l])

        x = x + g2 * expert_choice_moe(modulate_2(x, sh2, sc2), w_router[l], w_gate[l], w_up[l], w_down[l])
        if not last:
            xc = xc + cg2 * expert_choice_moe(modulate_2(xc, csh2, csc2), w_router[l], w_gate[l], w_up[l], w_down[l])
    return x


def setup_inputs(seed=0):
    out = dict(first_inputs(seed))
    for name, value in second_inputs(seed + 1).items():
        if name != "x":
            out[name + "_2"] = value
    return out


def reference(
    x, c, l0_norm_mix, l0_norm_ffn, l0_mod_w, l0_mod_b, l0_w_in, l0_conv_w, l0_conv_b,
    l0_lru_wa, l0_lru_ba, l0_lru_wx, l0_lru_bx, l0_lru_lambda, l0_cmp_pe_k, l0_cmp_w1_k,
    l0_cmp_w2_k, l0_cmp_pe_v, l0_cmp_w1_v, l0_cmp_w2_v, l0_w_out, l0_ffn_wg, l0_ffn_wu,
    l0_ffn_wd, l1_norm_mix, l1_norm_ffn, l1_mod_w, l1_mod_b, l1_w_in, l1_w_out, l1_ffn_wg,
    l1_ffn_wu, l1_ffn_wd, final_norm, c_2, ctx_2, c_ctx_2, w_ada_2, b_ada_2, w_in_2, sgu_norm_2,
    w_sgu_2, b_sgu_2, q_lora_norm_2, w_uq_2, kv_lora_norm_2, w_ukv_2, q_norm_2, k_norm_2,
    w_out_2, w_router_2, w_gate_2, w_up_2, w_down_2,
):
    x = first_block(
        x, c, l0_norm_mix, l0_norm_ffn, l0_mod_w, l0_mod_b, l0_w_in, l0_conv_w, l0_conv_b,
        l0_lru_wa, l0_lru_ba, l0_lru_wx, l0_lru_bx, l0_lru_lambda, l0_cmp_pe_k, l0_cmp_w1_k,
        l0_cmp_w2_k, l0_cmp_pe_v, l0_cmp_w1_v, l0_cmp_w2_v, l0_w_out, l0_ffn_wg, l0_ffn_wu,
        l0_ffn_wd, l1_norm_mix, l1_norm_ffn, l1_mod_w, l1_mod_b, l1_w_in, l1_w_out, l1_ffn_wg,
        l1_ffn_wu, l1_ffn_wd, final_norm,
    )
    return second_block(
        x, c_2, ctx_2, c_ctx_2, w_ada_2, b_ada_2, w_in_2, sgu_norm_2, w_sgu_2, b_sgu_2,
        q_lora_norm_2, w_uq_2, kv_lora_norm_2, w_ukv_2, q_norm_2, k_norm_2, w_out_2, w_router_2,
        w_gate_2, w_up_2, w_down_2,
    )


_drawn_inputs = setup_inputs


def setup_inputs(seed=0):
    import zlib

    import numpy as np

    out = dict(_drawn_inputs(seed))
    spreads = {}
    factors = {'l0_norm_mix': 3.662,
     'l0_norm_ffn': 3.116,
     'l0_mod_b': 3.351,
     'l0_conv_b': 5.316,
     'l0_lru_ba': 8.0,
     'l0_lru_bx': 8.0,
     'l0_cmp_pe_k': 6.521,
     'l0_cmp_w1_k': 2.673,
     'l1_norm_mix': 3.104,
     'l1_norm_ffn': 3.239,
     'l1_mod_b': 3.961,
     'ctx_2': 3.563,
     'b_ada_2': 4.067,
     'sgu_norm_2': 8.0,
     'b_sgu_2': 8.0,
     'q_lora_norm_2': 8.0,
     'kv_lora_norm_2': 8.0,
     'q_norm_2': 8.0,
     'k_norm_2': 8.0}
    for name, (base, spread) in spreads.items():
        noise = np.random.default_rng([zlib.crc32(name.encode()), seed]).standard_normal(out[name].shape)
        drawn = base * np.exp(spread * noise) if base else spread * noise
        out[name] = __import__('jax').numpy.asarray(drawn.astype(out[name].dtype))
    for name, factor in factors.items():
        out[name] = (out[name] * factor).astype(out[name].dtype)
    return out
```

```python
from contextlib import ExitStack

import numpy as np

import concourse.bass as bass
from concourse import mybir

F32 = mybir.dt.float32
ACT = mybir.ActivationFunctionType
ALU = mybir.AluOpType
X = mybir.AxisListType.X

P = 128
D = 1024
DC = D // P
T = 256
NT = T // P
F = 2816
FC = F // P
EPS = 1e-6
HD = 64
TAKEN = -3e38
NEG = -1e30
FLOOR = -1e20

LRU = 512
LC = LRU // P
CMP_LEN, CMP_STRIDE = 32, 16
NBLK = (T - CMP_LEN) // CMP_STRIDE + 1
TOPK = min(256, T // 4)
IDX_HEADS = 8

NE, CAP, DE = 16, 2 * T // 16, 512
GE = P // CAP
NG = NE // GE
MH, NOPE, ROPE = 4, 128, 64
QKD = NOPE + ROPE

SLOTS = 6
SLOT = 4096

C_DFTN, C_DFTD = 0, 1024
C_CMP = C_DFTD + 256
C_CAUSAL = C_CMP + NT * 256
C_IDENT = C_CAUSAL + P
C_IOTA = C_IDENT + P
C_ROPE = C_IOTA + CAP
C_END = C_ROPE + NT * 2 * 64

VEC_NAMES = [
    ["l0_mod_b", "l1_mod_b", "l0_norm_mix", "l0_norm_ffn", "l1_norm_mix", "l1_norm_ffn"],
    ["b_ada_2", "final_norm", "c", "c_2", "c_ctx_2"],
    ["l0_conv_w", "l0_conv_b", "l0_lru_ba", "l0_lru_bx", "l0_lru_lambda", "b_sgu_2"],
]
VEC_ROWS = {"l0_mod_b": 48, "l1_mod_b": 48, "l0_norm_mix": 8, "l0_norm_ffn": 8, "l1_norm_mix": 8,
            "l1_norm_ffn": 8, "b_ada_2": 96, "final_norm": 8, "c": 8, "c_2": 8, "c_ctx_2": 8,
            "l0_conv_w": 16, "l0_conv_b": 4, "l0_lru_ba": 4, "l0_lru_bx": 4, "l0_lru_lambda": 4, "b_sgu_2": 8}


ROWS = {"sgu_norm_2": (0, 256), "q_lora_norm_2": (256, 256), "kv_lora_norm_2": (512, 128),
        "q_norm_2": (640, QKD), "k_norm_2": (832, QKD)}


def ffn_pieces(layer, extra):
    out, extra = [], list(extra)
    steps = -(-F // 512)
    per = -(-len(extra) // steps)
    for s in range(steps):
        out += [("wg", layer, s), ("wu", layer, s), ("wd", layer, s)]
        out += extra[:per]
        del extra[:per]
    return out


def ada(matrix):
    return [("ada", matrix, s) for s in range(12)]


def weight_pieces():
    out = ada(0)
    out += [("in0", s) for s in (1, 0, 2, 3, 4)]
    out += [("lru",), ("cmp", 0), ("cmp", 1), ("out", 0, 0), ("out", 0, 1)]
    out += ffn_pieces(0, ada(1) + ada(2))
    out += [("in1", s) for s in range(4)] + [("out", 1, 0), ("out", 1, 1)]
    out += ffn_pieces(1, ada(3))
    for layer in range(2):
        for stream in ("ctx", "x"):
            full = stream == "x" or layer == 0
            out += [("in2", layer, s) for s in ((0, 1, 2) if full else (2,))]
            out += [("mla", layer)]
            if full:
                out += [("tab",), ("out2", layer, 0), ("out2", layer, 1)]
        for g in range(NG):
            out += [("moe", layer, kind, g, s) for kind in range(3) for s in range(4)]
    return out


def program(nc, A):
    ctx = ExitStack()
    with ctx:
        def sb(name, cols):
            return ctx.enter_context(nc.sbuf_tensor(name, [P, cols], F32))

        def sem(name):
            return ctx.enter_context(nc.semaphore(name))

        ring = sb("ring", SLOTS * SLOT)
        xT_ = sb("xT", DC * T)
        cT_ = sb("ctxT", DC * T)
        hT_ = sb("hT", DC * T)
        tab = sb("tab", C_END - C_CAUSAL)
        ones = sb("ones", P)
        vecs = sb("vecs", 3 * P)
        mods = sb("mods", 48 * 6)
        acol = sb("acol", 80)
        csil = sb("csil", 24)
        small = sb("small", 256)
        brow = sb("brow", 1024)
        wrt = sb("wrt", 2 * P)
        SCR = 19456
        scr = sb("scr", SCR)
        banks = [ctx.enter_context(nc.psum_tensor(f"bank{i}", [P, 512], F32)) for i in range(8)]

        def v3(t, o, a, b):
            return t[:, o:o + a * b].rearrange("p (a b) -> p a b", a=a)

        xT, cT, hT = v3(xT_, 0, DC, T), v3(cT_, 0, DC, T), v3(hT_, 0, DC, T)
        causal = tab[:, 0:P]
        ident = tab[:, C_IDENT - C_CAUSAL:C_IDENT - C_CAUSAL + P]
        iota1 = tab[:, C_IOTA - C_CAUSAL:C_IOTA - C_CAUSAL + CAP]
        ropes = tab[:, C_ROPE - C_CAUSAL:C_END - C_CAUSAL].rearrange("p (t s n) -> p t s n", t=NT, s=2)

        vcol, o = {}, 0
        for t, names in enumerate(VEC_NAMES):
            o = t * P
            for n in names:
                vcol[n] = o
                o += VEC_ROWS[n]

        def vec(name, c=0, n=1):
            return vecs[:, vcol[name] + c:vcol[name] + c + n]

        MODO = [0, 48, 96, 192]

        def mod(matrix, seg, c, n=1, cond=0):
            if matrix < 2:
                o = MODO[matrix] + seg * 8 + c
                return mods[:, o:o + n]
            o = MODO[matrix] + (seg * 8 + c) * 2 + cond
            return mods[:, o:o + 2 * n - 1:2] if n > 1 else mods[:, o:o + 1]

        def ac(i, c=0, n=1):
            return acol[:, i * 8 + c:i * 8 + c + n]

        pieces = weight_pieces()
        index = {}
        for k, key in enumerate(pieces):
            index.setdefault(key, []).append(k)
        n_dma = {"lru": 4, "cmp": 2, "mla": 3, "moe": GE, "out": 1}

        def dmas_of(key):
            if key[0] == "out" and key[1:] == (0, 1) or key[0] == "out" and key[1] == 1:
                return 2
            if key[0] == "moe" and key[2] == 2:
                return GE
            return n_dma.get(key[0], 1)

        landed, count = [], [0] * SLOTS
        for k, key in enumerate(pieces):
            count[k % SLOTS] += 16 * dmas_of(key)
            landed.append(count[k % SLOTS])

        def slot(k):
            return ring[:, (k % SLOTS) * SLOT:(k % SLOTS + 1) * SLOT]

        slot_loaded = [sem(f"slot_loaded{i}") for i in range(SLOTS)]
        slots_released = sem("slots_released")

        loads = sem("loads")
        row_loads = sem("row_loads")
        out_copied, stored = sem("out_copied"), sem("stored")
        pe_to_dve, dve_read = sem("pe_to_dve"), sem("dve_read")
        pe_to_act, act_read = sem("pe_to_act"), sem("act_read")
        pe_phase, act_phase, dve_phase = sem("pe_phase"), sem("act_phase"), sem("dve_phase")
        dve_chain, act_chain = sem("dve_chain"), sem("act_chain")
        dve_made_for_pe, act_made_for_pe = sem("dve_made_for_pe"), sem("act_made_for_pe")
        dve_made_for_act, act_made_for_dve = sem("dve_made_for_act"), sem("act_made_for_dve")
        squares_ready, var_ready = sem("squares_ready"), sem("var_ready")
        std_ready, xn_ready = sem("std_ready"), sem("xn_ready")
        h_by_dve, h_by_act = sem("h_by_dve"), sem("h_by_act")
        ada_done = sem("ada_done")
        gu_ready, silu_ready, act_ready = sem("gate_up_ready"), sem("silu_ready"), sem("act_ready")
        acc_ready = sem("acc_ready")
        scores_ready, negmax_ready, exp_done = sem("scores_ready"), sem("negmax_ready"), sem("exp_done")
        probs_ready, turned, turned_copied = sem("probs_ready"), sem("turned"), sem("turned_copied")
        index_added = sem("index_added")
        xs_ready, gu_done, hid_silu, hid_ready = sem("xs_ready"), sem("gu_done"), sem("hid_silu"), sem("hid_ready")
        hid_turned, hid_copied, y_ready, y_read = sem("hid_turned"), sem("hid_copied"), sem("y_ready"), sem("y_read")

        class Arena:
            def __init__(self, at=0):
                self.at = at

            def take(self, *shape):
                n = 1
                for s in shape:
                    n *= s
                ap = scr[:, self.at:self.at + n]
                self.at += n
                assert self.at <= SCR, self.at
                if len(shape) == 2:
                    ap = ap.rearrange("p (a b) -> p a b", a=shape[0])
                elif len(shape) == 3:
                    ap = ap.rearrange("p (a b c) -> p a b c", a=shape[0], b=shape[1])
                return ap

        xn = v3(scr, 0, DC, T)
        std = scr[:, 2048:2304]
        tok_in = v3(scr, 4096, NT, D)
        tok_in2 = v3(scr, 6144, NT, D)
        vec_rows = v3(scr, 8192, 3, P)
        pe_rows = scr[0:CMP_LEN, 8576:8576 + 256]
        peT = small[:, 0:64]
        lam = small[:, 64:84]

        a0 = Arena(2304)
        axp = a0.take(LC, T + 3)
        xc = a0.take(LC, T)
        gg = a0.take(LC, T)
        rr = a0.take(LC, T)
        ii = a0.take(LC, T)
        aa = a0.take(LC, T)
        th = a0.take(LC, T)
        q0 = a0.take(4, T)
        ks0, kw0 = a0.take(T), a0.take(T)
        vs0, vw0 = a0.take(NT, P), a0.take(NT, P)
        gts = a0.take(NT, 8, 3)
        ft = [a0.take(2, CMP_STRIDE, NBLK) for _ in range(2)]
        h1 = a0.take(2, 2, CMP_STRIDE)
        kc = a0.take(CMP_STRIDE)
        vc = a0.take(2, HD)
        pc = a0.take(NT, 8, 32)
        pcT = a0.take(2, T)
        cmp_mask = a0.take(NT, 256)
        assert a0.at - NT * 256 >= 8832
        pr = a0.take(2, 512)
        pt = a0.take(2, 512)
        a1 = Arena(2304)
        q1 = a1.take(8, T)
        k1 = a1.take(T)
        v1 = a1.take(NT, P)
        qi = a1.take(4, T)
        ki = a1.take(T)
        wi = a1.take(NT, IDX_HEADS)
        idx = a1.take(NT, T)
        work = a1.take(NT, T)
        sel = a1.take(NT, T)
        rel = a1.take(2, 512)
        pr1 = a1.take(2, 512)
        pt1 = a1.take(2, 512)
        yT = v3(scr, 0, DC, T)
        assert a1.at + 0 < SCR
        af = Arena(2304)
        sil = af.take(2, T)
        actT = af.take(4, T)
        a2 = Arena(2304)
        kTn = a2.take(MH, 2 * T)
        kTr = a2.take(MH, 2 * T)
        vv = a2.take(4, 512)
        uv = a2.take(NT, 512)
        fq = a2.take(NT, 512)
        kvr = a2.take(NT, 192)
        full = a2.take(2, MH, QKD)
        sq2 = a2.take(MH * QKD)
        qTn = a2.take(MH, T)
        qTr = a2.take(MH, T)
        pr2 = a2.take(2, 512)
        pt2 = a2.take(2, 512)
        acs = a2.take(2, 2, T)
        cqT = a2.take(3, P)
        am = Arena(0)
        xsT = [am.take(DC, NE * CAP) for _ in range(2)]
        ys = [am.take(NG, D) for _ in range(2)]
        xs = [am.take(DC, P) for _ in range(2)]
        hid = [brow[:, s * 512:(s + 1) * 512] for s in range(2)]
        hidT = [am.take(4, P) for _ in range(2)]
        ay = Arena(8192)
        mxn = ay.take(DC, T)
        mhT = ay.take(DC, T)
        xtok = ay.take(NT, D)
        pm = ay.take(NT, NE * CAP)
        pg = ay.take(NT, NE * CAP)
        pgT = [v3(hT_, s * 1024, NG, T) for s in range(2)]
        mstd = scr[:, 17408:17664]
        ex = scr[:, 16384:16384 + 3 * T]
        exs = [ex[0:NE, i * T:(i + 1) * T] for i in range(3)]
        zrow = scr[0:NE, 17152:17152 + T]

        block = ctx.enter_context(nc.Block())

        in0_cols = [(s * 512, min(512, 2328 - s * 512)) for s in range(5)]
        in1_cols = [(s * 512, min(512, 1864 - s * 512)) for s in range(4)]
        in2_cols = [(0, 512), (512, 512), (1024, 192)]

        def source(key):
            kind = key[0]

            def cols(w, o, n):
                return [((0, P), (0, DC * n), w[:, o:o + n].rearrange("(c p) n -> p c n", p=P))]
            if kind == "ada":
                m, s = key[1:]
                w = A[f"l{m}_mod_w"] if m < 2 else A["w_ada_2"][m - 2]
                return cols(w, s * 512, 512)
            if kind == "in0":
                return cols(A["l0_w_in"], *in0_cols[key[1]])
            if kind == "in1":
                return cols(A["l1_w_in"], *in1_cols[key[1]])
            if kind == "in2":
                return cols(A["w_in_2"][key[1]], *in2_cols[key[2]])
            if kind == "lru":
                out = []
                for i, n in enumerate(("l0_lru_wa", "l0_lru_wx")):
                    out.append(((0, P), (i * 256, 256), A[n].rearrange("(a two) i j -> (two i) a j", two=2)))
                for i, n in enumerate(("l0_cmp_w2_k", "l0_cmp_w2_v")):
                    out.append(((0, P), (512 + i * HD, HD), A[n]))
                return out
            if kind == "cmp":
                w = A[("l0_cmp_w1_k", "l0_cmp_w1_v")[key[1]]].rearrange("(l d) n -> d l n", d=HD)
                return [((h * HD, h * HD + HD), (0, CMP_LEN * P), w) for h in range(2)]
            if kind == "out":
                layer, half = key[1:]
                w = A[f"l{layer}_w_out"]
                if layer == 0 and half == 0:
                    return [((0, P), (0, 4096), w[0:512, :].rearrange("(c p) n -> p c n", p=P))]
                out = []
                for g in range(2):
                    o = 512 + g * 256 if layer == 0 else g * 512 + half * 256
                    out.append(((g * HD, g * HD + HD), (0, 4096),
                                w[o:o + 256, :].rearrange("(c d) n -> d c n", d=HD)))
                return out
            if kind == "wg" or kind == "wu":
                n = min(512, F - key[2] * 512)
                return cols(A[f"l{key[1]}_ffn_{kind}"], key[2] * 512, n)
            if kind == "wd":
                n = min(512, F - key[2] * 512)
                w = A[f"l{key[1]}_ffn_wd"][key[2] * 512:key[2] * 512 + n, :]
                return [((0, P), (0, n // P * D), w.rearrange("(c p) n -> p c n", p=P))]
            if kind == "mla":
                l = key[1]
                return [((0, P), (0, 1536), A["w_uq_2"][l].rearrange("(c p) n -> p c n", p=P)),
                        ((0, P), (1536, 1024), A["w_ukv_2"][l]),
                        ((0, P), (2560, 512), A["w_sgu_2"][l].rearrange("h p q -> p h q"))]
            if kind == "tab":
                return [((0, P), (0, C_CAUSAL), A["shape_tables"][:, 0:C_CAUSAL])]
            if kind == "out2":
                w = A["w_out_2"][key[1]][key[2] * 512:key[2] * 512 + 512, :]
                return [((0, P), (0, 4096), w.rearrange("(c p) n -> p c n", p=P))]
            raise ValueError(key)

        def moe_source(layer, kind, group, s, j):
            name = ("w_gate_2", "w_up_2", "w_down_2")[kind]
            w = A[name][layer].rearrange("(g e) (s p) n -> g e s p n", e=GE, p=P)
            if kind < 2:
                return w[group, j, 2 * s:2 * s + 2].rearrange("s p n -> p s n")
            return w[group, j, s]

        @block.sync
        def _(sp):
            sp.dma_start(tab[:, :], A["shape_tables"][:, C_CAUSAL:C_END]).then_inc(loads, 16)
            for t, names in enumerate(VEC_NAMES):
                o = 0
                for n in names:
                    rows = VEC_ROWS[n]
                    a = A[n]
                    if len(a.shape) == 3:
                        a = a.rearrange("l h p -> (l h) p")
                    elif len(a.shape) == 2:
                        a = a.rearrange("a (r p) -> (a r) p", p=P)
                    else:
                        a = a.rearrange("(r p) -> r p", p=P)
                    sp.dma_start(vec_rows[o:o + rows, t, :], a).then_inc(loads, 16)
                    o += rows
            for i, n in enumerate(("l0_cmp_pe_k", "l0_cmp_pe_v")):
                for j in range(2):
                    sp.dma_start(pe_rows[:, i * P + j * HD:i * P + j * HD + HD], A[n]).then_inc(loads, 16)
            sp.dma_start(tok_in[:, :, :], A["x"][0].rearrange("(t p) d -> p t d", p=P)).then_inc(loads, 16)
            sp.dma_start(tok_in2[:, :, :], A["ctx_2"][0].rearrange("(t p) d -> p t d", p=P)).then_inc(loads, 16)

            sp.dma_start(cmp_mask, A["shape_tables"][:, C_CMP:C_CMP + NT * 256].rearrange(
                "p (t n) -> p t n", t=NT)).then_inc(loads, 16)
            for l in range(2):
                sp.dma_start(v3(wrt, l * P, DC, NE), A["w_router_2"][l].rearrange("(c p) n -> p c n", p=P))\
                    .then_inc(loads, 16)

            def load_rows(layer):
                for name, (o, m) in ROWS.items():
                    sp.dma_start(brow[:, o:o + m], A[name][layer:layer + 1, :].to_broadcast([P, m]))\
                        .then_inc(row_loads, 16)

            load_rows(0)
            k = 0
            while k < len(pieces):
                key = pieces[k]
                if key[0] == "moe":
                    layer, per = key[1], 12
                    with sp.Fori(0, NG) as g:
                        for m in range(per):
                            _, _, kind, _, s = pieces[k + m]
                            sp.wait_ge(slots_released, g * per + (k + m - SLOTS + 1))
                            for j in range(GE):
                                dst = slot(k + m)[:, j * 1024:(j + 1) * 1024]
                                if kind < 2:
                                    dst = dst.rearrange("p (s n) -> p s n", s=2)
                                sp.dma_start(dst, moe_source(layer, kind, g, s, j)).then_inc(
                                    slot_loaded[(k + m) % SLOTS], 16)
                    k += per * NG
                    continue
                if k >= SLOTS:
                    sp.wait_ge(slots_released, k - SLOTS + 1)
                for (p0, p1), (o, n), src in source(key):
                    dst = slot(k)[p0:p1, o:o + n]
                    if len(src.shape) == 3:
                        dst = dst.rearrange("p (a b) -> p a b", a=src.shape[1])
                    sp.dma_start(dst, src).then_inc(slot_loaded[k % SLOTS], 16)
                k += 1
                if key == ("mla", 1) and pieces[k - 2] == ("in2", 1, 2) and pieces[k - 3][0] == "moe":
                    sp.wait_ge(slots_released, k - 2)
                    load_rows(1)
            sp.wait_ge(out_copied, DC // 2)
            sp.dma_start(A["out"][0].rearrange("(t p) d -> p t d", p=P), tok_in[:, :, :]).then_inc(stored, 16)
            sp.wait_ge(stored, 16)

        N_LOADS = 16 * (1 + sum(len(n) for n in VEC_NAMES) + 4 + 2 + 1 + 2)
        LAYERS = 2

        def nsa_units():
            return [(qt, c, g) for qt in range(NT) for c in range(4) for g in range(2)]

        def dsa_units():
            return [(qt, cp, g) for qt in range(NT) for cp in range(4) for g in range(2)]

        def mla_units():
            return [(qt, h) for qt in range(NT) for h in range(MH)]

        @block.tensor
        def _(pe):
            n = {"dve": 0, "act": 0, "piece": 0, "phase": 0, "ln": 0, "unit": 0, "ada": 0, "gu": 0,
                 "from_act": 0, "from_dve": 0}
            owed = []

            def mm(out, lhsT, rhs, start=True, stop=True, signal=None):
                ins = nc.tensor.matmul(out, lhsT, rhs, start=start, stop=stop, skip_group_check=True)
                if signal is not None:
                    ins.then_inc(signal, 1)
                elif owed:
                    owed.pop(0)
                    ins.then_inc(slots_released, 1)
                return ins

            def turn(out, in_, signal=None):
                k = in_.shape[0]
                ins = nc.tensor.transpose(out, in_, ident[0:k, 0:k])
                if signal is not None:
                    ins.then_inc(signal, 1)
                return ins

            def barrier():
                n["phase"] += 1
                pe.drain().then_inc(pe_phase, 1)
                pe.wait_ge(act_phase, n["phase"])
                pe.wait_ge(dve_phase, n["phase"])

            def from_dve():
                n["from_dve"] += 1
                pe.wait_ge(dve_made_for_pe, n["from_dve"])

            def from_act():
                n["from_act"] += 1
                pe.wait_ge(act_made_for_pe, n["from_act"])

            def bank_for_dve():
                k = n["dve"]
                n["dve"] += 1
                if k >= 2:
                    pe.wait_ge(dve_read, k - 1)
                return banks[k % 2]

            def bank_for_act():
                k = n["act"]
                n["act"] += 1
                if k >= 2:
                    pe.wait_ge(act_read, k - 1)
                return banks[2 + k % 2]

            def use(key):
                k = n["piece"]
                assert pieces[k] == key, (pieces[k], key)
                n["piece"] += 1
                pe.wait_ge(slot_loaded[k % SLOTS], landed[k])
                return slot(k)

            def release():
                owed.append(1)

            def settle():
                while owed:
                    owed.pop(0)
                    pe.drain().then_inc(slots_released, 1)

            def norm_sums():
                k = n["ln"]
                n["ln"] += 1
                b = bank_for_dve()
                pe.wait_ge(squares_ready, k + 1)
                return b

            def norm(sq):
                b = norm_sums()
                for c in range(DC):
                    mm(b[:, 0:T], ones[:, :], sq[:, c, :], start=(c == 0), stop=(c == DC - 1),
                       signal=pe_to_dve if c == DC - 1 else None)

            def wait_h(c):
                if c % 2 == 0:
                    pe.wait_ge(h_by_dve, (n["ln"] - 1) * 4 + c // 2 + 1)
                else:
                    pe.wait_ge(h_by_act, (n["ln"] - 1) * 4 + c // 2 + 1)

            def to_T(out, w, o, m, h=hT, signal=None):
                for c in range(DC):
                    mm(out, w[:, c, o:o + m], h[:, c, :], start=(c == 0), stop=(c == DC - 1),
                       signal=signal if c == DC - 1 else None)

            def to_tok(out, w, o, m, t, h=hT, signal=None):
                for c in range(DC):
                    mm(out, h[:, c, t * P:(t + 1) * P], w[:, c, o:o + m], start=(c == 0),
                       stop=(c == DC - 1), signal=signal if c == DC - 1 else None)

            def ada_piece(matrix, s):
                w = use(("ada", matrix, s)).rearrange("p (c n) -> p c n", c=DC)
                nc_ = 1 if matrix < 2 else 2
                base = 0 if matrix == 0 else MODO[matrix]
                for j in range(4):
                    o = base + (s * 4 + j) * nc_
                    for c in range(DC):
                        rhs = csil[:, c:c + 1] if matrix < 2 else csil[:, 8 + 2 * c:10 + 2 * c]
                        last = s == 11 and j == 3 and c == DC - 1
                        mm(banks[3][:, o:o + nc_], w[:, c, j * P:(j + 1) * P], rhs,
                           start=(c == 0), stop=(c == DC - 1), signal=ada_done if last else None)
                release()

            def accumulate(out_bank0, lhs, rhs, first, last):
                for c in range(DC):
                    b = banks[out_bank0 + c // 2]
                    mm(b[:, (c % 2) * T:(c % 2 + 1) * T], lhs[:, c * P:(c + 1) * P], rhs,
                       start=first and c % 2 == 0, stop=last,
                       signal=acc_ready if last and c == DC - 1 else None)

            def out_proj(keys, y):
                for half, key in enumerate(keys):
                    w = use(key).rearrange("p (c n) -> p c n", c=4)
                    for k in range(4):
                        accumulate(4, w[:, k, :], y[:, half * 4 + k, :], half == 0 and k == 0,
                                   half == 1 and k == 3)
                    release()

            def ffn(layer, extra):
                keys = ffn_pieces(layer, extra)
                steps = -(-F // 512)

                def down(f, wdp, k, rel):
                    pe.wait_ge(act_ready, f_base + f + 1)
                    accumulate(4, wdp[:, k, :], actT[:, f % 4, :], f == 0, f == FC - 1)
                    if rel:
                        release()
                f_base = n["gu"]
                at = 0
                for s in range(steps):
                    nf = min(4, FC - 4 * s)
                    wg = use(("wg", layer, s))[:, 0:DC * nf * P].rearrange("p (c n) -> p c n", c=DC)
                    wu = use(("wu", layer, s))[:, 0:DC * nf * P].rearrange("p (c n) -> p c n", c=DC)
                    for k in range(nf):
                        f = 4 * s + k
                        b = banks[(f_base + f) % 2]
                        if f >= 2:
                            pe.wait_ge(act_ready, f_base + f - 1)
                        for c in range(DC):
                            if f == 0:
                                wait_h(c)
                            mm(b[:, 0:T], wg[:, c, k * P:(k + 1) * P], hT[:, c, :], start=(c == 0),
                               stop=(c == DC - 1))
                        for c in range(DC):
                            mm(b[:, T:2 * T], wu[:, c, k * P:(k + 1) * P], hT[:, c, :],
                               start=(c == 0), stop=(c == DC - 1),
                               signal=gu_ready if c == DC - 1 else None)
                        if k > 0:
                            if k == 1:
                                wd = use(("wd", layer, s))[:, 0:nf * D].rearrange("p (c n) -> p c n", c=nf)
                            down(f - 1, wd, k - 1, False)
                    release()
                    release()
                    down(4 * s + nf - 1, wd, nf - 1, True)
                    at += 3
                    while at < len(keys) and keys[at][0] == "ada":
                        ada_piece(*keys[at][1:])
                        at += 1
                n["gu"] += FC
                settle()

            def attention(N, S, V, n_blocks, pt_, pr_):
                u0 = n["unit"]
                for i in range(N + 2):
                    if i < N:
                        u = u0 + i
                        if u >= 2:
                            pe.wait_ge(exp_done, u - 1)
                        S(i, banks[4 + u % 2])
                    if 1 <= i <= N:
                        u = u0 + i - 1
                        pe.wait_ge(probs_ready, u + 1)
                        if u >= 2:
                            pe.wait_ge(turned_copied, u - 1)
                        nb = n_blocks(i - 1)
                        for b in range(nb):
                            turn(banks[6 + u % 2][:, b * P:(b + 1) * P],
                                 pr_[:, u % 2, b * P:(b + 1) * P], turned if b == nb - 1 else None)
                    if i >= 2:
                        u = u0 + i - 2
                        pe.wait_ge(turned_copied, u + 1)
                        V(i - 2, pt_[:, u % 2, :])
                n["unit"] += N

            pe.wait_ge(loads, N_LOADS)
            from_dve()
            b = bank_for_dve()
            for t in range(3):
                rows = sum(VEC_ROWS[m] for m in VEC_NAMES[t])
                turn(b[:, t * P:t * P + rows], vec_rows[0:rows, t, :])
            for i in range(2):
                turn(b[:, 384 + i * 32:416 + i * 32], pe_rows[:, i * P:(i + 1) * P],
                     pe_to_dve if i == 1 else None)
            for src in (tok_in, tok_in2):
                for c in range(DC):
                    b = bank_for_dve() if c % 2 == 0 else b
                    for t in range(NT):
                        turn(b[:, (c % 2) * T + t * P:(c % 2) * T + (t + 1) * P],
                             src[:, t, c * P:(c + 1) * P], pe_to_dve if c % 2 and t == 1 else None)
            from_act()
            for s in range(12):
                ada_piece(0, s)

            norm(hT)
            w = use(("in0", 1)).rearrange("p (c n) -> p c n", c=DC)
            for c in range(DC):
                wait_h(c)
            for m in range(LC):
                b = bank_for_dve()
                to_T(b[:, 0:T], w, m * P, P, signal=pe_to_dve)
            release()
            w = use(("in0", 0)).rearrange("p (c n) -> p c n", c=DC)
            for m in range(LC):
                b = bank_for_act()
                to_T(b[:, 0:T], w, m * P, P, signal=pe_to_act)
            release()
            w = use(("in0", 2)).rearrange("p (c n) -> p c n", c=DC)
            for m in range(4):
                b = bank_for_act()
                for g in range(2):
                    to_T(b[g * HD:(g + 1) * HD, 0:T], w, g * 256 + m * HD, HD,
                         signal=pe_to_act if g else None)
            release()
            w = use(("in0", 3)).rearrange("p (c n) -> p c n", c=DC)
            for m in range(2):
                b = bank_for_dve()
                to_T(b[:, 0:T], w, m * P, P, signal=pe_to_dve)
            b = bank_for_act()
            to_T(b[:, 0:T], w, 256, P, signal=pe_to_act)
            b = bank_for_act()
            for t in range(NT):
                to_tok(b[:, t * P:(t + 1) * P], w, 384, P, t, signal=pe_to_act if t else None)
            release()
            w = use(("in0", 4))[:, 0:DC * 280].rearrange("p (c n) -> p c n", c=DC)
            b = bank_for_act()
            to_T(b[:, 0:T], w, 0, P, signal=pe_to_act)
            b = bank_for_act()
            for t in range(NT):
                to_tok(b[:, t * P:(t + 1) * P], w, 128, P, t, signal=pe_to_act if t else None)
            b = bank_for_act()
            for t in range(NT):
                to_tok(b[:, t * 24:(t + 1) * 24], w, 256, 24, t, signal=pe_to_act if t else None)
            release()
            wl = use(("lru",))
            wax = wl[:, 0:512].rearrange("p (i a j) -> p i a j", i=2, a=LC)
            for m in range(LC):
                b = bank_for_act()
                from_dve()
                for i in range(2):
                    for h in range(2):
                        lo = h * HD
                        mm(b[lo:lo + HD, i * T:(i + 1) * T], wax[lo:lo + HD, i, m, :],
                           xc[lo:lo + HD, m, :], start=True, stop=True,
                           signal=pe_to_act if i and h else None)
            b = bank_for_act()
            b2 = bank_for_act()
            for kv in range(2):
                w = use(("cmp", kv)).rearrange("p (l n) -> p l n", l=CMP_LEN)
                from_dve()
                for l in range(CMP_LEN):
                    for g in range(2):
                        lo = g * HD
                        mm((b, b2)[g][:, kv * 16:kv * 16 + NBLK], w[lo:lo + HD, l, :],
                           ft[kv][lo:lo + HD, l // 16, l % 16, :], start=(l == 0),
                           stop=(l == CMP_LEN - 1),
                           signal=pe_to_act if kv and l == CMP_LEN - 1 else None)
            w2 = wl[:, 512:640].rearrange("p (i d) -> p i d", i=2)
            from_act()
            b = bank_for_dve()
            for g in range(2):
                mm(b[g * HD:(g + 1) * HD, 0:NBLK], w2[:, 0, :], h1[:, 0, g, 0:NBLK])
            for j in range(4):
                for g in range(2):
                    mm(b[32 * j:32 * j + NBLK, 64 + g * HD:64 + (g + 1) * HD],
                       h1[:, 1, g, 0:NBLK], w2[:, 1, :],
                       signal=pe_to_dve if j == 3 and g else None)
            for _ in range(3):
                release()
            from_dve()
            for t in range(NT):
                for g in range(2):
                    b = bank_for_dve()
                    mm(b[:, 0:P], ident, cmp_mask[:, t, 0:P], start=True, stop=False)
                    for c in range(4):
                        mm(b[:, c * 32:c * 32 + NBLK], q0[g * HD:(g + 1) * HD, c, t * P:(t + 1) * P],
                           kc[g * HD:(g + 1) * HD, 0:NBLK], start=False, stop=True,
                           signal=pe_to_dve if c == 3 else None)
            for t in range(NT):
                b = bank_for_dve()
                from_dve()
                for i in range(2):
                    turn(b[:, i * P:(i + 1) * P],
                         pc[:, t, 4 * i:4 * i + 4, :].rearrange("p a b -> p (a b)"),
                         pe_to_dve if i else None)
            from_dve()
            units = nsa_units()
            bank = [None]

            def S(i, b):
                qt, c, g = units[i]
                nk, lo = (qt + 1) * P, g * HD
                for s, kk in enumerate((ks0, kw0)):
                    mm(b[:, s * nk:(s + 1) * nk], q0[lo:lo + HD, c, qt * P:(qt + 1) * P],
                       kk[lo:lo + HD, 0:nk], start=(s == 0), stop=False)
                for s in range(2):
                    mm(b[:, (s + 1) * nk - P:(s + 1) * nk], ident, causal, start=False, stop=True,
                       signal=scores_ready if s else None)

            def V(i, ptu):
                qt, c, g = units[i]
                lo, nb = g * HD, qt + 1
                if g == 0:
                    bank[0] = bank_for_dve()
                o = bank[0][lo:lo + HD, 0:P]
                h = 4 * g + c
                mm(o, vc[32 * c:32 * c + NBLK, g, :],
                   pcT[32 * c:32 * c + NBLK, g, qt * P:(qt + 1) * P], start=True, stop=False)
                for s, vt in enumerate((vs0, vw0)):
                    for k in range(nb):
                        last = s == 1 and k == nb - 1
                        mm(o, vt[:, k, lo:lo + HD], ptu[:, (s * nb + k) * P:(s * nb + k + 1) * P],
                           start=False, stop=last, signal=pe_to_dve if last and g else None)

            attention(len(units), S, V, lambda i: 2 * (units[i][0] + 1), pt, pr)
            barrier()
            out_proj([("out", 0, 0), ("out", 0, 1)], yT)
            settle()
            norm(hT)
            ffn(0, ada(1) + ada(2))

            norm(hT)
            for c in range(DC):
                wait_h(c)
            wq = [use(("in1", s)).rearrange("p (c n) -> p c n", c=DC) for s in range(2)]
            for m in range(8):
                b = bank_for_act() if m % 2 else bank_for_dve()
                for g in range(2):
                    to_T(b[g * HD:(g + 1) * HD, 0:T], wq[g], m * HD, HD,
                         signal=(pe_to_act if m % 2 else pe_to_dve) if g else None)
            release()
            release()
            w = use(("in1", 2)).rearrange("p (c n) -> p c n", c=DC)
            w3 = use(("in1", 3))[:, 0:DC * 328].rearrange("p (c n) -> p c n", c=DC)
            b = bank_for_act()
            to_T(b[:, 0:T], w, 0, P, signal=pe_to_act)
            b = bank_for_dve()
            for t in range(NT):
                to_tok(b[:, t * P:(t + 1) * P], w, 128, P, t, signal=pe_to_dve if t else None)
            for m in range(4):
                b = bank_for_act() if m % 2 else bank_for_dve()
                sg = pe_to_act if m % 2 else pe_to_dve
                if m < 2:
                    to_T(b[:, 0:T], w, 256 + m * P, P, signal=sg)
                else:
                    to_T(b[:, 0:T], w3, (m - 2) * P, P, signal=sg)
            b = bank_for_dve()
            for g in range(2):
                to_T(b[g * HD:(g + 1) * HD, 0:T], w3, 256, HD, signal=pe_to_dve if g else None)
            b = bank_for_dve()
            for t in range(NT):
                to_tok(b[:, t * 8:(t + 1) * 8], w3, 320, 8, t, signal=pe_to_dve if t else None)
            release()
            release()
            barrier()
            for t in range(NT):
                for g in range(2):
                    for mp in range(2):
                        b = bank_for_act()
                        for i in range(2):
                            mm(b[:, i * T:(i + 1) * T],
                               qi[g * HD:(g + 1) * HD, 2 * mp + i, t * P:(t + 1) * P],
                               ki[g * HD:(g + 1) * HD, :], signal=pe_to_act if i else None)
            units1 = dsa_units()
            def S1(i, b):
                qt, cp, g = units1[i]
                nk, lo = (qt + 1) * P, g * HD
                if cp == 0 and g == 0:
                    from_dve()
                for s in range(2):
                    mm(b[:, s * nk:(s + 1) * nk], q1[lo:lo + HD, 2 * cp + s, qt * P:(qt + 1) * P],
                       k1[lo:lo + HD, 0:nk], start=(s == 0), stop=False)
                for s in range(2):
                    mm(b[:, s * nk:(s + 1) * nk], ident, sel[:, qt, 0:nk], start=False, stop=True,
                       signal=scores_ready if s else None)

            def V1(i, ptu):
                qt, cp, g = units1[i]
                nb, lo = qt + 1, g * HD
                if g == 0:
                    bank[0] = bank_for_dve()
                b = bank[0]
                for s in range(2):
                    for k in range(nb):
                        last = k == nb - 1
                        mm(b[lo:lo + HD, s * P:(s + 1) * P], v1[:, k, lo:lo + HD],
                           ptu[:, (s * nb + k) * P:(s * nb + k + 1) * P], start=(k == 0), stop=last,
                           signal=pe_to_dve if last and s and g else None)

            attention(len(units1), S1, V1, lambda i: 2 * (units1[i][0] + 1), pt1, pr1)
            barrier()
            out_proj([("out", 1, 0), ("out", 1, 1)], yT)
            settle()
            norm(hT)
            ffn(1, ada(3))
            norm(hT)

            def mixers(layer, stream):
                full_ = stream == 1 or layer == 0
                norm(hT)
                for c in range(DC):
                    wait_h(c)
                if full_:
                    w = use(("in2", layer, 0)).rearrange("p (c n) -> p c n", c=DC)
                    for t in range(NT):
                        b = bank_for_act()
                        to_tok(b[:, :], w, 0, 512, t, signal=pe_to_act)
                    release()
                    w = use(("in2", layer, 1)).rearrange("p (c n) -> p c n", c=DC)
                    for t in range(NT):
                        b = bank_for_dve()
                        to_tok(b[:, :], w, 0, 512, t, signal=pe_to_dve)
                    release()
                w = use(("in2", layer, 2))[:, 0:DC * 192].rearrange("p (c n) -> p c n", c=DC)
                for t in range(NT):
                    b = bank_for_dve()
                    to_tok(b[:, 0:192], w, 0, 192, t, signal=pe_to_dve)
                release()
                wm = use(("mla", layer))
                wuq = wm[:, 0:1536].rearrange("p (c n) -> p c n", c=2)
                wukv = wm[:, 1536:2560]
                wsg = wm[:, 2560:3072].rearrange("p (h q) -> p h q", h=4)
                from_dve()
                for t in range(NT):
                    b = bank_for_dve()
                    if full_:
                        for c in range(2):
                            turn(b[:, c * P:(c + 1) * P], fq[:, t, 256 + c * P:256 + (c + 1) * P])
                    turn(b[:, 2 * P:3 * P], kvr[:, t, 0:P], pe_to_dve)
                    from_dve()
                    for half in range(2 if full_ else 0):
                        b = bank_for_dve()
                        for c in range(2):
                            mm(b[:, 0:384], cqT[:, c, :], wuq[:, c, half * 384:(half + 1) * 384],
                               start=(c == 0), stop=(c == 1), signal=pe_to_dve if c else None)
                    for half in range(2):
                        b = bank_for_dve()
                        mm(b[:, :], cqT[:, 2, :], wukv[:, half * 512:(half + 1) * 512],
                           signal=pe_to_dve)
                    from_dve()
                    for w_ in (0, 1) if full_ else (1,):
                        b = bank_for_dve()
                        for h in range(MH):
                            turn(b[:, h * P:(h + 1) * P], full[:, w_, h, 0:NOPE],
                                 pe_to_dve if h == MH - 1 else None)
                        b = bank_for_dve()
                        for h in range(MH):
                            turn(b[0:ROPE, h * P:(h + 1) * P], full[:, w_, h, NOPE:QKD],
                                 pe_to_dve if h == MH - 1 else None)
                if not full_:
                    release()
                    settle()
                    barrier()
                    return
                b = bank_for_dve()
                for h in range(4):
                    turn(b[:, h * P:(h + 1) * P], wsg[:, h, :], pe_to_dve if h == 3 else None)
                from_dve()
                for t in range(NT):
                    b = bank_for_dve()
                    for h in range(4):
                        mm(b[:, h * HD:(h + 1) * HD], sq2[:, h * P:(h + 1) * P],
                           uv[:, t, 256 + h * HD:256 + (h + 1) * HD],
                           signal=pe_to_dve if h == 3 else None)
                for t in range(NT):
                    b = bank_for_dve()
                    from_dve()
                    for c in range(2):
                        turn(b[:, c * P:(c + 1) * P], uv[:, t, c * P:(c + 1) * P],
                             pe_to_dve if c else None)
                release()
                tb = use(("tab",))
                dftn = tb[:, C_DFTN:C_DFTN + 1024].rearrange("p (t s n) -> p t s n", t=NT, s=2)
                dftd = tb[:, C_DFTD:C_DFTD + 256].rearrange("p (s n) -> p s n", s=2)
                for c in range(2):
                    b = bank_for_dve()
                    for s in range(2):
                        for t in range(NT):
                            mm(b[:, s * T:(s + 1) * T], fq[:, t, c * P:(c + 1) * P], dftn[:, t, s, :],
                               start=(t == 0), stop=(t == 1), signal=pe_to_dve if s and t else None)
                from_dve()
                for c in range(2):
                    b = bank_for_dve()
                    for s in range(2):
                        mm(b[:, 0:T], dftd[:, s, :], acs[:, s, c, :], start=(s == 0), stop=(s == 1),
                           signal=pe_to_dve if s else None)
                release()
                k0, nk = (0, 2 * T) if stream else (0, T)
                units2 = mla_units()

                def S2(i, b):
                    qt, h = units2[i]
                    mm(b[:, 0:nk], qTn[:, h, qt * P:(qt + 1) * P], kTn[:, h, 0:nk], start=True, stop=False)
                    mm(b[:, 0:nk], qTr[0:ROPE, h, qt * P:(qt + 1) * P], kTr[0:ROPE, h, 0:nk],
                       start=False, stop=True, signal=scores_ready)

                def V2(i, ptu):
                    qt, h = units2[i]
                    b = bank_for_dve()
                    nb = nk // P
                    for k in range(nb):
                        mm(b[:, 0:P], vv[:, k, h * P:(h + 1) * P], ptu[:, k * P:(k + 1) * P],
                           start=(k == 0), stop=(k == nb - 1), signal=pe_to_dve if k == nb - 1 else None)

                barrier()
                attention(len(units2), S2, V2, lambda i: nk // P, pt2, pr2)
                barrier()
                out_proj([("out2", layer, 0), ("out2", layer, 1)], yT)
                settle()
                barrier()

            def route(layer, stream):
                norm(mhT)
                for c in range(DC):
                    wait_h(c)
                wr = v3(wrt, layer * P, DC, NE)
                b = bank_for_dve()
                for t in range(NT):
                    to_tok(b[:, t * NE:(t + 1) * NE], wr, 0, NE, t, h=mhT, signal=pe_to_dve if t else None)
                for t in range(NT):
                    for half in range(2):
                        b = bank_for_act()
                        for c in range(4):
                            turn(b[:, c * P:(c + 1) * P], mxn[:, half * 4 + c, t * P:(t + 1) * P],
                                 pe_to_act if c == 3 else None)
                from_dve()
                b = bank_for_dve()
                for t in range(NT):
                    turn(b[0:NE, t * P:(t + 1) * P], small[:, 128 + t * NE:128 + (t + 1) * NE],
                         pe_to_dve if t else None)
                from_dve()
                b = bank_for_dve()
                for t in range(NT):
                    turn(b[:, t * NE:(t + 1) * NE], exs[2][:, t * P:(t + 1) * P],
                         pe_to_dve if t else None)
                from_dve()
                from_act()
                for c in range(DC):
                    b = bank_for_act() if c % 2 else bank_for_dve()
                    for t in range(NT):
                        mm(b[:, :], xtok[:, t, c * P:(c + 1) * P], pm[:, t, :], start=(t == 0),
                           stop=(t == 1), signal=(pe_to_act if c % 2 else pe_to_dve) if t else None)
                for half in range(2):
                    b = bank_for_dve()
                    for g in range(2):
                        for t in range(NT):
                            turn(b[:, g * T + t * P:g * T + (t + 1) * P],
                                 pg[:, t, (half * 2 + g) * P:(half * 2 + g + 1) * P],
                                 pe_to_dve if g and t else None)
                barrier()

            def experts(layer, streams):
                k0 = n["piece"]
                ns = len(streams)
                assert pieces[k0][0] == "moe"
                per = 12
                gain = [sum(16 * GE for m in range(per) if (k0 + m) % SLOTS == s) for s in range(SLOTS)]
                base = NG * layer
                base_s = 2 * NG * layer
                with pe.Fori(0, NG) as g:
                    def piece(m):
                        k = k0 + m
                        pe.wait_ge(slot_loaded[k % SLOTS], g * gain[k % SLOTS] + landed[k])
                        return slot(k)
                    pe.wait_ge(xs_ready, g + (base + 1))
                    for kind in range(2):
                        for s4 in range(4):
                            w = piece(kind * 4 + s4).rearrange("p (e s n) -> p e s n", e=GE, s=2)
                            for c2 in range(2):
                                c = 2 * s4 + c2
                                for i, s in enumerate(streams):
                                    b = banks[2 * s + kind]
                                    for j in range(GE):
                                        lastp = c2 == 1 and i == ns - 1 and j == GE - 1
                                        ins = nc.tensor.matmul(
                                            b[32 * j:32 * j + 32, :], xs[s][:, c, 32 * j:32 * j + 32],
                                            w[:, j, c2, :], start=(c == 0), stop=(c == DC - 1),
                                            skip_group_check=True)
                                        if lastp:
                                            ins.then_inc(slots_released, 1)
                    pe.drain().then_inc(gu_done, 1)
                    for i, s in enumerate(streams):
                        pe.wait_ge(hid_ready, g * ns + (base_s + i + 1))
                        for f in range(4):
                            ins = nc.tensor.transpose(banks[2 * s][:, f * P:(f + 1) * P],
                                                      hid[s][:, f * P:(f + 1) * P], ident)
                        ins.then_inc(hid_turned, 1)
                    pe.wait_ge(y_read, g + (base + 1))
                    for f in range(4):
                        w = piece(8 + f).rearrange("p (e n) -> p e n", e=GE)
                        for i, s in enumerate(streams):
                            if f == 0:
                                pe.wait_ge(hid_copied, g * ns + (base_s + i + 1))
                            for half in range(2):
                                for j in range(GE):
                                    lastp = half == 1 and i == ns - 1 and j == GE - 1
                                    ins = nc.tensor.matmul(
                                        banks[4 + 2 * s + half][32 * j:32 * j + 32, :],
                                        hidT[s][:, f, 32 * j:32 * j + 32],
                                        w[:, j, half * 512:(half + 1) * 512], start=(f == 0),
                                        stop=(f == 3), skip_group_check=True)
                                    if lastp:
                                        ins.then_inc(slots_released, 1)
                    pe.drain().then_inc(y_ready, 1)
                n["piece"] += per * NG
                barrier()
                for s in streams:
                    if s != streams[0]:
                        barrier()
                    for g in range(NG):
                        accumulate(4, ys[s][:, g, :], pgT[s][:, g, :], g == 0, g == NG - 1)
                barrier()

            for layer in range(LAYERS):
                mixers(layer, 0)
                mixers(layer, 1)
                for s in ((0, 1) if layer == 0 else (1,)):
                    route(layer, s)
                experts(layer, (0, 1) if layer == 0 else (1,))
            for c in range(DC):
                b = banks[c // 2]
                for t in range(NT):
                    turn(b[:, (c % 2) * T + t * P:(c % 2) * T + (t + 1) * P],
                         xT[:, c, t * P:(t + 1) * P], pe_to_dve if c % 2 and t else None)

        @block.scalar
        def _(act):
            n = {"act": 0, "phase": 0, "ln": 0, "chain": 0, "gu": 0, "unit": 0, "from_dve": 0}

            def barrier():
                n["phase"] += 1
                act.drain().then_inc(act_phase, 1)
                act.wait_ge(pe_phase, n["phase"])
                act.wait_ge(dve_phase, n["phase"])

            def link(ins):
                n["chain"] += 1
                ins.then_inc(act_chain, 1)
                act.wait_ge(act_chain, n["chain"])

            def job():
                k = n["act"]
                n["act"] += 1
                act.wait_ge(pe_to_act, k + 1)
                return banks[2 + k % 2]

            def from_dve():
                n["from_dve"] += 1
                act.wait_ge(dve_made_for_act, n["from_dve"])

            def norm(src, dst, xn_, B, std_, sq, A_):
                k = n["ln"]
                n["ln"] += 1
                nc.scalar.activation(sq, src, ACT.Square).then_inc(squares_ready, 1)
                act.wait_ge(var_ready, k + 1)
                nc.scalar.activation(std_, std_, ACT.Sqrt).then_inc(std_ready, 1)
                act.wait_ge(xn_ready, k + 1)
                for c in range(1, DC, 2):
                    nc.scalar.activation(dst[:, c, :], xn_[:, c, :], ACT.Identity,
                                         scale=A_(c), bias=B(c) if B else 0.0).then_inc(h_by_act, 1)

            def ffn():
                for f in range(FC):
                    k = n["gu"]
                    n["gu"] += 1
                    act.wait_ge(gu_ready, k + 1)
                    if f >= 2:
                        act.wait_ge(act_ready, k - 1)
                    nc.scalar.activation(sil[:, k % 2, :], banks[k % 2][:, 0:T], ACT.Silu)\
                        .then_inc(silu_ready, 1)

            def attention(N, segs, pr_, pt_, scale, nb_of, sums, negs):
                u0 = n["unit"]
                for i in range(N + 1):
                    if i < N:
                        u = u0 + i
                        nb = nb_of(i)
                        nk = nb * P // segs
                        act.wait_ge(negmax_ready, u + 1)
                        for s in range(segs):
                            ins = nc.scalar.activation(
                                pr_[:, u % 2, s * nk:(s + 1) * nk], banks[4 + u % 2][:, s * nk:(s + 1) * nk],
                                ACT.Exp, bias=negs[:, (u % 2) * 2 + s:(u % 2) * 2 + s + 1], scale=scale,
                                accum_out=sums[:, (u % 2) * 2 + s:(u % 2) * 2 + s + 1])
                        ins.then_inc(exp_done, 1)
                    if i >= 1:
                        u = u0 + i - 1
                        nb = nb_of(i - 1)
                        act.wait_ge(turned, u + 1)
                        nc.scalar.copy(pt_[:, u % 2, 0:nb * P], banks[6 + u % 2][:, 0:nb * P])\
                            .then_inc(turned_copied, 1)
                n["unit"] += N

            negs, sums = small[:, 84:88], small[:, 88:92]

            from_dve()
            nc.scalar.activation(csil[:, 0:8], vec("c", 0, 8), ACT.Silu)
            cs = csil[:, 8:24].rearrange("p (c s) -> p s c", s=2)
            nc.scalar.activation(cs[:, 0, :], vec("c_2", 0, 8), ACT.Silu)
            nc.scalar.activation(cs[:, 1, :], vec("c_ctx_2", 0, 8), ACT.Silu).then_inc(act_made_for_pe, 1)
            link(nc.scalar.activation(lam[:, 0:4], vec("l0_lru_lambda", 0, 4), ACT.Abs))
            link(nc.scalar.activation(lam[:, 4:8], lam[:, 0:4], ACT.Exp, scale=-1.0))
            nc.scalar.activation(lam[:, 8:12], lam[:, 4:8], ACT.Ln, bias=1.0).then_inc(act_made_for_dve, 1)

            from_dve()
            norm(xT, hT, xn, lambda c: mod(0, 0, c), std, hT, lambda c: ac(0, c))
            for m in range(LC):
                b = job()
                nc.scalar.activation(gg[:, m, :], b[:, 0:T], ACT.Gelu_apprx_tanh).then_inc(act_read, 1)
            for m in range(4):
                b = job()
                nc.scalar.copy(q0[:, m, :], b[:, 0:T]).then_inc(act_read, 1)
            b = job()
            nc.scalar.copy(ks0, b[:, 0:T]).then_inc(act_read, 1)
            b = job()
            nc.scalar.copy(vs0, b[:, 0:T].rearrange("p (a b) -> p a b", a=2)).then_inc(act_read, 1)
            b = job()
            nc.scalar.copy(kw0, b[:, 0:T]).then_inc(act_read, 1)
            b = job()
            nc.scalar.copy(vw0, b[:, 0:T].rearrange("p (a b) -> p a b", a=2)).then_inc(act_read, 1)
            b = job()
            nc.scalar.activation(gts.rearrange("p t h k -> p (t h k)"), b[:, 0:48], ACT.Sigmoid)\
                .then_inc(act_read, 1)
            for m in range(LC):
                b = job()
                nc.scalar.activation(rr[:, m, :], b[:, 0:T], ACT.Sigmoid, bias=vec("l0_lru_ba", m))
                nc.scalar.activation(ii[:, m, :], b[:, T:2 * T], ACT.Sigmoid, bias=vec("l0_lru_bx", m))\
                    .then_inc(act_read, 1)
            act.wait_ge(act_read, n["act"])
            for m in range(LC):
                nc.scalar.activation(aa[:, m, :], rr[:, m, :], ACT.Exp, scale=lam[:, 12 + m:13 + m])
                ins = nc.scalar.activation(th[:, m, :], rr[:, m, :], ACT.Tanh, scale=lam[:, 16 + m:17 + m])
            ins.then_inc(act_made_for_dve, 1)
            g1 = job()
            g2 = job()
            for g, b in enumerate((g1, g2)):
                for kv in range(2):
                    ins = nc.scalar.activation(h1[:, kv, g, 0:NBLK], b[:, kv * 16:kv * 16 + NBLK],
                                               ACT.Gelu_apprx_tanh)
                    if kv:
                        ins.then_inc(act_read, 1)
            act.drain().then_inc(act_made_for_pe, 1)
            from_dve()
            nc.scalar.activation(th, th, ACT.Sqrt).then_inc(act_made_for_dve, 1)
            for t in range(NT):
                from_dve()
                nc.scalar.activation(pc[:, t], pc[:, t], ACT.Exp, scale=HD ** -0.5).then_inc(act_made_for_dve, 1)
            units = nsa_units()
            attention(len(units), 2, pr, pt, HD ** -0.5, lambda i: 2 * (units[i][0] + 1), sums, negs)
            barrier()
            from_dve()
            norm(xT, hT, xn, lambda c: mod(0, 3, c), std, hT, lambda c: ac(1, c))
            ffn()

            from_dve()
            norm(xT, hT, xn, lambda c: mod(1, 0, c), std, hT, lambda c: ac(2, c))
            for m in range(1, 8, 2):
                b = job()
                nc.scalar.copy(q1[:, m, :], b[:, 0:T]).then_inc(act_read, 1)
            b = job()
            nc.scalar.copy(k1, b[:, 0:T]).then_inc(act_read, 1)
            for m in (1, 3):
                b = job()
                nc.scalar.copy(qi[:, m, :], b[:, 0:T]).then_inc(act_read, 1)
            barrier()
            for t in range(NT):
                for m in range(4):
                    b = job()
                    k = t * 4 + m
                    if k >= 2:
                        act.wait_ge(index_added, 2 * (k - 1))
                    nc.scalar.activation(rel[:, k % 2, :], b[:, :], ACT.Relu, scale=HD ** -0.5)\
                        .then_inc(act_read, 1)
                    act.drain().then_inc(act_made_for_dve, 1)
            units1 = dsa_units()
            attention(len(units1), 2, pr1, pt1, HD ** -0.5, lambda i: 2 * (units1[i][0] + 1), sums, negs)
            barrier()
            from_dve()
            norm(xT, hT, xn, lambda c: mod(1, 3, c), std, hT, lambda c: ac(3, c))
            ffn()
            from_dve()
            norm(xT, xT, xn, None, std, hT, lambda c: vec("final_norm", c))

            def mixers(layer, stream):
                full_ = stream == 1 or layer == 0
                src = xT if stream else cT
                cond = 0 if stream else 1
                from_dve()
                norm(src, hT, xn, lambda c: mod(2 + layer, 0, c, 1, cond), std, hT,
                     lambda c: ac(4, c))
                if full_:
                    for t in range(NT):
                        b = job()
                        nc.scalar.activation(uv[:, t, :], b[:, :], ACT.Gelu_apprx_tanh).then_inc(act_read, 1)
                    act.drain().then_inc(act_made_for_dve, 1)
                from_dve()
                nc.scalar.activation(small[:, 112:118], small[:, 112:118], ACT.Sqrt)\
                    .then_inc(act_made_for_dve, 1)
                for t in range(NT):
                    from_dve()
                    nc.scalar.activation(small[:, 120:128], small[:, 120:128], ACT.Sqrt)\
                        .then_inc(act_made_for_dve, 1)
                if full_:
                    barrier()
                    units2 = mla_units()
                    nk = 2 * T if stream else T
                    attention(len(units2), 1, pr2, pt2, QKD ** -0.5, lambda i: nk // P, sums, negs)
                    barrier()
                barrier()

            def route(layer, stream):
                src = xT if stream else cT
                cond = 0 if stream else 1
                from_dve()
                norm(src, mhT, mxn, lambda c: mod(2 + layer, 3, c, 1, cond), mstd, mhT,
                     lambda c: ac(8, c))
                for t in range(NT):
                    for half in range(2):
                        b = job()
                        nc.scalar.copy(xtok[:, t, half * 512:(half + 1) * 512], b[:, :]).then_inc(act_read, 1)
                act.drain().then_inc(act_made_for_pe, 1)
                from_dve()
                nc.scalar.activation(small[:, 128:128 + NT * NE], small[:, 128:128 + NT * NE], ACT.Exp)\
                    .then_inc(act_made_for_dve, 1)
                for c in range(1, DC, 2):
                    b = job()
                    nc.scalar.activation(xsT[stream][:, c, :], b[:, :], ACT.Identity, scale=ac(8, c),
                                         bias=mod(2 + layer, 3, c, 1, cond)).then_inc(act_read, 1)
                barrier()

            def experts(layer, streams):
                ns = len(streams)
                base = NG * layer
                base_s = 2 * NG * layer
                with act.Fori(0, NG) as g:
                    for i, s in enumerate(streams):
                        ins = nc.scalar.copy(xs[s], xsT[s][:, :, bass.ts(g, P)])
                    ins.then_inc(xs_ready, 1)
                    act.wait_ge(gu_done, g + (base + 1))
                    for i, s in enumerate(streams):
                        ins = nc.scalar.activation(hid[s], banks[2 * s][:, :], ACT.Silu)
                        ins.then_inc(hid_silu, 1)
                    for i, s in enumerate(streams):
                        act.wait_ge(hid_turned, g * ns + (base_s + i + 1))
                        nc.scalar.copy(hidT[s], banks[2 * s][:, :].rearrange("p (a b) -> p a b", a=4))\
                            .then_inc(hid_copied, 1)
                barrier()
                for s in streams[1:]:
                    barrier()
                barrier()

            for layer in range(LAYERS):
                mixers(layer, 0)
                mixers(layer, 1)
                for s in ((0, 1) if layer == 0 else (1,)):
                    route(layer, s)
                experts(layer, (0, 1) if layer == 0 else (1,))

        @block.vector
        def _(dve):
            n = {"dve": 0, "phase": 0, "ln": 0, "chain": 0, "gu": 0, "unit": 0, "from_act": 0, "acc": 0,
                 "ada": 0, "index": 0}

            def barrier():
                n["phase"] += 1
                dve.drain().then_inc(dve_phase, 1)
                dve.wait_ge(pe_phase, n["phase"])
                dve.wait_ge(act_phase, n["phase"])

            def link(ins):
                n["chain"] += 1
                ins.then_inc(dve_chain, 1)
                dve.wait_ge(dve_chain, n["chain"])

            def job():
                k = n["dve"]
                n["dve"] += 1
                dve.wait_ge(pe_to_dve, k + 1)
                return banks[k % 2]

            def from_act():
                n["from_act"] += 1
                dve.wait_ge(act_made_for_dve, n["from_act"])

            tt, ts_, stt = nc.vector.tensor_tensor, nc.vector.tensor_scalar, nc.vector.scalar_tensor_tensor

            def bc(ap, axis, shape):
                return ap.unsqueeze(axis).to_broadcast(shape)

            def norm(src, dst, xn_, B, std_, A_):
                k = n["ln"]
                n["ln"] += 1
                b = job()
                ts_(std_, b[:, 0:T], 1.0 / D, EPS, ALU.mult, ALU.add).then_inc(var_ready, 1)
                dve.wait_ge(std_ready, k + 1)
                link(nc.vector.reciprocal(b[:, T:2 * T], std_))
                tt(xn_, src, bc(b[:, T:2 * T], 1, [P, DC, T]), ALU.mult).then_inc(dve_read, 1)
                dve.drain().then_inc(xn_ready, 1)
                dve.wait_ge(xn_ready, k + 1)
                for c in range(0, DC, 2):
                    if B is None:
                        ins = ts_(dst[:, c, :], xn_[:, c, :], A_(c), None, ALU.mult)
                    else:
                        ins = ts_(dst[:, c, :], xn_[:, c, :], A_(c), B(c), ALU.mult, ALU.add)
                    ins.then_inc(h_by_dve, 1)

            def residual(dst, gate):
                n["acc"] += 1
                dve.wait_ge(acc_ready, n["acc"])
                for c in range(DC):
                    ins = stt(dst[:, c, :], banks[4 + c // 2][:, (c % 2) * T:(c % 2 + 1) * T], gate(c),
                              dst[:, c, :], ALU.mult, ALU.add)
                return ins

            def ada_out(matrix):
                n["ada"] += 1
                dve.wait_ge(ada_done, n["ada"])
                m = 1 if matrix < 2 else 2
                src = banks[3][:, MODO[matrix] if matrix else 0:(MODO[matrix] if matrix else 0) + 48 * m]
                dst = mods[:, MODO[matrix]:MODO[matrix] + 48 * m]
                if matrix < 2:
                    bias = vec(f"l{matrix}_mod_b", 0, 48)
                else:
                    bias = bc(vec("b_ada_2", (matrix - 2) * 48, 48), 2, [P, 48, 2])
                    src = src.rearrange("p (a b) -> p a b", b=2)
                    dst = dst.rearrange("p (a b) -> p a b", b=2)
                ins = tt(dst, src, bias, ALU.add)
                link(ins)

            def scale_cols(i, matrix, seg, cond=0, gain=None):
                s = mod(matrix, seg, 0, 8, cond)
                if gain is None:
                    return ts_(ac(i, 0, 8), s, 1.0, None, ALU.add)
                return stt(ac(i, 0, 8), s, 1.0, vec(gain, 0, 8), ALU.add, ALU.mult)

            def ffn(extra):
                for f in range(FC):
                    k = n["gu"]
                    n["gu"] += 1
                    dve.wait_ge(silu_ready, k + 1)
                    tt(actT[:, f % 4, :], sil[:, k % 2, :], banks[k % 2][:, T:2 * T], ALU.mult)\
                        .then_inc(act_ready, 1)
                    if f in done_at(extra):
                        ada_out(done_at(extra)[f])

            def done_at(extra):
                out, keys = {}, ffn_pieces(0, sum((ada(m) for m in extra), []))
                step = -1
                for key in keys:
                    if key[0] == "wg":
                        step += 1
                    if key[0] == "ada" and key[2] == 11:
                        out[min(4 * step + 3, FC - 1)] = key[1]
                return out

            def attention(N, segs, pr_, scale, nb_of, sums, negs, gate, V, every):
                u0 = n["unit"]
                rs = small[:, 94:98]
                for i in range(N + 2):
                    if i < N:
                        u = u0 + i
                        nk = nb_of(i) * P // segs
                        dve.wait_ge(scores_ready, u + 1)
                        ng = negs[:, (u % 2) * 2:(u % 2) * 2 + segs]
                        link(nc.vector.tensor_reduce(
                            ng, banks[4 + u % 2][:, 0:segs * nk].rearrange("p (s k) -> p s k", s=segs),
                            X, ALU.max))
                        ts_(ng, ng, FLOOR, -scale, ALU.max, ALU.mult).then_inc(negmax_ready, 1)
                    if 1 <= i <= N:
                        u = u0 + i - 1
                        nk = nb_of(i - 1) * P // segs
                        dve.wait_ge(exp_done, u + 1)
                        sm = sums[:, (u % 2) * 2:(u % 2) * 2 + segs]
                        r = rs[:, (u % 2) * 2:(u % 2) * 2 + segs]
                        link(ts_(r, sm, 1e-30, None, ALU.max))
                        link(nc.vector.reciprocal(r, r))
                        if gate is not None:
                            link(tt(r, r, gate(i - 1), ALU.mult))
                        for s in range(segs):
                            p_ = pr_[:, u % 2, s * nk:(s + 1) * nk]
                            ins = ts_(p_, p_, r[:, s:s + 1], None, ALU.mult)
                        ins.then_inc(probs_ready, 1)
                    if i >= 2 and (i - 2) % every == every - 1:
                        b = job()
                        V(i - 2, b)
                n["unit"] += N

            negs, sums = small[:, 84:88], small[:, 88:92]

            nc.vector.memset(ones[:, :], 1.0).then_inc(dve_made_for_pe, 1)
            dve.wait_ge(loads, N_LOADS)
            b = job()
            for t in range(3):
                rows = sum(VEC_ROWS[m] for m in VEC_NAMES[t])
                nc.vector.tensor_copy(vecs[:, t * P:t * P + rows], b[:, t * P:t * P + rows])
            nc.vector.tensor_copy(peT, b[:, 384:448]).then_inc(dve_read, 1)
            dve.drain().then_inc(dve_made_for_act, 1)
            for dst in (xT, cT):
                for c in range(0, DC, 2):
                    b = job()
                    nc.vector.tensor_copy(dst[:, c:c + 2, :], b[:, :].rearrange("p (a b) -> p a b", a=2))\
                        .then_inc(dve_read, 1)
            from_act()
            link(ts_(lam[:, 12:16], vec("l0_lru_lambda", 0, 4), -1.0, 0.0, ALU.mult, ALU.max))
            e_, l_, s_ = lam[:, 4:8], lam[:, 8:12], lam[:, 12:16]
            w1, w2, w3 = small[:, 100:104], small[:, 104:108], small[:, 108:112]
            link(ts_(w1, e_, 1.0, None, ALU.add))
            link(ts_(w1, w1, 1.0, None, ALU.subtract))
            link(ts_(w2, w1, 0.0, None, ALU.is_equal))
            link(tt(w1, w1, w2, ALU.add))
            link(nc.vector.reciprocal(w1, w1))
            link(tt(w1, w1, e_, ALU.mult))
            link(tt(w1, w1, l_, ALU.mult))
            link(tt(w3, w2, e_, ALU.mult))
            link(tt(w1, w1, w3, ALU.add))
            link(tt(s_, s_, w1, ALU.add))
            link(ts_(lam[:, 16:20], s_, 8.0, None, ALU.mult))
            link(ts_(s_, s_, -8.0, None, ALU.mult))
            ada_out(0)
            scale_cols(0, 0, 1, gain="l0_norm_mix")
            scale_cols(1, 0, 4, gain="l0_norm_ffn")
            dve.drain().then_inc(dve_made_for_act, 1)

            norm(xT, hT, xn, lambda c: mod(0, 0, c), std, lambda c: ac(0, c))
            link(nc.vector.memset(axp[:, :, 0:3], 0.0))
            for m in range(LC):
                b = job()
                nc.vector.tensor_copy(axp[:, m, 3:], b[:, 0:T]).then_inc(dve_read, 1)
                dve.wait_ge(dve_read, n["dve"])
                link(ts_(xc[:, m, :], axp[:, m, 0:T], vec("l0_conv_w", m), vec("l0_conv_b", m),
                         ALU.mult, ALU.add))
                for k in range(1, 4):
                    ins = stt(xc[:, m, :], axp[:, m, k:k + T], vec("l0_conv_w", 4 * k + m), xc[:, m, :],
                              ALU.mult, ALU.add)
                    if k < 3:
                        link(ins)
                ins.then_inc(dve_made_for_pe, 1)
            for kv in range(2):
                b = job()
                src = b[:, 0:T].rearrange("p (b l) -> p l b", l=CMP_STRIDE)
                for hf in range(2):
                    pos = peT[:, kv * 32 + hf * 16:kv * 32 + hf * 16 + 16]
                    ins = tt(ft[kv][:, hf], src[:, :, hf:hf + NBLK], bc(pos, 2, [P, CMP_STRIDE, NBLK]),
                             ALU.add)
                ins.then_inc(dve_read, 1)
                dve.drain().then_inc(dve_made_for_pe, 1)
            from_act()
            link(tt(rr, aa, aa, ALU.mult))
            stt(th, rr, 1.0, th, ALU.add, ALU.mult).then_inc(dve_made_for_act, 1)
            b = job()
            nc.vector.tensor_copy(kc[:, 0:NBLK], b[:, 0:NBLK])
            for j in range(4):
                ins = nc.vector.tensor_copy(vc[32 * j:32 * j + NBLK],
                                            b[32 * j:32 * j + NBLK, 64:192].rearrange("p (g d) -> p g d", g=2))
            ins.then_inc(dve_read, 1)
            dve.drain().then_inc(dve_made_for_pe, 1)
            from_act()
            nc.vector.memset(th[:, :, 0:1], 1.0)
            link(tt(ii, ii, xc, ALU.mult))
            dve.drain().then_inc(dve_chain, 1)
            n["chain"] += 1
            dve.wait_ge(dve_chain, n["chain"])
            link(tt(ii, ii, th, ALU.mult))
            for m in range(LC):
                ins = nc.vector.tensor_tensor_scan(xc[:, m, :], aa[:, m, :], ii[:, m, :], 0.0,
                                                   ALU.mult, ALU.add)
                link(ins)
            link(tt(yT[:, 0:4, :], xc, gg, ALU.mult))
            mx, sm8 = small[:, 100:108], small[:, 108:116]
            for t in range(NT):
                for g in range(2):
                    b = job()
                    s3 = b[:, 0:P].rearrange("p (h k) -> p h k", h=4)
                    mg = mx[:, 4 * g:4 * g + 4]
                    link(nc.vector.tensor_reduce(mg, s3, X, ALU.max))
                    link(ts_(mg, mg, FLOOR, None, ALU.max))
                    tt(pc[:, t, 4 * g:4 * g + 4, :], s3, bc(mg, 2, [P, 4, 32]), ALU.subtract)\
                        .then_inc(dve_read, 1)
                dve.drain().then_inc(dve_made_for_act, 1)
                from_act()
                link(nc.vector.tensor_reduce(sm8, pc[:, t], X, ALU.add))
                link(ts_(sm8, sm8, 1e-30, None, ALU.max))
                link(nc.vector.reciprocal(sm8, sm8))
                link(tt(sm8, sm8, gts[:, t, :, 0], ALU.mult))
                tt(pc[:, t], pc[:, t], bc(sm8, 2, [P, 8, 32]), ALU.mult).then_inc(dve_made_for_pe, 1)
            for t in range(NT):
                b = job()
                nc.vector.tensor_copy(pcT[:, :, t * P:(t + 1) * P],
                                      b[:, 0:256].rearrange("p (a b) -> p a b", a=2)).then_inc(dve_read, 1)
            dve.drain().then_inc(dve_made_for_pe, 1)
            units = nsa_units()

            def V0(i, b):
                qt, c, g = units[i]
                nc.vector.tensor_copy(yT[:, 4 + c, qt * P:(qt + 1) * P], b[:, 0:P]).then_inc(dve_read, 1)

            def gate0(i):
                qt, c, g = units[i]
                return gts[:, qt, 4 * g + c, 1:3]

            attention(len(units), 2, pr, HD ** -0.5, lambda i: 2 * (units[i][0] + 1), sums, negs, gate0,
                      V0, 2)
            barrier()
            residual(xT, lambda c: mod(0, 2, c))
            dve.drain().then_inc(dve_made_for_act, 1)
            norm(xT, hT, xn, lambda c: mod(0, 3, c), std, lambda c: ac(1, c))
            ffn([1, 2])
            residual(xT, lambda c: mod(0, 5, c))
            scale_cols(2, 1, 1, gain="l1_norm_mix")
            scale_cols(3, 1, 4, gain="l1_norm_ffn")
            scale_cols(4, 2, 1, 0)
            scale_cols(5, 2, 1, 1)
            dve.drain().then_inc(dve_made_for_act, 1)

            norm(xT, hT, xn, lambda c: mod(1, 0, c), std, lambda c: ac(2, c))
            for m in range(0, 8, 2):
                b = job()
                nc.vector.tensor_copy(q1[:, m, :], b[:, 0:T]).then_inc(dve_read, 1)
            b = job()
            nc.vector.tensor_copy(v1, b[:, 0:T].rearrange("p (a b) -> p a b", a=2)).then_inc(dve_read, 1)
            for m in (0, 2):
                b = job()
                nc.vector.tensor_copy(qi[:, m, :], b[:, 0:T]).then_inc(dve_read, 1)
            b = job()
            nc.vector.tensor_copy(ki, b[:, 0:T]).then_inc(dve_read, 1)
            b = job()
            ts_(wi.rearrange("p t h -> p (t h)"), b[:, 0:16], IDX_HEADS ** -0.5, None, ALU.mult)\
                .then_inc(dve_read, 1)
            barrier()
            for t in range(NT):
                for m in range(4):
                    k = t * 4 + m
                    from_act()
                    for i in range(2):
                        g, mp = m // 2, m % 2
                        h = 4 * mp + 2 * i + g
                        r = rel[:, k % 2, i * T:(i + 1) * T]
                        if h == 0:
                            ins = ts_(idx[:, t, :], r, wi[:, t, h:h + 1], None, ALU.mult)
                        else:
                            ins = stt(idx[:, t, :], r, wi[:, t, h:h + 1], idx[:, t, :], ALU.mult, ALU.add)
                        n["index"] += 1
                        ins.then_inc(index_added, 1)
                        dve.wait_ge(index_added, n["index"])
                nk = (t + 1) * P
                link(tt(idx[:, t, nk - P:nk], idx[:, t, nk - P:nk], causal, ALU.add))
                m8 = small[:, 100:108]
                src = idx[:, t, 0:nk]
                wk = work[:, t, 0:nk]
                for r in range(TOPK // 8):
                    link(nc.vector.max(m8, src))
                    link(nc.vector.match_replace(wk, m8, src, TAKEN))
                    src = wk
                link(ts_(sel[:, t, 0:nk], wk, TAKEN / 2, NEG, ALU.is_gt, ALU.mult))
                tt(sel[:, t, nk - P:nk], sel[:, t, nk - P:nk], causal, ALU.add).then_inc(dve_made_for_pe, 1)
            units1 = dsa_units()

            def V1(i, b):
                qt, cp, g = units1[i]
                nc.vector.tensor_copy(yT[:, 2 * cp:2 * cp + 2, qt * P:(qt + 1) * P],
                                      b[:, 0:2 * P].rearrange("p (s t) -> p s t", s=2)).then_inc(dve_read, 1)

            attention(len(units1), 2, pr1, HD ** -0.5, lambda i: 2 * (units1[i][0] + 1), sums, negs, None,
                      V1, 2)
            barrier()
            residual(xT, lambda c: mod(1, 2, c))
            dve.drain().then_inc(dve_made_for_act, 1)
            norm(xT, hT, xn, lambda c: mod(1, 3, c), std, lambda c: ac(3, c))
            ffn([3])
            residual(xT, lambda c: mod(1, 5, c))
            dve.drain().then_inc(dve_made_for_act, 1)
            norm(xT, xT, xn, None, std, lambda c: vec("final_norm", c))

            def row(name):
                o, m = ROWS[name]
                return brow[:, o:o + m]

            def mixers(layer, stream):
                full_ = stream == 1 or layer == 0
                src = xT if stream else cT
                cond = 0 if stream else 1
                scale_cols(4, 2 + layer, 1, cond)
                dve.drain().then_inc(dve_made_for_act, 1)
                norm(src, hT, xn, lambda c: mod(2 + layer, 0, c, 1, cond), std, lambda c: ac(4, c))
                for t in range(NT if full_ else 0):
                    b = job()
                    nc.vector.tensor_copy(fq[:, t, :], b[:, :]).then_inc(dve_read, 1)
                for t in range(NT):
                    b = job()
                    nc.vector.tensor_copy(kvr[:, t, :], b[:, 0:192]).then_inc(dve_read, 1)
                if full_:
                    from_act()
                ms = small[:, 112:118]
                dve.wait_ge(dve_read, n["dve"])
                if not full_:
                    nc.vector.memset(ms, 1.0)
                    dve.drain().then_inc(dve_chain, 1)
                    n["chain"] += 1
                    dve.wait_ge(dve_chain, n["chain"])
                latents = [(4, lambda t: kvr[:, t, 0:P])]
                if full_:
                    latents += [(0, lambda t: uv[:, t, 256:512]), (2, lambda t: fq[:, t, 256:512])]
                for o, view in latents:
                    for t in range(NT):
                        v = view(t)
                        link(nc.vector.tensor_tensor_reduce(
                            sq2[:, 0:v.shape[1]], v, v, 1.0, 0.0, ALU.mult, ALU.add, ms[:, o + t:o + t + 1]))
                link(ts_(ms[:, 0:4], ms[:, 0:4], 1.0 / 256, EPS, ALU.mult, ALU.add))
                ts_(ms[:, 4:6], ms[:, 4:6], 1.0 / 128, EPS, ALU.mult, ALU.add).then_inc(dve_made_for_act, 1)
                from_act()
                link(nc.vector.reciprocal(ms, ms))
                names = {4: "kv_lora_norm_2", 0: "sgu_norm_2", 2: "q_lora_norm_2"}
                dve.wait_ge(row_loads, 16 * len(ROWS) * (layer + 1))
                for o, view in latents:
                    for t in range(NT):
                        v = view(t)
                        ins = stt(v, v, ms[:, o + t:o + t + 1], row(names[o]), ALU.mult, ALU.mult)
                ins.then_inc(dve_made_for_pe, 1)
                hs = small[:, 120:128]
                kept = slice(0, 2) if full_ else slice(1, 2)
                for t in range(NT):
                    b = job()
                    lo = 0 if full_ else 2
                    nc.vector.tensor_copy(cqT[:, lo:3, :], b[:, lo * P:3 * P].rearrange(
                        "p (a b) -> p a b", b=P)).then_inc(dve_read, 1)
                    dve.drain().then_inc(dve_made_for_pe, 1)
                    for half in range(2 if full_ else 0):
                        b = job()
                        nc.vector.tensor_copy(full[:, 0, 2 * half:2 * half + 2, :],
                                              b[:, 0:384].rearrange("p (a b) -> p a b", a=2)).then_inc(dve_read, 1)
                    kt = 2 * stream + t
                    for half in range(2):
                        b = job()
                        kvb = b[:, :].rearrange("p (h w d) -> p h w d", h=2, w=2)
                        nc.vector.tensor_copy(full[:, 1, 2 * half:2 * half + 2, 0:NOPE], kvb[:, :, 0, :])
                        nc.vector.tensor_copy(vv[:, kt, half * 256:(half + 1) * 256].rearrange(
                            "p (h d) -> p h d", h=2), kvb[:, :, 1, :]).then_inc(dve_read, 1)
                    link(nc.vector.tensor_copy(full[:, 1, :, NOPE:QKD],
                                               bc(kvr[:, t, P:P + ROPE], 1, [P, MH, ROPE])))
                    dve.drain().then_inc(dve_chain, 1)
                    n["chain"] += 1
                    dve.wait_ge(dve_chain, n["chain"])
                    if not full_:
                        link(nc.vector.memset(hs, 1.0))
                    sqv = sq2.rearrange("p (h d) -> p h d", h=MH)
                    for w in range(2)[kept]:
                        link(tt(sqv, full[:, w], full[:, w], ALU.mult))
                        link(nc.vector.tensor_reduce(hs[:, w * 4:w * 4 + 4], sqv, X, ALU.add))
                    ts_(hs, hs, 1.0 / QKD, EPS, ALU.mult, ALU.add).then_inc(dve_made_for_act, 1)
                    from_act()
                    link(nc.vector.reciprocal(hs, hs))
                    for w in range(2)[kept]:
                        fw = full[:, w]
                        gain = row(("q_norm_2", "k_norm_2")[w])
                        link(tt(fw, fw, bc(hs[:, w * 4:w * 4 + 4], 2, [P, MH, QKD]), ALU.mult))
                        ins = tt(fw, fw, bc(gain, 1, [P, MH, QKD]), ALU.mult)
                        if stream:
                            link(ins)
                            rot = fw[:, :, NOPE:QKD]
                            ra = sq2[:, 0:256].rearrange("p (h d) -> p h d", h=MH)
                            rb = sq2[:, 256:512].rearrange("p (h d) -> p h d", h=MH)
                            tt(ra, rot, bc(ropes[:, t, 0, :], 1, [P, MH, ROPE]), ALU.mult)
                            for rc in range(2):
                                for hf in range(2):
                                    a, o = rc * 32 + (1 - hf) * 16, rc * 32 + hf * 16
                                    ins = tt(rb[:, :, o:o + 16], rot[:, :, a:a + 16],
                                             bc(ropes[:, t, 1, o:o + 16], 1, [P, MH, 16]), ALU.mult)
                            link(ins)
                            ins = tt(rot, ra, rb, ALU.add)
                            if w == 0:
                                link(ins)
                    ins.then_inc(dve_made_for_pe, 1)
                    for w in range(2)[kept]:
                        o = (0 if w == 0 else T * stream) + t * P
                        for part, dst in enumerate(((qTn, kTn)[w], (qTr, kTr)[w])):
                            b = job()
                            rows = P if part == 0 else ROPE
                            nc.vector.tensor_copy(dst[0:rows, :, o:o + P],
                                                  b[0:rows, :].rearrange("p (h t) -> p h t", h=MH))\
                                .then_inc(dve_read, 1)
                if not full_:
                    barrier()
                    return
                b = job()
                nc.vector.tensor_copy(sq2[:, 0:512], b[:, :]).then_inc(dve_read, 1)
                dve.drain().then_inc(dve_made_for_pe, 1)
                for t in range(NT):
                    b = job()
                    for h in range(4):
                        u = uv[:, t, h * HD:(h + 1) * HD]
                        ins = stt(u, b[:, h * HD:(h + 1) * HD], vec("b_sgu_2", layer * 4 + h), u,
                                  ALU.add, ALU.mult)
                    ins.then_inc(dve_read, 1)
                    dve.drain().then_inc(dve_made_for_pe, 1)
                for t in range(NT):
                    b = job()
                    nc.vector.tensor_copy(yT[:, 0:2, t * P:(t + 1) * P],
                                          b[:, 0:2 * P].rearrange("p (c t) -> p c t", c=2)).then_inc(dve_read, 1)
                for c in range(2):
                    b = job()
                    nc.vector.tensor_copy(acs[:, :, c, :], b[:, :].rearrange("p (s n) -> p s n", s=2))\
                        .then_inc(dve_read, 1)
                dve.drain().then_inc(dve_made_for_pe, 1)
                for c in range(2):
                    b = job()
                    nc.vector.tensor_copy(yT[:, 2 + c, :], b[:, 0:T]).then_inc(dve_read, 1)
                barrier()
                units2 = mla_units()
                nk = 2 * T if stream else T

                def V2(i, b):
                    qt, h = units2[i]
                    nc.vector.tensor_copy(yT[:, 4 + h, qt * P:(qt + 1) * P], b[:, 0:P]).then_inc(dve_read, 1)

                attention(len(units2), 1, pr2, QKD ** -0.5, lambda i: nk // P, sums, negs, None, V2, 1)
                barrier()
                residual(src, lambda c: mod(2 + layer, 2, c, 1, cond))
                barrier()

            def route(layer, stream):
                src = xT if stream else cT
                cond = 0 if stream else 1
                scale_cols(8, 2 + layer, 4, cond)
                dve.drain().then_inc(dve_made_for_act, 1)
                norm(src, mhT, mxn, lambda c: mod(2 + layer, 3, c, 1, cond), mstd, lambda c: ac(8, c))
                aff = small[:, 128:160].rearrange("p (t e) -> p t e", t=NT)
                place = small[:, 160:192].rearrange("p (t e) -> p t e", t=NT)
                m2 = small[:, 100:102]
                b = job()
                lg = b[:, 0:32].rearrange("p (t e) -> p t e", t=NT)
                link(nc.vector.tensor_reduce(m2, lg, X, ALU.max))
                tt(aff, lg, bc(m2, 2, [P, NT, NE]), ALU.subtract).then_inc(dve_read, 1)
                dve.drain().then_inc(dve_made_for_act, 1)
                from_act()
                link(nc.vector.tensor_reduce(m2, aff, X, ALU.add))
                link(nc.vector.reciprocal(m2, m2))
                tt(aff, aff, bc(m2, 2, [P, NT, NE]), ALU.mult).then_inc(dve_made_for_pe, 1)
                b = job()
                arow, wrow, prow = exs
                link(nc.vector.tensor_copy(arow, b[0:NE, 0:T]))
                nc.vector.memset(zrow, 0.0).then_inc(dve_read, 1)
                m8 = small[0:NE, 104:112]
                s_ = arow
                for r in range(CAP // 8):
                    link(nc.vector.max(m8, s_))
                    link(nc.vector.match_replace(wrow, m8, s_, -1.0))
                    s_ = wrow
                link(ts_(arow, wrow, 0.0, None, ALU.is_lt))
                link(nc.vector.tensor_tensor_scan(prow, arow, zrow, 0.0, ALU.add, ALU.add))
                tt(prow, prow, arow, ALU.mult).then_inc(dve_made_for_pe, 1)
                b = job()
                nc.vector.tensor_copy(small[:, 160:192], b[:, 0:32]).then_inc(dve_read, 1)
                dve.drain().then_inc(dve_chain, 1)
                n["chain"] += 1
                dve.wait_ge(dve_chain, n["chain"])
                for t in range(NT):
                    one = pm[:, t, :].rearrange("p (e s) -> p e s", e=NE)
                    wtd = pg[:, t, :].rearrange("p (e s) -> p e s", e=NE)
                    link(tt(one, bc(iota1, 1, [P, NE, CAP]), bc(place[:, t, :], 2, [P, NE, CAP]),
                            ALU.is_equal))
                    ins = tt(wtd, one, bc(aff[:, t, :], 2, [P, NE, CAP]), ALU.mult)
                ins.then_inc(dve_made_for_pe, 1)
                for c in range(0, DC, 2):
                    b = job()
                    ts_(xsT[stream][:, c, :], b[:, :], ac(8, c), mod(2 + layer, 3, c, 1, cond),
                        ALU.mult, ALU.add).then_inc(dve_read, 1)
                for half in range(2):
                    b = job()
                    nc.vector.tensor_copy(pgT[stream][:, 2 * half:2 * half + 2, :],
                                          b[:, :].rearrange("p (g t) -> p g t", g=2)).then_inc(dve_read, 1)
                barrier()

            def experts(layer, streams):
                ns = len(streams)
                base = NG * layer
                base_s = 2 * NG * layer
                if layer == 0:
                    dve.drain().then_inc(y_read, 1)
                with dve.Fori(0, NG) as g:
                    for i, s in enumerate(streams):
                        dve.wait_ge(hid_silu, g * ns + (base_s + i + 1))
                        tt(hid[s], hid[s], banks[2 * s + 1][:, :], ALU.mult).then_inc(hid_ready, 1)
                    dve.wait_ge(y_ready, g + (base + 1))
                    for s in streams:
                        for half in range(2):
                            ins = nc.vector.tensor_copy(
                                ys[s].rearrange("p g d -> p (g d)")[:, bass.ds(g * D + half * 512, 512)],
                                banks[4 + 2 * s + half][:, :])
                    ins.then_inc(y_read, 1)
                barrier()
                for s in streams:
                    if s != streams[0]:
                        barrier()
                    residual((cT, xT)[s], lambda c: mod(2 + layer, 5, c, 1, 1 - s))
                barrier()

            for layer in range(LAYERS):
                mixers(layer, 0)
                mixers(layer, 1)
                for s in ((0, 1) if layer == 0 else (1,)):
                    route(layer, s)
                experts(layer, (0, 1) if layer == 0 else (1,))
            for c in range(0, DC, 2):
                job()
                b = banks[c // 2]
                nc.vector.tensor_copy(
                    tok_in[:, :, c * P:(c + 2) * P].rearrange("p t (c q) -> p c t q", c=2),
                    b[:, :].rearrange("p (c t q) -> p c t q", c=2, t=NT)).then_inc(out_copied, 1)


INS = ["x", "c", "l0_norm_mix", "l0_norm_ffn", "l0_mod_w", "l0_mod_b", "l0_w_in", "l0_conv_w",
       "l0_conv_b", "l0_lru_wa", "l0_lru_ba", "l0_lru_wx", "l0_lru_bx", "l0_lru_lambda",
       "l0_cmp_pe_k", "l0_cmp_w1_k", "l0_cmp_w2_k", "l0_cmp_pe_v", "l0_cmp_w1_v", "l0_cmp_w2_v",
       "l0_w_out", "l0_ffn_wg", "l0_ffn_wu", "l0_ffn_wd", "l1_norm_mix", "l1_norm_ffn", "l1_mod_w",
       "l1_mod_b", "l1_w_in", "l1_w_out", "l1_ffn_wg", "l1_ffn_wu", "l1_ffn_wd", "final_norm", "c_2",
       "ctx_2", "c_ctx_2", "w_ada_2", "b_ada_2", "w_in_2", "sgu_norm_2", "w_sgu_2", "b_sgu_2",
       "q_lora_norm_2", "w_uq_2", "kv_lora_norm_2", "w_ukv_2", "q_norm_2", "k_norm_2", "w_out_2",
       "w_router_2", "w_gate_2", "w_up_2", "w_down_2"]


def shape_tables():
    tab = np.zeros((P, C_END), np.float64)
    n = np.arange(T)
    ang = 2 * np.pi * (np.outer(n, n) % T) / T
    dft = np.stack([np.cos(ang), np.sin(ang)], 1) / np.sqrt(T)
    tab[:, C_DFTN:C_DFTN + 1024] = dft.reshape(NT, P, 2 * T).transpose(1, 0, 2).reshape(P, -1)
    d = np.arange(64)
    angd = 2 * np.pi * (np.outer(d, d) % 64) / 64
    for g in range(2):
        o = g * 64
        tab[o:o + 64, C_DFTD + o:C_DFTD + o + 64] = np.cos(angd) / 8
        tab[o:o + 64, C_DFTD + P + o:C_DFTD + P + o + 64] = -np.sin(angd) / 8
    q = np.arange(P)
    tab[:, C_CAUSAL:C_CAUSAL + P] = np.where(q[None, :] > q[:, None], NEG, 0.0)
    blk = np.arange(32)
    for t in range(NT):
        seen = (blk[None, :] * CMP_STRIDE + CMP_LEN - 1 <= (t * P + q)[:, None]) & (blk[None, :] < NBLK)
        tab[:, C_CMP + t * 256:C_CMP + (t + 1) * 256] = np.tile(np.where(seen, 0.0, NEG), (1, 8))
    tab[:, C_IDENT:C_IDENT + P] = np.eye(P)
    tab[:, C_IOTA:C_IOTA + CAP] = np.arange(1, CAP + 1)
    freqs = (np.float32(10000.0) ** (-np.arange(16, dtype=np.float32) / np.float32(16))).astype(np.float32)
    for t in range(NT):
        tok = t * P + q
        for rc, pos in enumerate((tok // 64, tok % 64)):
            a = (pos[:, None].astype(np.float32) * freqs).astype(np.float64)
            o = C_ROPE + t * 128 + rc * 32
            for hf in range(2):
                tab[:, o + hf * 16:o + hf * 16 + 16] = np.cos(a)
                tab[:, o + 64 + hf * 16:o + 64 + hf * 16 + 16] = np.sin(a) * (1 if hf else -1)
    return tab.astype(np.float32)


def kernel(**inputs):
    import concourse.bacc as bacc
    from concourse.bass_utils import run_bass_kernel_spmd

    nc = bacc.Bacc("TRN2", target_bir_lowering=False, num_devices=1)
    arrays, aps = {}, {}
    for name in INS:
        a = np.ascontiguousarray(inputs[name])
        arrays[f"in_{name}"] = a
        aps[name] = nc.dram_tensor(f"in_{name}", a.shape, mybir.dt.from_np(a.dtype), kind="ExternalInput").ap()
    table = shape_tables()
    arrays["shape_tables"] = table
    aps["shape_tables"] = nc.dram_tensor("shape_tables", table.shape, F32, kind="ExternalInput").ap()
    aps["out"] = nc.dram_tensor("out", (1, T, D), F32, kind="ExternalOutput").ap()
    program(nc, aps)
    r = run_bass_kernel_spmd(nc, [arrays], core_ids=[0])
    return r.results[0]["out"]
```

```python
from contextlib import ExitStack

import numpy as np

import concourse.bass as bass
from concourse import mybir

F32 = mybir.dt.float32
ACT = mybir.ActivationFunctionType
ALU = mybir.AluOpType
X = mybir.AxisListType.X

P = 128
D = 1024
DC = D // P
T = 256
NT = T // P
F = 2816
FC = F // P
EPS = 1e-6
HD = 64
TAKEN = -3e38
NEG = -1e30
FLOOR = -1e20

LRU = 512
LC = LRU // P
CMP_LEN, CMP_STRIDE = 32, 16
NBLK = (T - CMP_LEN) // CMP_STRIDE + 1
TOPK = min(256, T // 4)
IDX_HEADS = 8

NE, CAP, DE = 16, 2 * T // 16, 512
GE = P // CAP
NG = NE // GE
MH, NOPE, ROPE = 4, 128, 64
QKD = NOPE + ROPE

SLOTS = 6
SLOT = 4096

C_DFTN, C_DFTD = 0, 1024
C_CMP = C_DFTD + 256
C_CAUSAL = C_CMP + NT * 256
C_IDENT = C_CAUSAL + P
C_IOTA = C_IDENT + P
C_ROPE = C_IOTA + CAP
C_END = C_ROPE + NT * 2 * 64

VEC_NAMES = [
    ["l0_mod_b", "l1_mod_b", "l0_norm_mix", "l0_norm_ffn", "l1_norm_mix", "l1_norm_ffn"],
    ["b_ada_2", "final_norm", "c", "c_2", "c_ctx_2"],
    ["l0_conv_w", "l0_conv_b", "l0_lru_ba", "l0_lru_bx", "l0_lru_lambda", "b_sgu_2"],
]
VEC_ROWS = {"l0_mod_b": 48, "l1_mod_b": 48, "l0_norm_mix": 8, "l0_norm_ffn": 8, "l1_norm_mix": 8,
            "l1_norm_ffn": 8, "b_ada_2": 96, "final_norm": 8, "c": 8, "c_2": 8, "c_ctx_2": 8,
            "l0_conv_w": 16, "l0_conv_b": 4, "l0_lru_ba": 4, "l0_lru_bx": 4, "l0_lru_lambda": 4, "b_sgu_2": 8}


ROWS = {"sgu_norm_2": (0, 256), "q_lora_norm_2": (256, 256), "kv_lora_norm_2": (512, 128),
        "q_norm_2": (640, QKD), "k_norm_2": (832, QKD)}


def ffn_pieces(layer, extra):
    out, extra = [], list(extra)
    steps = -(-F // 512)
    per = -(-len(extra) // steps)
    for s in range(steps):
        out += [("wg", layer, s), ("wu", layer, s), ("wd", layer, s)]
        out += extra[:per]
        del extra[:per]
    return out


def ada_after(extra):
    out, step = {}, -1
    for key in ffn_pieces(0, extra):
        step += key[0] == "wg"
        if key[0] == "ada":
            f = min(4 * step + 3, FC - 1)
            out[f] = out.get(f, 0) + 1
    return out


def ada(matrix, first=0, end=12):
    return [("ada", matrix, s) for s in range(first, end)]


ADA_AT = {
    "start": ada(0, 0, 4),
    "lru": ada(0, 4, 8),
    "attention0": ada(0, 8, 12) + ada(1, 0, 4),
    "ffn0": ada(1, 4, 12) + ada(2, 0, 4),
    "norm1": ada(2, 4, 5),
    "attention1": ada(2, 5, 12) + ada(3, 0, 1),
    "ffn1": ada(3, 1, 12),
}


def weight_pieces():
    out = list(ADA_AT["start"])
    out += [("in0", s) for s in (1, 0, 2, 3, 4)]
    out += [("lru",), ("cmp", 0), ("cmp", 1)] + ADA_AT["lru"] + ADA_AT["attention0"]
    out += [("out", 0, 0), ("out", 0, 1)]
    out += ffn_pieces(0, ADA_AT["ffn0"]) + ADA_AT["norm1"]
    out += [("in1", s) for s in range(4)] + ADA_AT["attention1"] + [("out", 1, 0), ("out", 1, 1)]
    out += ffn_pieces(1, ADA_AT["ffn1"])
    for layer in range(2):
        for stream in ("ctx", "x"):
            full = stream == "x" or layer == 0
            out += [("in2", layer, s) for s in ((0, 1, 2) if full else (2,))]
            out += [("mla", layer)]
            if full:
                out += [("tab",), ("out2", layer, 0), ("out2", layer, 1)]
        for g in range(NG):
            out += [("moe", layer, kind, g, s) for kind in range(3) for s in range(4)]
    return out


def program(nc, A):
    ctx = ExitStack()
    with ctx:
        def sb(name, cols):
            return ctx.enter_context(nc.sbuf_tensor(name, [P, cols], F32))

        def sem(name):
            return ctx.enter_context(nc.semaphore(name))

        ring = sb("ring", SLOTS * SLOT)
        xT_ = sb("xT", DC * T)
        cT_ = sb("ctxT", DC * T)
        hT_ = sb("hT", DC * T)
        tab = sb("tab", C_END - C_CAUSAL)
        ones = sb("ones", P)
        vecs = sb("vecs", 2 * P + 48)
        mods = sb("mods", 48 * 6)
        acol = sb("acol", 72)
        csil_ = sb("csil", DC * 32)
        small = sb("small", 200)
        brow = sb("brow", 1024)
        SCR = 19456
        scr = sb("scr", SCR)
        banks = [ctx.enter_context(nc.psum_tensor(f"bank{i}", [P, 512], F32)) for i in range(8)]

        def v3(t, o, a, b):
            return t[:, o:o + a * b].rearrange("p (a b) -> p a b", a=a)

        csil, wrt = v3(csil_, 0, DC, 32), csil_
        xT, cT, hT = v3(xT_, 0, DC, T), v3(cT_, 0, DC, T), v3(hT_, 0, DC, T)
        causal = tab[:, 0:P]
        ident = tab[:, C_IDENT - C_CAUSAL:C_IDENT - C_CAUSAL + P]
        iota1 = tab[:, C_IOTA - C_CAUSAL:C_IOTA - C_CAUSAL + CAP]
        ropes = tab[:, C_ROPE - C_CAUSAL:C_END - C_CAUSAL].rearrange("p (t s n) -> p t s n", t=NT, s=2)

        vcol, o = {}, 0
        for t, names in enumerate(VEC_NAMES):
            o = t * P
            for n in names:
                vcol[n] = o
                o += VEC_ROWS[n]

        def vec(name, c=0, n=1):
            return vecs[:, vcol[name] + c:vcol[name] + c + n]

        MODO = [0, 48, 96, 192]

        def mod(matrix, seg, c, n=1, cond=0):
            if matrix < 2:
                o = MODO[matrix] + seg * 8 + c
                return mods[:, o:o + n]
            o = MODO[matrix] + (seg * 8 + c) * 2 + cond
            return mods[:, o:o + 2 * n - 1:2] if n > 1 else mods[:, o:o + 1]

        def ac(i, c=0, n=1):
            return acol[:, i * 8 + c:i * 8 + c + n]

        pieces = weight_pieces()
        index = {}
        for k, key in enumerate(pieces):
            index.setdefault(key, []).append(k)
        n_dma = {"lru": 4, "cmp": 2, "mla": 3, "moe": GE, "out": 1}

        def dmas_of(key):
            if key[0] == "out" and key[1:] == (0, 1) or key[0] == "out" and key[1] == 1:
                return 2
            if key[0] == "moe" and key[2] == 2:
                return GE
            return n_dma.get(key[0], 1)

        landed, count = [], [0] * SLOTS
        for k, key in enumerate(pieces):
            count[k % SLOTS] += 16 * dmas_of(key)
            landed.append(count[k % SLOTS])

        def slot(k):
            return ring[:, (k % SLOTS) * SLOT:(k % SLOTS + 1) * SLOT]

        slot_loaded = [sem(f"slot_loaded{i}") for i in range(SLOTS)]
        slots_released = sem("slots_released")

        loads = sem("loads")
        row_loads = sem("row_loads")
        out_copied, stored = sem("out_copied"), sem("stored")
        pe_to_dve, dve_read = sem("pe_to_dve"), sem("dve_read")
        pe_to_act, act_read = sem("pe_to_act"), sem("act_read")
        pe_phase, act_phase, dve_phase = sem("pe_phase"), sem("act_phase"), sem("dve_phase")
        dve_chain, act_chain = sem("dve_chain"), sem("act_chain")
        dve_made_for_pe, act_made_for_pe = sem("dve_made_for_pe"), sem("act_made_for_pe")
        dve_made_for_act, act_made_for_dve = sem("dve_made_for_act"), sem("act_made_for_dve")
        x_ready = sem("x_ready")
        squares_ready, var_ready = sem("squares_ready"), sem("var_ready")
        std_ready, xn_ready, h_ready = sem("std_ready"), sem("xn_ready"), sem("h_ready")
        ada_rows, ada_copied = sem("ada_rows"), sem("ada_copied")
        ada_cols, ada_read = sem("ada_cols"), sem("ada_read")
        gu_ready, silu_ready, act_ready = sem("gate_up_ready"), sem("silu_ready"), sem("act_ready")
        acc_ready = sem("acc_ready")
        scores_ready, negmax_ready, exp_done = sem("scores_ready"), sem("negmax_ready"), sem("exp_done")
        probs_ready, turned, turned_copied = sem("probs_ready"), sem("turned"), sem("turned_copied")
        index_added = sem("index_added")
        xs_ready, gu_done, hid_silu, hid_ready = sem("xs_ready"), sem("gu_done"), sem("hid_silu"), sem("hid_ready")
        hid_turned, hid_copied, y_ready, y_read = sem("hid_turned"), sem("hid_copied"), sem("y_ready"), sem("y_read")

        class Arena:
            def __init__(self, at=0):
                self.at = at

            def take(self, *shape):
                n = 1
                for s in shape:
                    n *= s
                ap = scr[:, self.at:self.at + n]
                self.at += n
                assert self.at <= SCR, self.at
                if len(shape) == 2:
                    ap = ap.rearrange("p (a b) -> p a b", a=shape[0])
                elif len(shape) == 3:
                    ap = ap.rearrange("p (a b c) -> p a b c", a=shape[0], b=shape[1])
                return ap

        xn = v3(scr, 0, DC, T)
        std = scr[:, 2048:2304]
        tok_in = v3(scr, 4096, NT, D)
        tok_in2 = v3(scr, 6144, NT, D)
        vec_rows = v3(scr, 8192, 3, P)
        pe_rows = scr[0:CMP_LEN, 8576:8576 + 256]
        peT = small[:, 0:64]
        selector = small[:, 192:195]
        lam = small[:, 64:84]

        a0 = Arena(2304)
        axp = a0.take(LC, T + 3)
        xc = a0.take(LC, T)
        gg = a0.take(LC, T)
        rr = a0.take(LC, T)
        ii = a0.take(LC, T)
        aa = a0.take(LC, T)
        th = a0.take(LC, T)
        q0 = a0.take(4, T)
        ks0, kw0 = a0.take(T), a0.take(T)
        vs0, vw0 = a0.take(NT, P), a0.take(NT, P)
        gts = a0.take(NT, 8, 3)
        ft = [a0.take(2, CMP_STRIDE, NBLK) for _ in range(2)]
        h1 = a0.take(2, 2, CMP_STRIDE)
        kc = a0.take(CMP_STRIDE)
        vc = a0.take(2, HD)
        pc = a0.take(NT, 8, 32)
        pcT = a0.take(2, T)
        cmp_mask = a0.take(NT, 256)
        assert a0.at - NT * 256 >= 8832
        pr = a0.take(2, 512)
        pt = a0.take(2, 512)
        a1 = Arena(2304)
        q1 = a1.take(8, T)
        k1 = a1.take(T)
        v1 = a1.take(NT, P)
        qi = a1.take(4, T)
        ki = a1.take(T)
        wi = a1.take(NT, IDX_HEADS)
        idx = a1.take(NT, T)
        work = a1.take(NT, T)
        sel = a1.take(NT, T)
        rel = a1.take(2, 512)
        pr1 = a1.take(2, 512)
        pt1 = a1.take(2, 512)
        yT = v3(scr, 0, DC, T)
        assert a1.at + 0 < SCR
        af = Arena(2304)
        sil = af.take(2, T)
        actT = af.take(4, T)
        a2 = Arena(2304)
        kTn = a2.take(MH, 2 * T)
        kTr = a2.take(MH, 2 * T)
        vv = a2.take(4, 512)
        uv = a2.take(NT, 512)
        fq = a2.take(NT, 512)
        kvr = a2.take(NT, 192)
        full = a2.take(2, MH, QKD)
        sq2 = a2.take(MH * QKD)
        qTn = a2.take(MH, T)
        qTr = a2.take(MH, T)
        pr2 = a2.take(2, 512)
        pt2 = a2.take(2, 512)
        acs = a2.take(2, 2, T)
        cqT = a2.take(3, P)
        am = Arena(0)
        xsT = [am.take(DC, NE * CAP) for _ in range(2)]
        ys = [am.take(NG, D) for _ in range(2)]
        xs = [am.take(DC, P) for _ in range(2)]
        hid = [brow[:, s * 512:(s + 1) * 512] for s in range(2)]
        hidT = [am.take(4, P) for _ in range(2)]
        ay = Arena(8192)
        mxn = ay.take(DC, T)
        mhT = ay.take(DC, T)
        xtok = ay.take(NT, D)
        pm = ay.take(NT, NE * CAP)
        pg = ay.take(NT, NE * CAP)
        pgT = [v3(hT_, s * 1024, NG, T) for s in range(2)]
        mstd = scr[:, 17408:17664]
        ex = scr[:, 16384:16384 + 3 * T]
        exs = [ex[0:NE, i * T:(i + 1) * T] for i in range(3)]
        zrow = scr[0:NE, 17152:17152 + T]

        block = ctx.enter_context(nc.Block())

        in0_cols = [(s * 512, min(512, 2328 - s * 512)) for s in range(5)]
        in1_cols = [(s * 512, min(512, 1864 - s * 512)) for s in range(4)]
        in2_cols = [(0, 512), (512, 512), (1024, 192)]

        def source(key):
            kind = key[0]

            def cols(w, o, n):
                return [((0, P), (0, DC * n), w[:, o:o + n].rearrange("(c p) n -> p c n", p=P))]
            if kind == "ada":
                m, s = key[1:]
                w = A[f"l{m}_mod_w"] if m < 2 else A["w_ada_2"][m - 2]
                return cols(w, s * 512, 512)
            if kind == "in0":
                return cols(A["l0_w_in"], *in0_cols[key[1]])
            if kind == "in1":
                return cols(A["l1_w_in"], *in1_cols[key[1]])
            if kind == "in2":
                return cols(A["w_in_2"][key[1]], *in2_cols[key[2]])
            if kind == "lru":
                out = []
                for i, n in enumerate(("l0_lru_wa", "l0_lru_wx")):
                    out.append(((0, P), (i * 256, 256), A[n].rearrange("(a two) i j -> (two i) a j", two=2)))
                for i, n in enumerate(("l0_cmp_w2_k", "l0_cmp_w2_v")):
                    out.append(((0, P), (512 + i * HD, HD), A[n]))
                return out
            if kind == "cmp":
                w = A[("l0_cmp_w1_k", "l0_cmp_w1_v")[key[1]]].rearrange("(l d) n -> d l n", d=HD)
                return [((h * HD, h * HD + HD), (0, CMP_LEN * P), w) for h in range(2)]
            if kind == "out":
                layer, half = key[1:]
                w = A[f"l{layer}_w_out"]
                if layer == 0 and half == 0:
                    return [((0, P), (0, 4096), w[0:512, :].rearrange("(c p) n -> p c n", p=P))]
                out = []
                for g in range(2):
                    o = 512 + g * 256 if layer == 0 else g * 512 + half * 256
                    out.append(((g * HD, g * HD + HD), (0, 4096),
                                w[o:o + 256, :].rearrange("(c d) n -> d c n", d=HD)))
                return out
            if kind == "wg" or kind == "wu":
                n = min(512, F - key[2] * 512)
                return cols(A[f"l{key[1]}_ffn_{kind}"], key[2] * 512, n)
            if kind == "wd":
                n = min(512, F - key[2] * 512)
                w = A[f"l{key[1]}_ffn_wd"][key[2] * 512:key[2] * 512 + n, :]
                return [((0, P), (0, n // P * D), w.rearrange("(c p) n -> p c n", p=P))]
            if kind == "mla":
                l = key[1]
                return [((0, P), (0, 1536), A["w_uq_2"][l].rearrange("(c p) n -> p c n", p=P)),
                        ((0, P), (1536, 1024), A["w_ukv_2"][l]),
                        ((0, P), (2560, 512), A["w_sgu_2"][l].rearrange("h p q -> p h q"))]
            if kind == "tab":
                return [((0, P), (0, C_CAUSAL), A["shape_tables"][:, 0:C_CAUSAL])]
            if kind == "out2":
                w = A["w_out_2"][key[1]][key[2] * 512:key[2] * 512 + 512, :]
                return [((0, P), (0, 4096), w.rearrange("(c p) n -> p c n", p=P))]
            raise ValueError(key)

        def moe_source(layer, kind, group, s, j):
            name = ("w_gate_2", "w_up_2", "w_down_2")[kind]
            w = A[name][layer].rearrange("(g e) (s p) n -> g e s p n", e=GE, p=P)
            if kind < 2:
                return w[group, j, 2 * s:2 * s + 2].rearrange("s p n -> p s n")
            return w[group, j, s]

        @block.sync
        def _(sp):
            sp.dma_start(tab[:, :], A["shape_tables"][:, C_CAUSAL:C_END]).then_inc(loads, 16)
            for t, names in enumerate(VEC_NAMES):
                o = 0
                for n in names:
                    rows = VEC_ROWS[n]
                    a = A[n]
                    if len(a.shape) == 3:
                        a = a.rearrange("l h p -> (l h) p")
                    elif len(a.shape) == 2:
                        a = a.rearrange("a (r p) -> (a r) p", p=P)
                    else:
                        a = a.rearrange("(r p) -> r p", p=P)
                    sp.dma_start(vec_rows[o:o + rows, t, :], a).then_inc(loads, 16)
                    o += rows
            for i, n in enumerate(("l0_cmp_pe_k", "l0_cmp_pe_v")):
                for j in range(2):
                    sp.dma_start(pe_rows[:, i * P + j * HD:i * P + j * HD + HD], A[n]).then_inc(loads, 16)
            sp.dma_start(tok_in[:, :, :], A["x"][0].rearrange("(t p) d -> p t d", p=P)).then_inc(loads, 16)
            sp.dma_start(tok_in2[:, :, :], A["ctx_2"][0].rearrange("(t p) d -> p t d", p=P)).then_inc(loads, 16)

            sp.dma_start(cmp_mask, A["shape_tables"][:, C_CMP:C_CMP + NT * 256].rearrange(
                "p (t n) -> p t n", t=NT)).then_inc(loads, 16)

            def load_rows(layer):
                for name, (o, m) in ROWS.items():
                    sp.dma_start(brow[:, o:o + m], A[name][layer:layer + 1, :].to_broadcast([P, m]))\
                        .then_inc(row_loads, 16)

            k = 0
            while k < len(pieces):
                key = pieces[k]
                if key[0] == "moe":
                    layer, per = key[1], 12
                    with sp.Fori(0, NG) as g:
                        for m in range(per):
                            _, _, kind, _, s = pieces[k + m]
                            sp.wait_ge(slots_released, g * per + (k + m - SLOTS + 1))
                            for j in range(GE):
                                dst = slot(k + m)[:, j * 1024:(j + 1) * 1024]
                                if kind < 2:
                                    dst = dst.rearrange("p (s n) -> p s n", s=2)
                                sp.dma_start(dst, moe_source(layer, kind, g, s, j)).then_inc(
                                    slot_loaded[(k + m) % SLOTS], 16)
                    k += per * NG
                    continue
                if k >= SLOTS:
                    sp.wait_ge(slots_released, k - SLOTS + 1)
                for (p0, p1), (o, n), src in source(key):
                    dst = slot(k)[p0:p1, o:o + n]
                    if len(src.shape) == 3:
                        dst = dst.rearrange("p (a b) -> p a b", a=src.shape[1])
                    sp.dma_start(dst, src).then_inc(slot_loaded[k % SLOTS], 16)
                k += 1
                if key == ("mla", 0) and pieces[k - 2] == ("in2", 0, 2) and pieces[k] == ("tab",) \
                        and ("mla", 0) not in pieces[:k - 1]:
                    sp.wait_ge(ada_cols, 48)
                    for l in range(2):
                        sp.dma_start(v3(wrt, l * P, DC, NE),
                                     A["w_router_2"][l].rearrange("(c p) n -> p c n", p=P))\
                            .then_inc(row_loads, 16)
                    load_rows(0)
                if key == ("mla", 1) and pieces[k - 2] == ("in2", 1, 2) and pieces[k - 3][0] == "moe":
                    sp.wait_ge(slots_released, k - 2)
                    load_rows(1)
            sp.wait_ge(out_copied, DC // 2)
            sp.dma_start(A["out"][0].rearrange("(t p) d -> p t d", p=P), tok_in[:, :, :]).then_inc(stored, 16)
            sp.wait_ge(stored, 16)

        N_LOADS = 16 * (1 + sum(len(n) for n in VEC_NAMES) + 4 + 2 + 1)
        LAYERS = 2

        def nsa_units():
            return [(qt, c, g) for qt in range(NT) for c in range(4) for g in range(2)]

        def dsa_units():
            return [(qt, cp, g) for qt in range(NT) for cp in range(4) for g in range(2)]

        def mla_units():
            return [(qt, h) for qt in range(NT) for h in range(MH)]

        @block.tensor
        def _(pe):
            n = {"dve": 0, "act": 0, "columns_read": 0, "piece": 0, "phase": 0, "ln": 0, "unit": 0, "ada": 0, "gu": 0,
                 "squares": 0, "h": 0, "turned": 0, "from_act": 0, "from_dve": 0}
            ada_log = []
            owed = []

            def mm(out, lhsT, rhs, start=True, stop=True, signal=None):
                ins = nc.tensor.matmul(out, lhsT, rhs, start=start, stop=stop, skip_group_check=True)
                if signal is not None:
                    ins.then_inc(signal, 1)
                elif owed:
                    owed.pop(0)
                    ins.then_inc(slots_released, 1)
                return ins

            def turn(out, in_, signal=None):
                k = in_.shape[0]
                ins = nc.tensor.transpose(out, in_, ident[0:k, 0:k])
                if signal is not None:
                    ins.then_inc(signal, 1)
                return ins

            def barrier():
                n["phase"] += 1
                pe.drain().then_inc(pe_phase, 1)
                pe.wait_ge(act_phase, n["phase"])
                pe.wait_ge(dve_phase, n["phase"])

            def from_dve():
                n["from_dve"] += 1
                pe.wait_ge(dve_made_for_pe, n["from_dve"])

            def from_act():
                n["from_act"] += 1
                pe.wait_ge(act_made_for_pe, n["from_act"])

            def bank_for_dve():
                k = n["dve"]
                n["dve"] += 1
                if k >= 2:
                    pe.wait_ge(dve_read, k - 1)
                return banks[k % 2]

            def bank_for_act():
                k = n["act"]
                n["act"] += 1
                if k >= 2:
                    pe.wait_ge(act_read, k - 1)
                if n["turned"] > n["columns_read"]:
                    pe.wait_ge(ada_read, n["turned"])
                    n["columns_read"] = n["turned"]
                return banks[2 + k % 2]

            def use(key):
                k = n["piece"]
                assert pieces[k] == key, (pieces[k], key)
                n["piece"] += 1
                pe.wait_ge(slot_loaded[k % SLOTS], landed[k])
                return slot(k)

            def release():
                owed.append(1)

            def settle():
                while owed:
                    owed.pop(0)
                    pe.drain().then_inc(slots_released, 1)

            def norm(sq, modulated=True):
                b = bank_for_dve()
                for c in range(DC):
                    n["squares"] += 1
                    pe.wait_ge(squares_ready, n["squares"])
                    mm(b[:, 0:T], ones[:, :], sq[:, c, :], start=(c == 0), stop=(c == DC - 1),
                       signal=pe_to_dve if c == DC - 1 else None)
                if modulated:
                    n["h"] += 1

            def wait_h(c):
                pe.wait_ge(h_ready, (n["h"] - 1) * DC + c + 1)

            def to_T(out, w, o, m, h=hT, signal=None):
                for c in range(DC):
                    mm(out, w[:, c, o:o + m], h[:, c, :], start=(c == 0), stop=(c == DC - 1),
                       signal=signal if c == DC - 1 else None)

            def to_tok(out, w, o, m, t, h=hT, signal=None):
                for c in range(DC):
                    mm(out, h[:, c, t * P:(t + 1) * P], w[:, c, o:o + m], start=(c == 0),
                       stop=(c == DC - 1), signal=signal if c == DC - 1 else None)

            def ada_columns():
                k = n["ada"] - 1
                matrix, s = ada_log[-1]
                lo, m = (0, 1) if matrix < 2 else (1, 2)
                pe.wait_ge(ada_copied, k + 1)
                if k >= 1:
                    pe.wait_ge(ada_read, k)
                for j in range(4):
                    mm(banks[3][:, j * m:(j + 1) * m], brow[:, (k % 2) * 512 + j * P:(k % 2) * 512 + (j + 1) * P],
                       selector[:, lo:lo + m], signal=ada_cols if j == 3 else None)

            def ada_pieces(keys, turn_last=True):
                for key in keys:
                    w = use(key).rearrange("p (c n) -> p c n", c=DC)
                    k = n["ada"]
                    if k >= 1:
                        pe.wait_ge(ada_copied, k)
                    for c in range(DC):
                        j = c % 4
                        mm(banks[2][32 * j:32 * j + 32, :], csil[:, c, :], w[:, c, :], start=(c < 4),
                           stop=(c >= 4), signal=ada_rows if c == DC - 1 else None)
                    release()
                    if n["ada"] > n["turned"]:
                        ada_columns()
                        n["turned"] += 1
                    n["ada"] += 1
                    ada_log.append(key[1:])
                if turn_last and n["ada"] > n["turned"]:
                    ada_columns()
                    n["turned"] += 1

            def accumulate(out_bank0, lhs, rhs, first, last):
                for c in range(DC):
                    b = banks[out_bank0 + c // 2]
                    mm(b[:, (c % 2) * T:(c % 2 + 1) * T], lhs[:, c * P:(c + 1) * P], rhs,
                       start=first and c % 2 == 0, stop=last,
                       signal=acc_ready if last and c == DC - 1 else None)

            def mixed():
                pe.wait_ge(dve_read, n["dve"])
                pe.wait_ge(exp_done, n["unit"])
                pe.wait_ge(turned_copied, n["unit"])

            def out_proj(keys, y):
                for half, key in enumerate(keys):
                    w = use(key).rearrange("p (c n) -> p c n", c=4)
                    for k in range(4):
                        accumulate(4, w[:, k, :], y[:, half * 4 + k, :], half == 0 and k == 0,
                                   half == 1 and k == 3)
                    release()

            def ffn(layer, extra):
                keys = ffn_pieces(layer, extra)
                steps = -(-F // 512)

                def down(f, wdp, k, rel):
                    pe.wait_ge(act_ready, f_base + f + 1)
                    accumulate(4, wdp[:, k, :], actT[:, f % 4, :], f == 0, f == FC - 1)
                    if rel:
                        release()
                f_base = n["gu"]
                at = 0
                for s in range(steps):
                    nf = min(4, FC - 4 * s)
                    wg = use(("wg", layer, s))[:, 0:DC * nf * P].rearrange("p (c n) -> p c n", c=DC)
                    wu = use(("wu", layer, s))[:, 0:DC * nf * P].rearrange("p (c n) -> p c n", c=DC)
                    for k in range(nf):
                        f = 4 * s + k
                        b = banks[(f_base + f) % 2]
                        if f >= 2:
                            pe.wait_ge(act_ready, f_base + f - 1)
                        elif f == 0:
                            pe.wait_ge(dve_read, n["dve"])
                        for c in range(DC):
                            if f == 0:
                                wait_h(c)
                            mm(b[:, 0:T], wg[:, c, k * P:(k + 1) * P], hT[:, c, :], start=(c == 0),
                               stop=(c == DC - 1))
                        for c in range(DC):
                            mm(b[:, T:2 * T], wu[:, c, k * P:(k + 1) * P], hT[:, c, :],
                               start=(c == 0), stop=(c == DC - 1),
                               signal=gu_ready if c == DC - 1 else None)
                        if k > 0:
                            if k == 1:
                                wd = use(("wd", layer, s))[:, 0:nf * D].rearrange("p (c n) -> p c n", c=nf)
                            down(f - 1, wd, k - 1, False)
                    release()
                    release()
                    down(4 * s + nf - 1, wd, nf - 1, True)
                    at += 3
                    mods_ = []
                    while at < len(keys) and keys[at][0] == "ada":
                        mods_.append(keys[at])
                        at += 1
                    ada_pieces(mods_, s == steps - 1)
                n["gu"] += FC
                settle()

            def attention(N, S, V, n_blocks, pt_, pr_, fill=()):
                u0 = n["unit"]
                for i in range(N + 2):
                    if i < N:
                        u = u0 + i
                        if u >= 2:
                            pe.wait_ge(exp_done, u - 1)
                        S(i, banks[4 + u % 2])
                    if 1 <= i <= N:
                        u = u0 + i - 1
                        pe.wait_ge(probs_ready, u + 1)
                        if u >= 2:
                            pe.wait_ge(turned_copied, u - 1)
                        nb = n_blocks(i - 1)
                        for b in range(nb):
                            turn(banks[6 + u % 2][:, b * P:(b + 1) * P],
                                 pr_[:, u % 2, b * P:(b + 1) * P], turned if b == nb - 1 else None)
                    if i >= 2:
                        u = u0 + i - 2
                        pe.wait_ge(turned_copied, u + 1)
                        V(i - 2, pt_[:, u % 2, :])
                    if fill and i % 2 == 1 and i // 2 < len(fill):
                        ada_pieces([fill[i // 2]], i // 2 == len(fill) - 1)
                n["unit"] += N

            pe.wait_ge(loads, N_LOADS)
            from_dve()
            b = bank_for_dve()
            for t in range(3):
                rows = sum(VEC_ROWS[m] for m in VEC_NAMES[t])
                turn(b[:, t * P:t * P + rows], vec_rows[0:rows, t, :])
            for i in range(2):
                turn(b[:, 384 + i * 32:416 + i * 32], pe_rows[:, i * P:(i + 1) * P],
                     pe_to_dve if i == 1 else None)
            for src in (tok_in, tok_in2):
                for c in range(DC):
                    b = bank_for_dve() if c % 2 == 0 else b
                    for t in range(NT):
                        turn(b[:, (c % 2) * T + t * P:(c % 2) * T + (t + 1) * P],
                             src[:, t, c * P:(c + 1) * P], pe_to_dve if c % 2 and t == 1 else None)
            from_act()
            ada_pieces(ADA_AT["start"])

            norm(hT)
            w = use(("in0", 1)).rearrange("p (c n) -> p c n", c=DC)
            for c in range(DC):
                wait_h(c)
            for m in range(LC):
                b = bank_for_dve()
                to_T(b[:, 0:T], w, m * P, P, signal=pe_to_dve)
            release()
            w = use(("in0", 0)).rearrange("p (c n) -> p c n", c=DC)
            for m in range(LC):
                b = bank_for_act()
                to_T(b[:, 0:T], w, m * P, P, signal=pe_to_act)
            release()
            w = use(("in0", 2)).rearrange("p (c n) -> p c n", c=DC)
            for m in range(4):
                b = bank_for_act()
                for g in range(2):
                    to_T(b[g * HD:(g + 1) * HD, 0:T], w, g * 256 + m * HD, HD,
                         signal=pe_to_act if g else None)
            release()
            w = use(("in0", 3)).rearrange("p (c n) -> p c n", c=DC)
            for m in range(2):
                b = bank_for_dve()
                to_T(b[:, 0:T], w, m * P, P, signal=pe_to_dve)
            b = bank_for_act()
            to_T(b[:, 0:T], w, 256, P, signal=pe_to_act)
            b = bank_for_act()
            for t in range(NT):
                to_tok(b[:, t * P:(t + 1) * P], w, 384, P, t, signal=pe_to_act if t else None)
            release()
            w = use(("in0", 4))[:, 0:DC * 280].rearrange("p (c n) -> p c n", c=DC)
            b = bank_for_act()
            to_T(b[:, 0:T], w, 0, P, signal=pe_to_act)
            b = bank_for_act()
            for t in range(NT):
                to_tok(b[:, t * P:(t + 1) * P], w, 128, P, t, signal=pe_to_act if t else None)
            b = bank_for_act()
            for t in range(NT):
                to_tok(b[:, t * 24:(t + 1) * 24], w, 256, 24, t, signal=pe_to_act if t else None)
            release()
            wl = use(("lru",))
            wax = wl[:, 0:512].rearrange("p (i a j) -> p i a j", i=2, a=LC)
            for m in range(LC):
                b = bank_for_act()
                from_dve()
                for i in range(2):
                    for h in range(2):
                        lo = h * HD
                        mm(b[lo:lo + HD, i * T:(i + 1) * T], wax[lo:lo + HD, i, m, :],
                           xc[lo:lo + HD, m, :], start=True, stop=True,
                           signal=pe_to_act if i and h else None)
            b = bank_for_act()
            b2 = bank_for_act()
            for kv in range(2):
                w = use(("cmp", kv)).rearrange("p (l n) -> p l n", l=CMP_LEN)
                from_dve()
                for l in range(CMP_LEN):
                    for g in range(2):
                        lo = g * HD
                        mm((b, b2)[g][:, kv * 16:kv * 16 + NBLK], w[lo:lo + HD, l, :],
                           ft[kv][lo:lo + HD, l // 16, l % 16, :], start=(l == 0),
                           stop=(l == CMP_LEN - 1),
                           signal=pe_to_act if kv and l == CMP_LEN - 1 else None)
            w2 = wl[:, 512:640].rearrange("p (i d) -> p i d", i=2)
            from_act()
            b = bank_for_dve()
            for g in range(2):
                mm(b[g * HD:(g + 1) * HD, 0:NBLK], w2[:, 0, :], h1[:, 0, g, 0:NBLK])
            for j in range(4):
                for g in range(2):
                    mm(b[32 * j:32 * j + NBLK, 64 + g * HD:64 + (g + 1) * HD],
                       h1[:, 1, g, 0:NBLK], w2[:, 1, :],
                       signal=pe_to_dve if j == 3 and g else None)
            for _ in range(3):
                release()
            from_dve()
            for t in range(NT):
                for g in range(2):
                    b = bank_for_dve()
                    mm(b[:, 0:P], ident, cmp_mask[:, t, 0:P], start=True, stop=False)
                    for c in range(4):
                        mm(b[:, c * 32:c * 32 + NBLK], q0[g * HD:(g + 1) * HD, c, t * P:(t + 1) * P],
                           kc[g * HD:(g + 1) * HD, 0:NBLK], start=False, stop=True,
                           signal=pe_to_dve if c == 3 else None)
            for t in range(NT):
                b = bank_for_dve()
                from_dve()
                for i in range(2):
                    turn(b[:, i * P:(i + 1) * P],
                         pc[:, t, 4 * i:4 * i + 4, :].rearrange("p a b -> p (a b)"),
                         pe_to_dve if i else None)
            from_dve()
            units = nsa_units()
            bank = [None]

            def S(i, b):
                qt, c, g = units[i]
                nk, lo = (qt + 1) * P, g * HD
                for s, kk in enumerate((ks0, kw0)):
                    mm(b[:, s * nk:(s + 1) * nk], q0[lo:lo + HD, c, qt * P:(qt + 1) * P],
                       kk[lo:lo + HD, 0:nk], start=(s == 0), stop=False)
                for s in range(2):
                    mm(b[:, (s + 1) * nk - P:(s + 1) * nk], ident, causal, start=False, stop=True,
                       signal=scores_ready if s else None)

            def V(i, ptu):
                qt, c, g = units[i]
                lo, nb = g * HD, qt + 1
                if g == 0:
                    bank[0] = bank_for_dve()
                o = bank[0][lo:lo + HD, 0:P]
                h = 4 * g + c
                mm(o, vc[32 * c:32 * c + NBLK, g, :],
                   pcT[32 * c:32 * c + NBLK, g, qt * P:(qt + 1) * P], start=True, stop=False)
                for s, vt in enumerate((vs0, vw0)):
                    for k in range(nb):
                        last = s == 1 and k == nb - 1
                        mm(o, vt[:, k, lo:lo + HD], ptu[:, (s * nb + k) * P:(s * nb + k + 1) * P],
                           start=False, stop=last, signal=pe_to_dve if last and g else None)

            ada_pieces(ADA_AT["lru"])
            attention(len(units), S, V, lambda i: 2 * (units[i][0] + 1), pt, pr, ADA_AT["attention0"])
            mixed()
            out_proj([("out", 0, 0), ("out", 0, 1)], yT)
            settle()
            norm(hT)
            ffn(0, ADA_AT["ffn0"])

            norm(hT)
            ada_pieces(ADA_AT["norm1"])
            for c in range(DC):
                wait_h(c)
            wq = [use(("in1", s)).rearrange("p (c n) -> p c n", c=DC) for s in range(2)]
            for m in range(8):
                b = bank_for_act() if m % 2 else bank_for_dve()
                for g in range(2):
                    to_T(b[g * HD:(g + 1) * HD, 0:T], wq[g], m * HD, HD,
                         signal=(pe_to_act if m % 2 else pe_to_dve) if g else None)
            release()
            release()
            w = use(("in1", 2)).rearrange("p (c n) -> p c n", c=DC)
            w3 = use(("in1", 3))[:, 0:DC * 328].rearrange("p (c n) -> p c n", c=DC)
            b = bank_for_act()
            to_T(b[:, 0:T], w, 0, P, signal=pe_to_act)
            b = bank_for_dve()
            for t in range(NT):
                to_tok(b[:, t * P:(t + 1) * P], w, 128, P, t, signal=pe_to_dve if t else None)
            for m in range(4):
                b = bank_for_act() if m % 2 else bank_for_dve()
                sg = pe_to_act if m % 2 else pe_to_dve
                if m < 2:
                    to_T(b[:, 0:T], w, 256 + m * P, P, signal=sg)
                else:
                    to_T(b[:, 0:T], w3, (m - 2) * P, P, signal=sg)
            b = bank_for_dve()
            for g in range(2):
                to_T(b[g * HD:(g + 1) * HD, 0:T], w3, 256, HD, signal=pe_to_dve if g else None)
            b = bank_for_dve()
            for t in range(NT):
                to_tok(b[:, t * 8:(t + 1) * 8], w3, 320, 8, t, signal=pe_to_dve if t else None)
            release()
            release()
            barrier()
            for t in range(NT):
                for g in range(2):
                    for mp in range(2):
                        b = bank_for_act()
                        for i in range(2):
                            mm(b[:, i * T:(i + 1) * T],
                               qi[g * HD:(g + 1) * HD, 2 * mp + i, t * P:(t + 1) * P],
                               ki[g * HD:(g + 1) * HD, :], signal=pe_to_act if i else None)
            units1 = dsa_units()
            def S1(i, b):
                qt, cp, g = units1[i]
                nk, lo = (qt + 1) * P, g * HD
                if cp == 0 and g == 0:
                    from_dve()
                for s in range(2):
                    mm(b[:, s * nk:(s + 1) * nk], q1[lo:lo + HD, 2 * cp + s, qt * P:(qt + 1) * P],
                       k1[lo:lo + HD, 0:nk], start=(s == 0), stop=False)
                for s in range(2):
                    mm(b[:, s * nk:(s + 1) * nk], ident, sel[:, qt, 0:nk], start=False, stop=True,
                       signal=scores_ready if s else None)

            def V1(i, ptu):
                qt, cp, g = units1[i]
                nb, lo = qt + 1, g * HD
                if g == 0:
                    bank[0] = bank_for_dve()
                b = bank[0]
                for s in range(2):
                    for k in range(nb):
                        last = k == nb - 1
                        mm(b[lo:lo + HD, s * P:(s + 1) * P], v1[:, k, lo:lo + HD],
                           ptu[:, (s * nb + k) * P:(s * nb + k + 1) * P], start=(k == 0), stop=last,
                           signal=pe_to_dve if last and s and g else None)

            attention(len(units1), S1, V1, lambda i: 2 * (units1[i][0] + 1), pt1, pr1, ADA_AT["attention1"])
            mixed()
            out_proj([("out", 1, 0), ("out", 1, 1)], yT)
            settle()
            norm(hT)
            ffn(1, ADA_AT["ffn1"])
            norm(hT, False)

            def mixers(layer, stream):
                full_ = stream == 1 or layer == 0
                norm(hT)
                for c in range(DC):
                    wait_h(c)
                if full_:
                    w = use(("in2", layer, 0)).rearrange("p (c n) -> p c n", c=DC)
                    for t in range(NT):
                        b = bank_for_act()
                        to_tok(b[:, :], w, 0, 512, t, signal=pe_to_act)
                    release()
                    w = use(("in2", layer, 1)).rearrange("p (c n) -> p c n", c=DC)
                    for t in range(NT):
                        b = bank_for_dve()
                        to_tok(b[:, :], w, 0, 512, t, signal=pe_to_dve)
                    release()
                w = use(("in2", layer, 2))[:, 0:DC * 192].rearrange("p (c n) -> p c n", c=DC)
                for t in range(NT):
                    b = bank_for_dve()
                    to_tok(b[:, 0:192], w, 0, 192, t, signal=pe_to_dve)
                release()
                wm = use(("mla", layer))
                wuq = wm[:, 0:1536].rearrange("p (c n) -> p c n", c=2)
                wukv = wm[:, 1536:2560]
                wsg = wm[:, 2560:3072].rearrange("p (h q) -> p h q", h=4)
                from_dve()
                for t in range(NT):
                    b = bank_for_dve()
                    if full_:
                        for c in range(2):
                            turn(b[:, c * P:(c + 1) * P], fq[:, t, 256 + c * P:256 + (c + 1) * P])
                    turn(b[:, 2 * P:3 * P], kvr[:, t, 0:P], pe_to_dve)
                    from_dve()
                    for half in range(2 if full_ else 0):
                        b = bank_for_dve()
                        for c in range(2):
                            mm(b[:, 0:384], cqT[:, c, :], wuq[:, c, half * 384:(half + 1) * 384],
                               start=(c == 0), stop=(c == 1), signal=pe_to_dve if c else None)
                    for half in range(2):
                        b = bank_for_dve()
                        mm(b[:, :], cqT[:, 2, :], wukv[:, half * 512:(half + 1) * 512],
                           signal=pe_to_dve)
                    from_dve()
                    for w_ in (0, 1) if full_ else (1,):
                        b = bank_for_dve()
                        for h in range(MH):
                            turn(b[:, h * P:(h + 1) * P], full[:, w_, h, 0:NOPE],
                                 pe_to_dve if h == MH - 1 else None)
                        b = bank_for_dve()
                        for h in range(MH):
                            turn(b[0:ROPE, h * P:(h + 1) * P], full[:, w_, h, NOPE:QKD],
                                 pe_to_dve if h == MH - 1 else None)
                if not full_:
                    release()
                    settle()
                    return
                b = bank_for_dve()
                for h in range(4):
                    turn(b[:, h * P:(h + 1) * P], wsg[:, h, :], pe_to_dve if h == 3 else None)
                from_dve()
                for t in range(NT):
                    b = bank_for_dve()
                    for h in range(4):
                        mm(b[:, h * HD:(h + 1) * HD], sq2[:, h * P:(h + 1) * P],
                           uv[:, t, 256 + h * HD:256 + (h + 1) * HD],
                           signal=pe_to_dve if h == 3 else None)
                for t in range(NT):
                    b = bank_for_dve()
                    from_dve()
                    for c in range(2):
                        turn(b[:, c * P:(c + 1) * P], uv[:, t, c * P:(c + 1) * P],
                             pe_to_dve if c else None)
                release()
                tb = use(("tab",))
                dftn = tb[:, C_DFTN:C_DFTN + 1024].rearrange("p (t s n) -> p t s n", t=NT, s=2)
                dftd = tb[:, C_DFTD:C_DFTD + 256].rearrange("p (s n) -> p s n", s=2)
                for c in range(2):
                    b = bank_for_dve()
                    for s in range(2):
                        for t in range(NT):
                            mm(b[:, s * T:(s + 1) * T], fq[:, t, c * P:(c + 1) * P], dftn[:, t, s, :],
                               start=(t == 0), stop=(t == 1), signal=pe_to_dve if s and t else None)
                from_dve()
                for c in range(2):
                    b = bank_for_dve()
                    for s in range(2):
                        mm(b[:, 0:T], dftd[:, s, :], acs[:, s, c, :], start=(s == 0), stop=(s == 1),
                           signal=pe_to_dve if s else None)
                release()
                k0, nk = (0, 2 * T) if stream else (0, T)
                units2 = mla_units()

                def S2(i, b):
                    qt, h = units2[i]
                    mm(b[:, 0:nk], qTn[:, h, qt * P:(qt + 1) * P], kTn[:, h, 0:nk], start=True, stop=False)
                    mm(b[:, 0:nk], qTr[0:ROPE, h, qt * P:(qt + 1) * P], kTr[0:ROPE, h, 0:nk],
                       start=False, stop=True, signal=scores_ready)

                def V2(i, ptu):
                    qt, h = units2[i]
                    b = bank_for_dve()
                    nb = nk // P
                    for k in range(nb):
                        mm(b[:, 0:P], vv[:, k, h * P:(h + 1) * P], ptu[:, k * P:(k + 1) * P],
                           start=(k == 0), stop=(k == nb - 1), signal=pe_to_dve if k == nb - 1 else None)

                pe.wait_ge(dve_read, n["dve"])
                attention(len(units2), S2, V2, lambda i: nk // P, pt2, pr2)
                mixed()
                out_proj([("out2", layer, 0), ("out2", layer, 1)], yT)
                settle()

            def route(layer, stream):
                norm(mhT)
                for c in range(DC):
                    wait_h(c)
                pe.wait_ge(row_loads, 32)
                wr = v3(wrt, layer * P, DC, NE)
                b = bank_for_dve()
                for t in range(NT):
                    to_tok(b[:, t * NE:(t + 1) * NE], wr, 0, NE, t, h=mhT, signal=pe_to_dve if t else None)
                for t in range(NT):
                    for half in range(2):
                        b = bank_for_act()
                        for c in range(4):
                            turn(b[:, c * P:(c + 1) * P], mxn[:, half * 4 + c, t * P:(t + 1) * P],
                                 pe_to_act if c == 3 else None)
                from_dve()
                b = bank_for_dve()
                for t in range(NT):
                    turn(b[0:NE, t * P:(t + 1) * P], small[:, 128 + t * NE:128 + (t + 1) * NE],
                         pe_to_dve if t else None)
                from_dve()
                b = bank_for_dve()
                for t in range(NT):
                    turn(b[:, t * NE:(t + 1) * NE], exs[2][:, t * P:(t + 1) * P],
                         pe_to_dve if t else None)
                from_dve()
                from_act()
                for c in range(DC):
                    b = bank_for_act() if c % 2 else bank_for_dve()
                    for t in range(NT):
                        mm(b[:, :], xtok[:, t, c * P:(c + 1) * P], pm[:, t, :], start=(t == 0),
                           stop=(t == 1), signal=(pe_to_act if c % 2 else pe_to_dve) if t else None)
                for half in range(2):
                    b = bank_for_dve()
                    for g in range(2):
                        for t in range(NT):
                            turn(b[:, g * T + t * P:g * T + (t + 1) * P],
                                 pg[:, t, (half * 2 + g) * P:(half * 2 + g + 1) * P],
                                 pe_to_dve if g and t else None)
                barrier()

            def experts(layer, streams):
                k0 = n["piece"]
                ns = len(streams)
                assert pieces[k0][0] == "moe"
                per = 12
                gain = [sum(16 * GE for m in range(per) if (k0 + m) % SLOTS == s) for s in range(SLOTS)]
                base = NG * layer
                base_s = 2 * NG * layer
                with pe.Fori(0, NG) as g:
                    def piece(m):
                        k = k0 + m
                        pe.wait_ge(slot_loaded[k % SLOTS], g * gain[k % SLOTS] + landed[k])
                        return slot(k)
                    pe.wait_ge(xs_ready, g + (base + 1))
                    for kind in range(2):
                        for s4 in range(4):
                            w = piece(kind * 4 + s4).rearrange("p (e s n) -> p e s n", e=GE, s=2)
                            for c2 in range(2):
                                c = 2 * s4 + c2
                                for i, s in enumerate(streams):
                                    b = banks[2 * s + kind]
                                    for j in range(GE):
                                        lastp = c2 == 1 and i == ns - 1 and j == GE - 1
                                        ins = nc.tensor.matmul(
                                            b[32 * j:32 * j + 32, :], xs[s][:, c, 32 * j:32 * j + 32],
                                            w[:, j, c2, :], start=(c == 0), stop=(c == DC - 1),
                                            skip_group_check=True)
                                        if lastp:
                                            ins.then_inc(slots_released, 1)
                    pe.drain().then_inc(gu_done, 1)
                    for i, s in enumerate(streams):
                        pe.wait_ge(hid_ready, g * ns + (base_s + i + 1))
                        for f in range(4):
                            ins = nc.tensor.transpose(banks[2 * s][:, f * P:(f + 1) * P],
                                                      hid[s][:, f * P:(f + 1) * P], ident)
                        ins.then_inc(hid_turned, 1)
                    pe.wait_ge(y_read, g + (base + 1))
                    for f in range(4):
                        w = piece(8 + f).rearrange("p (e n) -> p e n", e=GE)
                        for i, s in enumerate(streams):
                            if f == 0:
                                pe.wait_ge(hid_copied, g * ns + (base_s + i + 1))
                            for half in range(2):
                                for j in range(GE):
                                    lastp = half == 1 and i == ns - 1 and j == GE - 1
                                    ins = nc.tensor.matmul(
                                        banks[4 + 2 * s + half][32 * j:32 * j + 32, :],
                                        hidT[s][:, f, 32 * j:32 * j + 32],
                                        w[:, j, half * 512:(half + 1) * 512], start=(f == 0),
                                        stop=(f == 3), skip_group_check=True)
                                    if lastp:
                                        ins.then_inc(slots_released, 1)
                    pe.drain().then_inc(y_ready, 1)
                n["piece"] += per * NG
                barrier()
                for s in streams:
                    if s != streams[0]:
                        barrier()
                    for g in range(NG):
                        accumulate(4, ys[s][:, g, :], pgT[s][:, g, :], g == 0, g == NG - 1)
                barrier()

            for layer in range(LAYERS):
                mixers(layer, 0)
                mixers(layer, 1)
                for s in ((0, 1) if layer == 0 else (1,)):
                    route(layer, s)
                experts(layer, (0, 1) if layer == 0 else (1,))
            for c in range(DC):
                b = banks[c // 2]
                for t in range(NT):
                    turn(b[:, (c % 2) * T + t * P:(c % 2) * T + (t + 1) * P],
                         xT[:, c, t * P:(t + 1) * P], pe_to_dve if c % 2 and t else None)

        @block.scalar
        def _(act):
            n = {"act": 0, "phase": 0, "ln": 0, "chain": 0, "gu": 0, "unit": 0, "from_dve": 0,
                 "x": 0, "xn": 0, "ada": 0}

            def barrier():
                n["phase"] += 1
                act.drain().then_inc(act_phase, 1)
                act.wait_ge(pe_phase, n["phase"])
                act.wait_ge(dve_phase, n["phase"])

            def link(ins):
                n["chain"] += 1
                ins.then_inc(act_chain, 1)
                act.wait_ge(act_chain, n["chain"])

            def job():
                k = n["act"]
                n["act"] += 1
                act.wait_ge(pe_to_act, k + 1)
                return banks[2 + k % 2]

            def from_dve():
                n["from_dve"] += 1
                act.wait_ge(dve_made_for_act, n["from_dve"])

            def norm(src, dst, xn_, B, std_, sq, chunks=True, scale=None):
                k = n["ln"]
                n["ln"] += 1
                for c in range(DC):
                    if chunks:
                        n["x"] += 1
                        act.wait_ge(x_ready, n["x"])
                    nc.scalar.activation(sq[:, c, :], src[:, c, :], ACT.Square).then_inc(squares_ready, 1)
                act.wait_ge(var_ready, k + 1)
                nc.scalar.activation(std_, std_, ACT.Sqrt).then_inc(std_ready, 1)
                for c in range(DC if B else 0):
                    n["xn"] += 1
                    act.wait_ge(xn_ready, n["xn"])
                    nc.scalar.activation(dst[:, c, :], xn_[:, c, :], ACT.Identity, bias=B(c),
                                         scale=scale(c) if scale else 1.0).then_inc(h_ready, 1)

            def ada_pieces(count):
                for _ in range(count):
                    k = n["ada"]
                    n["ada"] += 1
                    act.wait_ge(ada_rows, k + 1)
                    if k >= 2:
                        act.wait_ge(ada_cols, k - 1)
                    nc.scalar.copy(brow[:, (k % 2) * 512:(k % 2 + 1) * 512], banks[2][:, :])\
                        .then_inc(ada_copied, 1)

            def ffn(extra):
                at = ada_after(extra)
                for f in range(FC):
                    k = n["gu"]
                    n["gu"] += 1
                    act.wait_ge(gu_ready, k + 1)
                    if f >= 2:
                        act.wait_ge(act_ready, k - 1)
                    nc.scalar.activation(sil[:, k % 2, :], banks[k % 2][:, 0:T], ACT.Silu)\
                        .then_inc(silu_ready, 1)
                    ada_pieces(at.get(f, 0))

            def attention(N, segs, pr_, pt_, scale, nb_of, sums, negs, fill=0):
                u0 = n["unit"]
                for i in range(N + 1):
                    if i < N:
                        u = u0 + i
                        nb = nb_of(i)
                        nk = nb * P // segs
                        act.wait_ge(negmax_ready, u + 1)
                        for s in range(segs):
                            ins = nc.scalar.activation(
                                pr_[:, u % 2, s * nk:(s + 1) * nk], banks[4 + u % 2][:, s * nk:(s + 1) * nk],
                                ACT.Exp, bias=negs[:, (u % 2) * 2 + s:(u % 2) * 2 + s + 1], scale=scale,
                                accum_out=sums[:, (u % 2) * 2 + s:(u % 2) * 2 + s + 1])
                        ins.then_inc(exp_done, 1)
                    if i >= 1:
                        u = u0 + i - 1
                        nb = nb_of(i - 1)
                        act.wait_ge(turned, u + 1)
                        nc.scalar.copy(pt_[:, u % 2, 0:nb * P], banks[6 + u % 2][:, 0:nb * P])\
                            .then_inc(turned_copied, 1)
                    if i % 2 == 1 and i // 2 < fill:
                        ada_pieces(1)
                n["unit"] += N

            negs, sums = small[:, 84:88], small[:, 88:92]

            from_dve()
            for i, name in enumerate(("c", "c_2", "c_ctx_2")):
                ins = nc.scalar.activation(csil[:, :, i], vec(name, 0, 8), ACT.Silu)
            ins.then_inc(act_made_for_pe, 1)
            link(nc.scalar.activation(lam[:, 0:4], vec("l0_lru_lambda", 0, 4), ACT.Abs))
            link(nc.scalar.activation(lam[:, 4:8], lam[:, 0:4], ACT.Exp, scale=-1.0))
            nc.scalar.activation(lam[:, 8:12], lam[:, 4:8], ACT.Ln, bias=1.0).then_inc(act_made_for_dve, 1)
            ada_pieces(len(ADA_AT["start"]))

            from_dve()
            norm(xT, hT, xn, lambda c: mod(0, 0, c), std, hT, False)
            for m in range(LC):
                b = job()
                nc.scalar.activation(gg[:, m, :], b[:, 0:T], ACT.Gelu_apprx_tanh).then_inc(act_read, 1)
            for m in range(4):
                b = job()
                nc.scalar.copy(q0[:, m, :], b[:, 0:T]).then_inc(act_read, 1)
            b = job()
            nc.scalar.copy(ks0, b[:, 0:T]).then_inc(act_read, 1)
            b = job()
            nc.scalar.copy(vs0, b[:, 0:T].rearrange("p (a b) -> p a b", a=2)).then_inc(act_read, 1)
            b = job()
            nc.scalar.copy(kw0, b[:, 0:T]).then_inc(act_read, 1)
            b = job()
            nc.scalar.copy(vw0, b[:, 0:T].rearrange("p (a b) -> p a b", a=2)).then_inc(act_read, 1)
            b = job()
            nc.scalar.activation(gts.rearrange("p t h k -> p (t h k)"), b[:, 0:48], ACT.Sigmoid)\
                .then_inc(act_read, 1)
            for m in range(LC):
                b = job()
                nc.scalar.activation(rr[:, m, :], b[:, 0:T], ACT.Sigmoid, bias=vec("l0_lru_ba", m))
                nc.scalar.activation(ii[:, m, :], b[:, T:2 * T], ACT.Sigmoid, bias=vec("l0_lru_bx", m))\
                    .then_inc(act_read, 1)
            act.wait_ge(act_read, n["act"])
            for m in range(LC):
                nc.scalar.activation(aa[:, m, :], rr[:, m, :], ACT.Exp, scale=lam[:, 12 + m:13 + m])
                ins = nc.scalar.activation(th[:, m, :], rr[:, m, :], ACT.Tanh, scale=lam[:, 16 + m:17 + m])
            ins.then_inc(act_made_for_dve, 1)
            g1 = job()
            g2 = job()
            for g, b in enumerate((g1, g2)):
                for kv in range(2):
                    ins = nc.scalar.activation(h1[:, kv, g, 0:NBLK], b[:, kv * 16:kv * 16 + NBLK],
                                               ACT.Gelu_apprx_tanh)
                    if kv:
                        ins.then_inc(act_read, 1)
            act.drain().then_inc(act_made_for_pe, 1)
            from_dve()
            nc.scalar.activation(th, th, ACT.Sqrt).then_inc(act_made_for_dve, 1)
            for t in range(NT):
                from_dve()
                nc.scalar.activation(pc[:, t], pc[:, t], ACT.Exp, scale=HD ** -0.5).then_inc(act_made_for_dve, 1)
            units = nsa_units()
            ada_pieces(len(ADA_AT["lru"]))
            attention(len(units), 2, pr, pt, HD ** -0.5, lambda i: 2 * (units[i][0] + 1), sums, negs,
                      len(ADA_AT["attention0"]))
            norm(xT, hT, xn, lambda c: mod(0, 3, c), std, hT)
            ffn(ADA_AT["ffn0"])

            norm(xT, hT, xn, lambda c: mod(1, 0, c), std, hT)
            ada_pieces(len(ADA_AT["norm1"]))
            for m in range(1, 8, 2):
                b = job()
                nc.scalar.copy(q1[:, m, :], b[:, 0:T]).then_inc(act_read, 1)
            b = job()
            nc.scalar.copy(k1, b[:, 0:T]).then_inc(act_read, 1)
            for m in (1, 3):
                b = job()
                nc.scalar.copy(qi[:, m, :], b[:, 0:T]).then_inc(act_read, 1)
            barrier()
            for t in range(NT):
                for m in range(4):
                    b = job()
                    k = t * 4 + m
                    if k >= 2:
                        act.wait_ge(index_added, 2 * (k - 1))
                    nc.scalar.activation(rel[:, k % 2, :], b[:, :], ACT.Relu, scale=HD ** -0.5)\
                        .then_inc(act_read, 1)
                    act.drain().then_inc(act_made_for_dve, 1)
            units1 = dsa_units()
            attention(len(units1), 2, pr1, pt1, HD ** -0.5, lambda i: 2 * (units1[i][0] + 1), sums, negs,
                      len(ADA_AT["attention1"]))
            norm(xT, hT, xn, lambda c: mod(1, 3, c), std, hT)
            ffn(ADA_AT["ffn1"])
            norm(xT, xT, xn, None, std, hT)

            def mixers(layer, stream):
                full_ = stream == 1 or layer == 0
                src = xT if stream else cT
                cond = 0 if stream else 1
                from_dve()
                norm(src, hT, xn, lambda c: mod(2 + layer, 0, c, 1, cond), std, hT, False)
                if full_:
                    for t in range(NT):
                        b = job()
                        nc.scalar.activation(uv[:, t, :], b[:, :], ACT.Gelu_apprx_tanh).then_inc(act_read, 1)
                    act.drain().then_inc(act_made_for_dve, 1)
                from_dve()
                nc.scalar.activation(small[:, 112:118], small[:, 112:118], ACT.Sqrt)\
                    .then_inc(act_made_for_dve, 1)
                for t in range(NT):
                    from_dve()
                    nc.scalar.activation(small[:, 120:128], small[:, 120:128], ACT.Sqrt)\
                        .then_inc(act_made_for_dve, 1)
                if full_:
                    units2 = mla_units()
                    nk = 2 * T if stream else T
                    attention(len(units2), 1, pr2, pt2, QKD ** -0.5, lambda i: nk // P, sums, negs)

            def route(layer, stream):
                src = xT if stream else cT
                cond = 0 if stream else 1
                from_dve()
                norm(src, mhT, mxn, lambda c: mod(2 + layer, 3, c, 1, cond), mstd, mhT, False,
                     lambda c: ac(8, c))
                for t in range(NT):
                    for half in range(2):
                        b = job()
                        nc.scalar.copy(xtok[:, t, half * 512:(half + 1) * 512], b[:, :]).then_inc(act_read, 1)
                act.drain().then_inc(act_made_for_pe, 1)
                from_dve()
                nc.scalar.activation(small[:, 128:128 + NT * NE], small[:, 128:128 + NT * NE], ACT.Exp)\
                    .then_inc(act_made_for_dve, 1)
                for c in range(1, DC, 2):
                    b = job()
                    nc.scalar.activation(xsT[stream][:, c, :], b[:, :], ACT.Identity, scale=ac(8, c),
                                         bias=mod(2 + layer, 3, c, 1, cond)).then_inc(act_read, 1)
                barrier()

            def experts(layer, streams):
                ns = len(streams)
                base = NG * layer
                base_s = 2 * NG * layer
                with act.Fori(0, NG) as g:
                    for i, s in enumerate(streams):
                        ins = nc.scalar.copy(xs[s], xsT[s][:, :, bass.ts(g, P)])
                    ins.then_inc(xs_ready, 1)
                    act.wait_ge(gu_done, g + (base + 1))
                    for i, s in enumerate(streams):
                        ins = nc.scalar.activation(hid[s], banks[2 * s][:, :], ACT.Silu)
                        ins.then_inc(hid_silu, 1)
                    for i, s in enumerate(streams):
                        act.wait_ge(hid_turned, g * ns + (base_s + i + 1))
                        nc.scalar.copy(hidT[s], banks[2 * s][:, :].rearrange("p (a b) -> p a b", a=4))\
                            .then_inc(hid_copied, 1)
                barrier()
                for s in streams[1:]:
                    barrier()
                barrier()

            for layer in range(LAYERS):
                mixers(layer, 0)
                mixers(layer, 1)
                for s in ((0, 1) if layer == 0 else (1,)):
                    route(layer, s)
                experts(layer, (0, 1) if layer == 0 else (1,))

        @block.vector
        def _(dve):
            n = {"dve": 0, "phase": 0, "ln": 0, "chain": 0, "gu": 0, "unit": 0, "from_act": 0, "acc": 0,
                 "ada": 0, "index": 0}

            def barrier():
                n["phase"] += 1
                dve.drain().then_inc(dve_phase, 1)
                dve.wait_ge(pe_phase, n["phase"])
                dve.wait_ge(act_phase, n["phase"])

            def link(ins):
                n["chain"] += 1
                ins.then_inc(dve_chain, 1)
                dve.wait_ge(dve_chain, n["chain"])

            def job():
                k = n["dve"]
                n["dve"] += 1
                dve.wait_ge(pe_to_dve, k + 1)
                return banks[k % 2]

            def from_act():
                n["from_act"] += 1
                dve.wait_ge(act_made_for_dve, n["from_act"])

            tt, ts_, stt = nc.vector.tensor_tensor, nc.vector.tensor_scalar, nc.vector.scalar_tensor_tensor

            def bc(ap, axis, shape):
                return ap.unsqueeze(axis).to_broadcast(shape)

            def norm(src, dst, xn_, std_, A_=None):
                k = n["ln"]
                n["ln"] += 1
                b = job()
                ts_(std_, b[:, 0:T], 1.0 / D, EPS, ALU.mult, ALU.add).then_inc(var_ready, 1)
                dve.wait_ge(std_ready, k + 1)
                nc.vector.reciprocal(std_, std_).then_inc(dve_read, 1)
                dve.wait_ge(dve_read, n["dve"])
                for c in range(DC):
                    if A_ is None:
                        ins = tt(xn_[:, c, :], src[:, c, :], std_, ALU.mult)
                    else:
                        ins = stt(xn_[:, c, :], src[:, c, :], A_(c), std_, ALU.mult, ALU.mult)
                    if dst is not None:
                        ins.then_inc(xn_ready, 1)

            def residual(dst, gate, normed=True):
                n["acc"] += 1
                dve.wait_ge(acc_ready, n["acc"])
                for c in range(DC):
                    ins = stt(dst[:, c, :], banks[4 + c // 2][:, (c % 2) * T:(c % 2 + 1) * T], gate(c),
                              dst[:, c, :], ALU.mult, ALU.add)
                    if normed:
                        ins.then_inc(x_ready, 1)

            def ada_pieces(keys):
                for _, matrix, s in keys:
                    n["ada"] += 1
                    dve.wait_ge(ada_cols, n["ada"])
                    if matrix < 2:
                        src, dst = banks[3][:, 0:4], mods[:, MODO[matrix] + 4 * s:MODO[matrix] + 4 * s + 4]
                        bias = vec(f"l{matrix}_mod_b", 4 * s, 4)
                    else:
                        src = banks[3][:, 0:8].rearrange("p (a b) -> p a b", b=2)
                        o = MODO[matrix] + 8 * s
                        dst = mods[:, o:o + 8].rearrange("p (a b) -> p a b", b=2)
                        bias = bc(vec("b_ada_2", (matrix - 2) * 48 + 4 * s, 4), 2, [P, 4, 2])
                    tt(dst, src, bias, ALU.add).then_inc(ada_read, 1)
                dve.wait_ge(ada_read, n["ada"])

            def scale_cols(i, matrix, seg, cond=0, gain=None):
                s = mod(matrix, seg, 0, 8, cond)
                if gain is None:
                    return ts_(ac(i, 0, 8), s, 1.0, None, ALU.add)
                return stt(ac(i, 0, 8), s, 1.0, vec(gain, 0, 8), ALU.add, ALU.mult)

            def ffn(extra):
                at, done = ada_after(extra), 0
                for f in range(FC):
                    k = n["gu"]
                    n["gu"] += 1
                    dve.wait_ge(silu_ready, k + 1)
                    tt(actT[:, f % 4, :], sil[:, k % 2, :], banks[k % 2][:, T:2 * T], ALU.mult)\
                        .then_inc(act_ready, 1)
                    if f in at:
                        upto = done + at[f]
                        end = upto if f == FC - 1 else upto - 1
                        ada_pieces(extra[n_ada[0]:end])
                        n_ada[0] = end
                        done = upto
                n_ada[0] = 0

            n_ada = [0]

            def attention(N, segs, pr_, scale, nb_of, sums, negs, gate, V, every, fill=()):
                u0 = n["unit"]
                rs = small[:, 94:98]
                for i in range(N + 2):
                    if i < N:
                        u = u0 + i
                        nk = nb_of(i) * P // segs
                        dve.wait_ge(scores_ready, u + 1)
                        ng = negs[:, (u % 2) * 2:(u % 2) * 2 + segs]
                        link(nc.vector.tensor_reduce(
                            ng, banks[4 + u % 2][:, 0:segs * nk].rearrange("p (s k) -> p s k", s=segs),
                            X, ALU.max))
                        ts_(ng, ng, FLOOR, -scale, ALU.max, ALU.mult).then_inc(negmax_ready, 1)
                    if 1 <= i <= N:
                        u = u0 + i - 1
                        nk = nb_of(i - 1) * P // segs
                        dve.wait_ge(exp_done, u + 1)
                        sm = sums[:, (u % 2) * 2:(u % 2) * 2 + segs]
                        r = rs[:, (u % 2) * 2:(u % 2) * 2 + segs]
                        link(ts_(r, sm, 1e-30, None, ALU.max))
                        link(nc.vector.reciprocal(r, r))
                        if gate is not None:
                            link(tt(r, r, gate(i - 1), ALU.mult))
                        for s in range(segs):
                            p_ = pr_[:, u % 2, s * nk:(s + 1) * nk]
                            ins = ts_(p_, p_, r[:, s:s + 1], None, ALU.mult)
                        ins.then_inc(probs_ready, 1)
                    if i >= 2 and (i - 2) % every == every - 1:
                        b = job()
                        V(i - 2, b)
                    if fill and i % 2 == 1 and 1 <= i // 2 < len(fill):
                        ada_pieces([fill[i // 2 - 1]])
                        if i // 2 == len(fill) - 1:
                            ada_pieces([fill[-1]])
                n["unit"] += N

            negs, sums = small[:, 84:88], small[:, 88:92]

            nc.vector.memset(csil_[:, :], 0.0)
            nc.vector.memset(ones[:, :], 1.0).then_inc(dve_made_for_pe, 1)
            dve.wait_ge(loads, N_LOADS)
            nc.vector.tensor_reduce(selector[:, 0:3], ident.rearrange("p (j i) -> p i j", j=4)[:, 0:3, :],
                                    X, ALU.add)
            b = job()
            for t in range(3):
                rows = sum(VEC_ROWS[m] for m in VEC_NAMES[t])
                nc.vector.tensor_copy(vecs[:, t * P:t * P + rows], b[:, t * P:t * P + rows])
            nc.vector.tensor_copy(peT, b[:, 384:448]).then_inc(dve_read, 1)
            dve.drain().then_inc(dve_made_for_act, 1)
            for dst in (xT, cT):
                for c in range(0, DC, 2):
                    b = job()
                    nc.vector.tensor_copy(dst[:, c:c + 2, :], b[:, :].rearrange("p (a b) -> p a b", a=2))\
                        .then_inc(dve_read, 1)
            from_act()
            link(ts_(lam[:, 12:16], vec("l0_lru_lambda", 0, 4), -1.0, 0.0, ALU.mult, ALU.max))
            e_, l_, s_ = lam[:, 4:8], lam[:, 8:12], lam[:, 12:16]
            w1, w2, w3 = small[:, 100:104], small[:, 104:108], small[:, 108:112]
            link(ts_(w1, e_, 1.0, None, ALU.add))
            link(ts_(w1, w1, 1.0, None, ALU.subtract))
            link(ts_(w2, w1, 0.0, None, ALU.is_equal))
            link(tt(w1, w1, w2, ALU.add))
            link(nc.vector.reciprocal(w1, w1))
            link(tt(w1, w1, e_, ALU.mult))
            link(tt(w1, w1, l_, ALU.mult))
            link(tt(w3, w2, e_, ALU.mult))
            link(tt(w1, w1, w3, ALU.add))
            link(tt(s_, s_, w1, ALU.add))
            link(ts_(lam[:, 16:20], s_, 8.0, None, ALU.mult))
            link(ts_(s_, s_, -8.0, None, ALU.mult))
            ada_pieces(ADA_AT["start"])
            link(scale_cols(0, 0, 1, gain="l0_norm_mix"))
            dve.drain().then_inc(dve_made_for_act, 1)

            norm(xT, hT, xn, std, lambda c: ac(0, c))
            link(nc.vector.memset(axp[:, :, 0:3], 0.0))
            for m in range(LC):
                b = job()
                nc.vector.tensor_copy(axp[:, m, 3:], b[:, 0:T]).then_inc(dve_read, 1)
                dve.wait_ge(dve_read, n["dve"])
                link(ts_(xc[:, m, :], axp[:, m, 0:T], vec("l0_conv_w", m), vec("l0_conv_b", m),
                         ALU.mult, ALU.add))
                for k in range(1, 4):
                    ins = stt(xc[:, m, :], axp[:, m, k:k + T], vec("l0_conv_w", 4 * k + m), xc[:, m, :],
                              ALU.mult, ALU.add)
                    if k < 3:
                        link(ins)
                ins.then_inc(dve_made_for_pe, 1)
            for kv in range(2):
                b = job()
                src = b[:, 0:T].rearrange("p (b l) -> p l b", l=CMP_STRIDE)
                for hf in range(2):
                    pos = peT[:, kv * 32 + hf * 16:kv * 32 + hf * 16 + 16]
                    ins = tt(ft[kv][:, hf], src[:, :, hf:hf + NBLK], bc(pos, 2, [P, CMP_STRIDE, NBLK]),
                             ALU.add)
                ins.then_inc(dve_read, 1)
                dve.drain().then_inc(dve_made_for_pe, 1)
            from_act()
            link(tt(rr, aa, aa, ALU.mult))
            stt(th, rr, 1.0, th, ALU.add, ALU.mult).then_inc(dve_made_for_act, 1)
            b = job()
            nc.vector.tensor_copy(kc[:, 0:NBLK], b[:, 0:NBLK])
            for j in range(4):
                ins = nc.vector.tensor_copy(vc[32 * j:32 * j + NBLK],
                                            b[32 * j:32 * j + NBLK, 64:192].rearrange("p (g d) -> p g d", g=2))
            ins.then_inc(dve_read, 1)
            dve.drain().then_inc(dve_made_for_pe, 1)
            from_act()
            nc.vector.memset(th[:, :, 0:1], 1.0)
            link(tt(ii, ii, xc, ALU.mult))
            dve.drain().then_inc(dve_chain, 1)
            n["chain"] += 1
            dve.wait_ge(dve_chain, n["chain"])
            link(tt(ii, ii, th, ALU.mult))
            for m in range(LC):
                ins = nc.vector.tensor_tensor_scan(xc[:, m, :], aa[:, m, :], ii[:, m, :], 0.0,
                                                   ALU.mult, ALU.add)
                link(ins)
            link(tt(yT[:, 0:4, :], xc, gg, ALU.mult))
            mx, sm8 = small[:, 100:108], small[:, 108:116]
            for t in range(NT):
                for g in range(2):
                    b = job()
                    s3 = b[:, 0:P].rearrange("p (h k) -> p h k", h=4)
                    mg = mx[:, 4 * g:4 * g + 4]
                    link(nc.vector.tensor_reduce(mg, s3, X, ALU.max))
                    link(ts_(mg, mg, FLOOR, None, ALU.max))
                    tt(pc[:, t, 4 * g:4 * g + 4, :], s3, bc(mg, 2, [P, 4, 32]), ALU.subtract)\
                        .then_inc(dve_read, 1)
                dve.drain().then_inc(dve_made_for_act, 1)
                from_act()
                link(nc.vector.tensor_reduce(sm8, pc[:, t], X, ALU.add))
                link(ts_(sm8, sm8, 1e-30, None, ALU.max))
                link(nc.vector.reciprocal(sm8, sm8))
                link(tt(sm8, sm8, gts[:, t, :, 0], ALU.mult))
                tt(pc[:, t], pc[:, t], bc(sm8, 2, [P, 8, 32]), ALU.mult).then_inc(dve_made_for_pe, 1)
            for t in range(NT):
                b = job()
                nc.vector.tensor_copy(pcT[:, :, t * P:(t + 1) * P],
                                      b[:, 0:256].rearrange("p (a b) -> p a b", a=2)).then_inc(dve_read, 1)
            dve.drain().then_inc(dve_made_for_pe, 1)
            units = nsa_units()

            def V0(i, b):
                qt, c, g = units[i]
                nc.vector.tensor_copy(yT[:, 4 + c, qt * P:(qt + 1) * P], b[:, 0:P]).then_inc(dve_read, 1)

            def gate0(i):
                qt, c, g = units[i]
                return gts[:, qt, 4 * g + c, 1:3]

            ada_pieces(ADA_AT["lru"])
            attention(len(units), 2, pr, HD ** -0.5, lambda i: 2 * (units[i][0] + 1), sums, negs, gate0,
                      V0, 2, ADA_AT["attention0"])
            link(scale_cols(1, 0, 4, gain="l0_norm_ffn"))
            residual(xT, lambda c: mod(0, 2, c))
            norm(xT, hT, xn, std, lambda c: ac(1, c))
            ffn(ADA_AT["ffn0"])
            link(scale_cols(2, 1, 1, gain="l1_norm_mix"))
            link(scale_cols(3, 1, 4, gain="l1_norm_ffn"))
            residual(xT, lambda c: mod(0, 5, c))

            norm(xT, hT, xn, std, lambda c: ac(2, c))
            ada_pieces(ADA_AT["norm1"])
            for m in range(0, 8, 2):
                b = job()
                nc.vector.tensor_copy(q1[:, m, :], b[:, 0:T]).then_inc(dve_read, 1)
            b = job()
            nc.vector.tensor_copy(v1, b[:, 0:T].rearrange("p (a b) -> p a b", a=2)).then_inc(dve_read, 1)
            for m in (0, 2):
                b = job()
                nc.vector.tensor_copy(qi[:, m, :], b[:, 0:T]).then_inc(dve_read, 1)
            b = job()
            nc.vector.tensor_copy(ki, b[:, 0:T]).then_inc(dve_read, 1)
            b = job()
            ts_(wi.rearrange("p t h -> p (t h)"), b[:, 0:16], IDX_HEADS ** -0.5, None, ALU.mult)\
                .then_inc(dve_read, 1)
            barrier()
            for t in range(NT):
                for m in range(4):
                    k = t * 4 + m
                    from_act()
                    for i in range(2):
                        g, mp = m // 2, m % 2
                        h = 4 * mp + 2 * i + g
                        r = rel[:, k % 2, i * T:(i + 1) * T]
                        if h == 0:
                            ins = ts_(idx[:, t, :], r, wi[:, t, h:h + 1], None, ALU.mult)
                        else:
                            ins = stt(idx[:, t, :], r, wi[:, t, h:h + 1], idx[:, t, :], ALU.mult, ALU.add)
                        n["index"] += 1
                        ins.then_inc(index_added, 1)
                        dve.wait_ge(index_added, n["index"])
                nk = (t + 1) * P
                link(tt(idx[:, t, nk - P:nk], idx[:, t, nk - P:nk], causal, ALU.add))
                m8 = small[:, 100:108]
                src = idx[:, t, 0:nk]
                wk = work[:, t, 0:nk]
                for r in range(TOPK // 8):
                    link(nc.vector.max(m8, src))
                    link(nc.vector.match_replace(wk, m8, src, TAKEN))
                    src = wk
                link(ts_(sel[:, t, 0:nk], wk, TAKEN / 2, NEG, ALU.is_gt, ALU.mult))
                tt(sel[:, t, nk - P:nk], sel[:, t, nk - P:nk], causal, ALU.add).then_inc(dve_made_for_pe, 1)
            units1 = dsa_units()

            def V1(i, b):
                qt, cp, g = units1[i]
                nc.vector.tensor_copy(yT[:, 2 * cp:2 * cp + 2, qt * P:(qt + 1) * P],
                                      b[:, 0:2 * P].rearrange("p (s t) -> p s t", s=2)).then_inc(dve_read, 1)

            attention(len(units1), 2, pr1, HD ** -0.5, lambda i: 2 * (units1[i][0] + 1), sums, negs, None,
                      V1, 2, ADA_AT["attention1"])
            residual(xT, lambda c: mod(1, 2, c))
            norm(xT, hT, xn, std, lambda c: ac(3, c))
            ffn(ADA_AT["ffn1"])
            residual(xT, lambda c: mod(1, 5, c))
            norm(xT, None, xT, std, lambda c: vec("final_norm", c))

            def row(name):
                o, m = ROWS[name]
                return brow[:, o:o + m]

            def mixers(layer, stream):
                full_ = stream == 1 or layer == 0
                src = xT if stream else cT
                cond = 0 if stream else 1
                link(scale_cols(4, 2 + layer, 1, cond))
                dve.drain().then_inc(dve_made_for_act, 1)
                norm(src, hT, xn, std, lambda c: ac(4, c))
                for t in range(NT if full_ else 0):
                    b = job()
                    nc.vector.tensor_copy(fq[:, t, :], b[:, :]).then_inc(dve_read, 1)
                for t in range(NT):
                    b = job()
                    nc.vector.tensor_copy(kvr[:, t, :], b[:, 0:192]).then_inc(dve_read, 1)
                if full_:
                    from_act()
                ms = small[:, 112:118]
                dve.wait_ge(dve_read, n["dve"])
                if not full_:
                    nc.vector.memset(ms, 1.0)
                    dve.drain().then_inc(dve_chain, 1)
                    n["chain"] += 1
                    dve.wait_ge(dve_chain, n["chain"])
                latents = [(4, lambda t: kvr[:, t, 0:P])]
                if full_:
                    latents += [(0, lambda t: uv[:, t, 256:512]), (2, lambda t: fq[:, t, 256:512])]
                for o, view in latents:
                    for t in range(NT):
                        v = view(t)
                        link(nc.vector.tensor_tensor_reduce(
                            sq2[:, 0:v.shape[1]], v, v, 1.0, 0.0, ALU.mult, ALU.add, ms[:, o + t:o + t + 1]))
                link(ts_(ms[:, 0:4], ms[:, 0:4], 1.0 / 256, EPS, ALU.mult, ALU.add))
                ts_(ms[:, 4:6], ms[:, 4:6], 1.0 / 128, EPS, ALU.mult, ALU.add).then_inc(dve_made_for_act, 1)
                from_act()
                link(nc.vector.reciprocal(ms, ms))
                names = {4: "kv_lora_norm_2", 0: "sgu_norm_2", 2: "q_lora_norm_2"}
                dve.wait_ge(row_loads, 16 * (2 + len(ROWS) * (layer + 1)))
                for o, view in latents:
                    for t in range(NT):
                        v = view(t)
                        ins = stt(v, v, ms[:, o + t:o + t + 1], row(names[o]), ALU.mult, ALU.mult)
                ins.then_inc(dve_made_for_pe, 1)
                hs = small[:, 120:128]
                kept = slice(0, 2) if full_ else slice(1, 2)
                for t in range(NT):
                    b = job()
                    lo = 0 if full_ else 2
                    nc.vector.tensor_copy(cqT[:, lo:3, :], b[:, lo * P:3 * P].rearrange(
                        "p (a b) -> p a b", b=P)).then_inc(dve_read, 1)
                    dve.drain().then_inc(dve_made_for_pe, 1)
                    for half in range(2 if full_ else 0):
                        b = job()
                        nc.vector.tensor_copy(full[:, 0, 2 * half:2 * half + 2, :],
                                              b[:, 0:384].rearrange("p (a b) -> p a b", a=2)).then_inc(dve_read, 1)
                    kt = 2 * stream + t
                    for half in range(2):
                        b = job()
                        kvb = b[:, :].rearrange("p (h w d) -> p h w d", h=2, w=2)
                        nc.vector.tensor_copy(full[:, 1, 2 * half:2 * half + 2, 0:NOPE], kvb[:, :, 0, :])
                        nc.vector.tensor_copy(vv[:, kt, half * 256:(half + 1) * 256].rearrange(
                            "p (h d) -> p h d", h=2), kvb[:, :, 1, :]).then_inc(dve_read, 1)
                    link(nc.vector.tensor_copy(full[:, 1, :, NOPE:QKD],
                                               bc(kvr[:, t, P:P + ROPE], 1, [P, MH, ROPE])))
                    dve.drain().then_inc(dve_chain, 1)
                    n["chain"] += 1
                    dve.wait_ge(dve_chain, n["chain"])
                    if not full_:
                        link(nc.vector.memset(hs, 1.0))
                    sqv = sq2.rearrange("p (h d) -> p h d", h=MH)
                    for w in range(2)[kept]:
                        link(tt(sqv, full[:, w], full[:, w], ALU.mult))
                        link(nc.vector.tensor_reduce(hs[:, w * 4:w * 4 + 4], sqv, X, ALU.add))
                    ts_(hs, hs, 1.0 / QKD, EPS, ALU.mult, ALU.add).then_inc(dve_made_for_act, 1)
                    from_act()
                    link(nc.vector.reciprocal(hs, hs))
                    for w in range(2)[kept]:
                        fw = full[:, w]
                        gain = row(("q_norm_2", "k_norm_2")[w])
                        link(tt(fw, fw, bc(hs[:, w * 4:w * 4 + 4], 2, [P, MH, QKD]), ALU.mult))
                        ins = tt(fw, fw, bc(gain, 1, [P, MH, QKD]), ALU.mult)
                        if stream:
                            link(ins)
                            rot = fw[:, :, NOPE:QKD]
                            ra = sq2[:, 0:256].rearrange("p (h d) -> p h d", h=MH)
                            rb = sq2[:, 256:512].rearrange("p (h d) -> p h d", h=MH)
                            tt(ra, rot, bc(ropes[:, t, 0, :], 1, [P, MH, ROPE]), ALU.mult)
                            for rc in range(2):
                                for hf in range(2):
                                    a, o = rc * 32 + (1 - hf) * 16, rc * 32 + hf * 16
                                    ins = tt(rb[:, :, o:o + 16], rot[:, :, a:a + 16],
                                             bc(ropes[:, t, 1, o:o + 16], 1, [P, MH, 16]), ALU.mult)
                            link(ins)
                            ins = tt(rot, ra, rb, ALU.add)
                            if w == 0:
                                link(ins)
                    ins.then_inc(dve_made_for_pe, 1)
                    for w in range(2)[kept]:
                        o = (0 if w == 0 else T * stream) + t * P
                        for part, dst in enumerate(((qTn, kTn)[w], (qTr, kTr)[w])):
                            b = job()
                            rows = P if part == 0 else ROPE
                            nc.vector.tensor_copy(dst[0:rows, :, o:o + P],
                                                  b[0:rows, :].rearrange("p (h t) -> p h t", h=MH))\
                                .then_inc(dve_read, 1)
                if not full_:
                    return
                b = job()
                nc.vector.tensor_copy(sq2[:, 0:512], b[:, :]).then_inc(dve_read, 1)
                dve.drain().then_inc(dve_made_for_pe, 1)
                for t in range(NT):
                    b = job()
                    for h in range(4):
                        u = uv[:, t, h * HD:(h + 1) * HD]
                        ins = stt(u, b[:, h * HD:(h + 1) * HD], vec("b_sgu_2", layer * 4 + h), u,
                                  ALU.add, ALU.mult)
                    ins.then_inc(dve_read, 1)
                    dve.drain().then_inc(dve_made_for_pe, 1)
                for t in range(NT):
                    b = job()
                    nc.vector.tensor_copy(yT[:, 0:2, t * P:(t + 1) * P],
                                          b[:, 0:2 * P].rearrange("p (c t) -> p c t", c=2)).then_inc(dve_read, 1)
                for c in range(2):
                    b = job()
                    nc.vector.tensor_copy(acs[:, :, c, :], b[:, :].rearrange("p (s n) -> p s n", s=2))\
                        .then_inc(dve_read, 1)
                dve.drain().then_inc(dve_made_for_pe, 1)
                for c in range(2):
                    b = job()
                    nc.vector.tensor_copy(yT[:, 2 + c, :], b[:, 0:T]).then_inc(dve_read, 1)
                units2 = mla_units()
                nk = 2 * T if stream else T

                def V2(i, b):
                    qt, h = units2[i]
                    nc.vector.tensor_copy(yT[:, 4 + h, qt * P:(qt + 1) * P], b[:, 0:P]).then_inc(dve_read, 1)

                attention(len(units2), 1, pr2, QKD ** -0.5, lambda i: nk // P, sums, negs, None, V2, 1)
                residual(src, lambda c: mod(2 + layer, 2, c, 1, cond), False)

            def route(layer, stream):
                src = xT if stream else cT
                cond = 0 if stream else 1
                link(scale_cols(8, 2 + layer, 4, cond))
                dve.drain().then_inc(dve_made_for_act, 1)
                norm(src, mhT, mxn, mstd)
                aff = small[:, 128:160].rearrange("p (t e) -> p t e", t=NT)
                place = small[:, 160:192].rearrange("p (t e) -> p t e", t=NT)
                m2 = small[:, 100:102]
                b = job()
                lg = b[:, 0:32].rearrange("p (t e) -> p t e", t=NT)
                link(nc.vector.tensor_reduce(m2, lg, X, ALU.max))
                tt(aff, lg, bc(m2, 2, [P, NT, NE]), ALU.subtract).then_inc(dve_read, 1)
                dve.drain().then_inc(dve_made_for_act, 1)
                from_act()
                link(nc.vector.tensor_reduce(m2, aff, X, ALU.add))
                link(nc.vector.reciprocal(m2, m2))
                tt(aff, aff, bc(m2, 2, [P, NT, NE]), ALU.mult).then_inc(dve_made_for_pe, 1)
                b = job()
                arow, wrow, prow = exs
                link(nc.vector.tensor_copy(arow, b[0:NE, 0:T]))
                nc.vector.memset(zrow, 0.0).then_inc(dve_read, 1)
                m8 = small[0:NE, 104:112]
                s_ = arow
                for r in range(CAP // 8):
                    link(nc.vector.max(m8, s_))
                    link(nc.vector.match_replace(wrow, m8, s_, -1.0))
                    s_ = wrow
                link(ts_(arow, wrow, 0.0, None, ALU.is_lt))
                link(nc.vector.tensor_tensor_scan(prow, arow, zrow, 0.0, ALU.add, ALU.add))
                tt(prow, prow, arow, ALU.mult).then_inc(dve_made_for_pe, 1)
                b = job()
                nc.vector.tensor_copy(small[:, 160:192], b[:, 0:32]).then_inc(dve_read, 1)
                dve.drain().then_inc(dve_chain, 1)
                n["chain"] += 1
                dve.wait_ge(dve_chain, n["chain"])
                for t in range(NT):
                    one = pm[:, t, :].rearrange("p (e s) -> p e s", e=NE)
                    wtd = pg[:, t, :].rearrange("p (e s) -> p e s", e=NE)
                    link(tt(one, bc(iota1, 1, [P, NE, CAP]), bc(place[:, t, :], 2, [P, NE, CAP]),
                            ALU.is_equal))
                    ins = tt(wtd, one, bc(aff[:, t, :], 2, [P, NE, CAP]), ALU.mult)
                ins.then_inc(dve_made_for_pe, 1)
                for c in range(0, DC, 2):
                    b = job()
                    ts_(xsT[stream][:, c, :], b[:, :], ac(8, c), mod(2 + layer, 3, c, 1, cond),
                        ALU.mult, ALU.add).then_inc(dve_read, 1)
                for half in range(2):
                    b = job()
                    nc.vector.tensor_copy(pgT[stream][:, 2 * half:2 * half + 2, :],
                                          b[:, :].rearrange("p (g t) -> p g t", g=2)).then_inc(dve_read, 1)
                barrier()

            def experts(layer, streams):
                ns = len(streams)
                base = NG * layer
                base_s = 2 * NG * layer
                if layer == 0:
                    dve.drain().then_inc(y_read, 1)
                with dve.Fori(0, NG) as g:
                    for i, s in enumerate(streams):
                        dve.wait_ge(hid_silu, g * ns + (base_s + i + 1))
                        tt(hid[s], hid[s], banks[2 * s + 1][:, :], ALU.mult).then_inc(hid_ready, 1)
                    dve.wait_ge(y_ready, g + (base + 1))
                    for s in streams:
                        for half in range(2):
                            ins = nc.vector.tensor_copy(
                                ys[s].rearrange("p g d -> p (g d)")[:, bass.ds(g * D + half * 512, 512)],
                                banks[4 + 2 * s + half][:, :])
                    ins.then_inc(y_read, 1)
                barrier()
                for s in streams:
                    if s != streams[0]:
                        barrier()
                    residual((cT, xT)[s], lambda c: mod(2 + layer, 5, c, 1, 1 - s), False)
                barrier()

            for layer in range(LAYERS):
                mixers(layer, 0)
                mixers(layer, 1)
                for s in ((0, 1) if layer == 0 else (1,)):
                    route(layer, s)
                experts(layer, (0, 1) if layer == 0 else (1,))
            for c in range(0, DC, 2):
                job()
                b = banks[c // 2]
                nc.vector.tensor_copy(
                    tok_in[:, :, c * P:(c + 2) * P].rearrange("p t (c q) -> p c t q", c=2),
                    b[:, :].rearrange("p (c t q) -> p c t q", c=2, t=NT)).then_inc(out_copied, 1)


INS = ["x", "c", "l0_norm_mix", "l0_norm_ffn", "l0_mod_w", "l0_mod_b", "l0_w_in", "l0_conv_w",
       "l0_conv_b", "l0_lru_wa", "l0_lru_ba", "l0_lru_wx", "l0_lru_bx", "l0_lru_lambda",
       "l0_cmp_pe_k", "l0_cmp_w1_k", "l0_cmp_w2_k", "l0_cmp_pe_v", "l0_cmp_w1_v", "l0_cmp_w2_v",
       "l0_w_out", "l0_ffn_wg", "l0_ffn_wu", "l0_ffn_wd", "l1_norm_mix", "l1_norm_ffn", "l1_mod_w",
       "l1_mod_b", "l1_w_in", "l1_w_out", "l1_ffn_wg", "l1_ffn_wu", "l1_ffn_wd", "final_norm", "c_2",
       "ctx_2", "c_ctx_2", "w_ada_2", "b_ada_2", "w_in_2", "sgu_norm_2", "w_sgu_2", "b_sgu_2",
       "q_lora_norm_2", "w_uq_2", "kv_lora_norm_2", "w_ukv_2", "q_norm_2", "k_norm_2", "w_out_2",
       "w_router_2", "w_gate_2", "w_up_2", "w_down_2"]


def shape_tables():
    tab = np.zeros((P, C_END), np.float64)
    n = np.arange(T)
    ang = 2 * np.pi * (np.outer(n, n) % T) / T
    dft = np.stack([np.cos(ang), np.sin(ang)], 1) / np.sqrt(T)
    tab[:, C_DFTN:C_DFTN + 1024] = dft.reshape(NT, P, 2 * T).transpose(1, 0, 2).reshape(P, -1)
    d = np.arange(64)
    angd = 2 * np.pi * (np.outer(d, d) % 64) / 64
    for g in range(2):
        o = g * 64
        tab[o:o + 64, C_DFTD + o:C_DFTD + o + 64] = np.cos(angd) / 8
        tab[o:o + 64, C_DFTD + P + o:C_DFTD + P + o + 64] = -np.sin(angd) / 8
    q = np.arange(P)
    tab[:, C_CAUSAL:C_CAUSAL + P] = np.where(q[None, :] > q[:, None], NEG, 0.0)
    blk = np.arange(32)
    for t in range(NT):
        seen = (blk[None, :] * CMP_STRIDE + CMP_LEN - 1 <= (t * P + q)[:, None]) & (blk[None, :] < NBLK)
        tab[:, C_CMP + t * 256:C_CMP + (t + 1) * 256] = np.tile(np.where(seen, 0.0, NEG), (1, 8))
    tab[:, C_IDENT:C_IDENT + P] = np.eye(P)
    tab[:, C_IOTA:C_IOTA + CAP] = np.arange(1, CAP + 1)
    freqs = (np.float32(10000.0) ** (-np.arange(16, dtype=np.float32) / np.float32(16))).astype(np.float32)
    for t in range(NT):
        tok = t * P + q
        for rc, pos in enumerate((tok // 64, tok % 64)):
            a = (pos[:, None].astype(np.float32) * freqs).astype(np.float64)
            o = C_ROPE + t * 128 + rc * 32
            for hf in range(2):
                tab[:, o + hf * 16:o + hf * 16 + 16] = np.cos(a)
                tab[:, o + 64 + hf * 16:o + 64 + hf * 16 + 16] = np.sin(a) * (1 if hf else -1)
    return tab.astype(np.float32)


def kernel(**inputs):
    import concourse.bacc as bacc
    from concourse.bass_utils import run_bass_kernel_spmd

    nc = bacc.Bacc("TRN2", target_bir_lowering=False, num_devices=1)
    arrays, aps = {}, {}
    for name in INS:
        a = np.ascontiguousarray(inputs[name])
        arrays[f"in_{name}"] = a
        aps[name] = nc.dram_tensor(f"in_{name}", a.shape, mybir.dt.from_np(a.dtype), kind="ExternalInput").ap()
    table = shape_tables()
    arrays["shape_tables"] = table
    aps["shape_tables"] = nc.dram_tensor("shape_tables", table.shape, F32, kind="ExternalInput").ap()
    aps["out"] = nc.dram_tensor("out", (1, T, D), F32, kind="ExternalOutput").ap()
    program(nc, aps)
    r = run_bass_kernel_spmd(nc, [arrays], core_ids=[0])
    return r.results[0]["out"]
```

```python
from contextlib import ExitStack

import numpy as np

import concourse.bass as bass
from concourse import mybir

F32 = mybir.dt.float32
ACT = mybir.ActivationFunctionType
ALU = mybir.AluOpType
X = mybir.AxisListType.X

P = 128
D = 1024
DC = D // P
T = 256
NT = T // P
F = 2816
FC = F // P
EPS = 1e-6
HD = 64
TAKEN = -3e38
NEG = -1e30
FLOOR = -1e20

LRU = 512
LC = LRU // P
CMP_LEN, CMP_STRIDE = 32, 16
NBLK = (T - CMP_LEN) // CMP_STRIDE + 1
TOPK = min(256, T // 4)
IDX_HEADS = 8

NE, CAP, DE = 16, 2 * T // 16, 512
GE = P // CAP
NG = NE // GE
MH, NOPE, ROPE = 4, 128, 64
QKD = NOPE + ROPE

SLOTS = 6
SLOT = 4096

C_DFTN, C_DFTD = 0, 1024
C_CMP = C_DFTD + 256
C_CAUSAL = C_CMP + NT * 256
C_IDENT = C_CAUSAL + P
C_IOTA = C_IDENT + P
C_ROPE = C_IOTA + CAP
C_END = C_ROPE + 2 * T + P

VEC_NAMES = [
    ["l0_mod_b", "l1_mod_b", "l0_norm_mix", "l0_norm_ffn", "l1_norm_mix", "l1_norm_ffn"],
    ["b_ada_2", "final_norm", "c", "c_2", "c_ctx_2"],
    ["l0_conv_w", "l0_conv_b", "l0_lru_ba", "l0_lru_bx", "l0_lru_lambda", "q_lora_norm_2",
     "kv_lora_norm_2"],
]
VEC_ROWS = {"l0_mod_b": 48, "l1_mod_b": 48, "l0_norm_mix": 8, "l0_norm_ffn": 8, "l1_norm_mix": 8,
            "l1_norm_ffn": 8, "b_ada_2": 96, "final_norm": 8, "c": 8, "c_2": 8, "c_ctx_2": 8,
            "l0_conv_w": 16, "l0_conv_b": 4, "l0_lru_ba": 4, "l0_lru_bx": 4, "l0_lru_lambda": 4,
            "q_lora_norm_2": 4, "kv_lora_norm_2": 2}


HEAD_VECS = {"q_nope": ("q_norm_2", 0, NOPE), "q_rope": ("q_norm_2", NOPE, ROPE),
             "k_nope": ("k_norm_2", 0, NOPE), "k_rope": ("k_norm_2", NOPE, ROPE)}


def ffn_pieces(layer, extra):
    out, extra = [], list(extra)
    steps = -(-F // 512)
    per = -(-len(extra) // steps)
    for s in range(steps):
        out += [("wg", layer, s), ("wu", layer, s), ("wd", layer, s)]
        out += extra[:per]
        del extra[:per]
    return out


def ada_after(extra):
    out, step = {}, -1
    for key in ffn_pieces(0, extra):
        step += key[0] == "wg"
        if key[0] == "ada":
            f = min(4 * step + 3, FC - 1)
            out[f] = out.get(f, 0) + 1
    return out


def ada(matrix, first=0, end=12):
    return [("ada", matrix, s) for s in range(first, end)]


ADA_AT = {
    "start": ada(0, 0, 4),
    "lru": ada(0, 4, 8),
    "attention0": ada(0, 8, 12) + ada(1, 0, 4),
    "ffn0": ada(1, 4, 12) + ada(2, 0, 4),
    "norm1": ada(2, 4, 5),
    "attention1": ada(2, 5, 12) + ada(3, 0, 1),
    "ffn1": ada(3, 1, 12),
}


def weight_pieces():
    out = list(ADA_AT["start"])
    out += [("in0", s) for s in (1, 0, 2, 3, 4)]
    out += [("lru",), ("cmp",)] + ADA_AT["lru"] + ADA_AT["attention0"]
    out += [("out", 0, 0), ("out", 0, 1)]
    out += ffn_pieces(0, ADA_AT["ffn0"]) + ADA_AT["norm1"]
    out += [("in1", s) for s in range(4)] + ADA_AT["attention1"] + [("out", 1, 0), ("out", 1, 1)]
    out += ffn_pieces(1, ADA_AT["ffn1"])
    for layer in range(2):
        for stream in ("ctx", "x"):
            full = stream == "x" or layer == 0
            out += [("in2", layer, s) for s in ((1, 2, 0) if full else (2,))]
            out += [("mla", layer)]
            if full:
                out += [("tab",), ("out2", layer, 0), ("out2", layer, 1)]
        for g in range(NG):
            out += [("moe", layer, kind, g, s) for kind in range(3) for s in range(4)]
    return out


def program(nc, A):
    ctx = ExitStack()
    with ctx:
        def sb(name, cols):
            return ctx.enter_context(nc.sbuf_tensor(name, [P, cols], F32))

        def sem(name):
            return ctx.enter_context(nc.semaphore(name))

        ring = sb("ring", SLOTS * SLOT)
        xT_ = sb("xT", DC * T)
        cT_ = sb("ctxT", DC * T)
        hT_ = sb("hT", DC * T)
        tab = sb("tab", C_ROPE - C_CAUSAL)
        ones = sb("ones", P)
        halves = sb("halves", 64)
        vecs = sb("vecs", 2 * P + 56)
        mods = sb("mods", 48 * 6)
        acol = sb("acol", 72)
        csil_ = sb("csil", DC * 32)
        small = sb("small", 200)
        brow = sb("brow", 1024)
        SCR = 19456
        scr = sb("scr", SCR)
        banks = [ctx.enter_context(nc.psum_tensor(f"bank{i}", [P, 512], F32)) for i in range(8)]

        def v3(t, o, a, b):
            return t[:, o:o + a * b].rearrange("p (a b) -> p a b", a=a)

        csil, wrt = v3(csil_, 0, DC, 32), csil_
        xT, cT, hT = v3(xT_, 0, DC, T), v3(cT_, 0, DC, T), v3(hT_, 0, DC, T)
        causal = tab[:, 0:P]
        ident = tab[:, C_IDENT - C_CAUSAL:C_IDENT - C_CAUSAL + P]
        iota1 = tab[:, C_IOTA - C_CAUSAL:C_IOTA - C_CAUSAL + CAP]

        vcol, o = {}, 0
        for t, names in enumerate(VEC_NAMES):
            o = t * P
            for n in names:
                vcol[n] = o
                o += VEC_ROWS[n]
        for n in HEAD_VECS:
            vcol[n] = o
            o += 2
        third_rows = o - 2 * P

        def vec(name, c=0, n=1):
            return vecs[:, vcol[name] + c:vcol[name] + c + n]

        MODO = [0, 48, 96, 192]

        def mod(matrix, seg, c, n=1, cond=0):
            if matrix < 2:
                o = MODO[matrix] + seg * 8 + c
                return mods[:, o:o + n]
            o = MODO[matrix] + (seg * 8 + c) * 2 + cond
            return mods[:, o:o + 2 * n - 1:2] if n > 1 else mods[:, o:o + 1]

        def ac(i, c=0, n=1):
            return acol[:, i * 8 + c:i * 8 + c + n]

        pieces = weight_pieces()
        index = {}
        for k, key in enumerate(pieces):
            index.setdefault(key, []).append(k)
        n_dma = {"lru": 4, "cmp": 2, "mla": 4, "moe": GE, "out": 1}

        def dmas_of(key):
            if key[0] == "out" and key[1:] == (0, 1) or key[0] == "out" and key[1] == 1:
                return 2
            if key[0] == "moe" and key[2] == 2:
                return GE
            return n_dma.get(key[0], 1)

        landed, count = [], [0] * SLOTS
        for k, key in enumerate(pieces):
            count[k % SLOTS] += 16 * dmas_of(key)
            landed.append(count[k % SLOTS])

        def slot(k):
            return ring[:, (k % SLOTS) * SLOT:(k % SLOTS + 1) * SLOT]

        slot_loaded = [sem(f"slot_loaded{i}") for i in range(SLOTS)]
        slots_released = sem("slots_released")

        loads = sem("loads")
        stream_loads = sem("stream_loads")
        row_loads = sem("row_loads")
        out_copied, stored = sem("out_copied"), sem("stored")
        pe_to_dve, dve_read = sem("pe_to_dve"), sem("dve_read")
        pe_to_act, act_read = sem("pe_to_act"), sem("act_read")
        pe_phase, act_phase, dve_phase = sem("pe_phase"), sem("act_phase"), sem("dve_phase")
        dve_chain, act_chain = sem("dve_chain"), sem("act_chain")
        dve_made_for_pe, act_made_for_pe = sem("dve_made_for_pe"), sem("act_made_for_pe")
        dve_made_for_act, act_made_for_dve = sem("dve_made_for_act"), sem("act_made_for_dve")
        pe_made_for_act, pe_made_for_dve = sem("pe_made_for_act"), sem("pe_made_for_dve")
        x_ready = sem("x_ready")
        squares_ready, var_ready = sem("squares_ready"), sem("var_ready")
        std_ready, xn_ready, h_ready = sem("std_ready"), sem("xn_ready"), sem("h_ready")
        ada_rows, ada_copied = sem("ada_rows"), sem("ada_copied")
        ada_cols, ada_read = sem("ada_cols"), sem("ada_read")
        gu_ready, silu_ready, act_ready = sem("gate_up_ready"), sem("silu_ready"), sem("act_ready")
        acc_ready = sem("acc_ready")
        scores_ready, negmax_ready, exp_done = sem("scores_ready"), sem("negmax_ready"), sem("exp_done")
        probs_ready, turned, turned_copied = sem("probs_ready"), sem("turned"), sem("turned_copied")
        index_added = sem("index_added")
        xs_ready, gu_done, hid_silu, hid_ready = sem("xs_ready"), sem("gu_done"), sem("hid_silu"), sem("hid_ready")
        hid_turned, hid_copied, y_ready, y_read = sem("hid_turned"), sem("hid_copied"), sem("y_ready"), sem("y_read")

        class Arena:
            def __init__(self, at=0):
                self.at = at

            def take(self, *shape):
                n = 1
                for s in shape:
                    n *= s
                ap = scr[:, self.at:self.at + n]
                self.at += n
                assert self.at <= SCR, self.at
                if len(shape) == 2:
                    ap = ap.rearrange("p (a b) -> p a b", a=shape[0])
                elif len(shape) == 3:
                    ap = ap.rearrange("p (a b c) -> p a b c", a=shape[0], b=shape[1])
                return ap

        xn = v3(scr, 0, DC, T)
        std = scr[:, 2048:2304]
        tok_in = v3(scr, 4096, NT, D)
        tok_in2 = v3(scr, 6144, NT, D)
        vec_rows = v3(scr, 8192, 3, P)
        pe_rows = scr[0:CMP_LEN, 8576:8576 + 256]
        peT = small[:, 0:64]
        selector = small[:, 192:195]
        lam = small[:, 64:84]

        a0 = Arena(2304)
        axp = a0.take(LC, T + 3)
        xc = a0.take(LC, T)
        gg = a0.take(LC, T)
        rr = a0.take(LC, T)
        ii = a0.take(LC, T)
        aa = a0.take(LC, T)
        th = a0.take(LC, T)
        q0 = a0.take(4, T)
        ks0, kw0 = a0.take(T), a0.take(T)
        vs0, vw0 = a0.take(NT, P), a0.take(NT, P)
        gts = a0.take(NT, 8, 3)
        ft = [a0.take(CMP_STRIDE, 2, NBLK) for _ in range(2)]
        h1 = a0.take(2, 2, NBLK)
        kc = a0.take(CMP_STRIDE)
        vc = a0.take(2, HD)
        pc = a0.take(NT, 8, 32)
        pcT = a0.take(2, T)
        cmp_mask = a0.take(NT, 256)
        assert a0.at - NT * 256 >= 8832
        pr = a0.take(2, 512)
        pt = a0.take(2, 512)
        a1 = Arena(2304)
        q1 = a1.take(8, T)
        k1 = a1.take(T)
        v1 = a1.take(NT, P)
        qi = a1.take(4, T)
        ki = a1.take(T)
        wi = a1.take(NT, IDX_HEADS)
        idx = a1.take(NT, T)
        work = a1.take(NT, T)
        sel = a1.take(NT, T)
        rel = a1.take(2, 512)
        pr1 = a1.take(2, 512)
        pt1 = a1.take(2, 512)
        yT = v3(scr, 0, DC, T)
        assert a1.at + 0 < SCR
        af = Arena(2304)
        sil = af.take(2, T)
        actT = af.take(4, T)
        a2 = Arena(2304)
        kTn = a2.take(MH, 2 * T)
        kTr = a2.take(2, 2 * T)
        vv = a2.take(4, 512)
        uT = a2.take(2, T)
        vg = a2.take(NT, 256)
        fq = a2.take(NT, 256)
        cqT = a2.take(3, T)
        lsq = a2.take(4, T)
        lrs = a2.take(2, T)
        qraw = lrs
        krg = a2.take(T)
        rk = a2.take(T)
        rq = a2.take(T)
        acs = a2.take(2, 2, T)
        pr2 = a2.take(2, 512)
        pt2 = a2.take(2, 512)
        ksq = pr2.rearrange("p h (c t) -> p h c t", c=2)
        qsq = pt2.rearrange("p h (c t) -> p h c t", c=2)
        qrsq = a2.take(2, T)
        ra = a2.take(2, T)
        rb = a2.take(2, T)
        qTn = a2.take(MH, T)
        qTr = a2.take(2, T)
        wsT = a2.take(512)
        sgu_gain = brow[:, 0:256]
        sgu_bias = brow[:, 256:512].rearrange("p (c q) -> p c q", c=2)
        am = Arena(0)
        xsT = [am.take(DC, NE * CAP) for _ in range(2)]
        ys = [am.take(NG, D) for _ in range(2)]
        xs = [am.take(DC, P) for _ in range(2)]
        hid = [brow[:, s * 512:(s + 1) * 512] for s in range(2)]
        hidT = [am.take(4, P) for _ in range(2)]
        ay = Arena(8192)
        mxn = ay.take(DC, T)
        mhT = ay.take(DC, T)
        xtok = ay.take(NT, D)
        pm = ay.take(NT, NE * CAP)
        pg = ay.take(NT, NE * CAP)
        pgT = [v3(hT_, s * 1024, NG, T) for s in range(2)]
        mstd = scr[:, 17408:17664]
        ex = scr[:, 16384:16384 + 3 * T]
        exs = [ex[0:NE, i * T:(i + 1) * T] for i in range(3)]
        zrow = scr[0:NE, 17152:17152 + T]

        block = ctx.enter_context(nc.Block())

        in0_cols = [(s * 512, min(512, 2328 - s * 512)) for s in range(5)]
        in1_cols = [(s * 512, min(512, 1864 - s * 512)) for s in range(4)]
        in2_cols = [(0, 512), (512, 512), (1024, 192)]

        def source(key):
            kind = key[0]

            def cols(w, o, n):
                return [((0, P), (0, DC * n), w[:, o:o + n].rearrange("(c p) n -> p c n", p=P))]
            if kind == "ada":
                m, s = key[1:]
                w = A[f"l{m}_mod_w"] if m < 2 else A["w_ada_2"][m - 2]
                return cols(w, s * 512, 512)
            if kind == "in0":
                return cols(A["l0_w_in"], *in0_cols[key[1]])
            if kind == "in1":
                return cols(A["l1_w_in"], *in1_cols[key[1]])
            if kind == "in2":
                return cols(A["w_in_2"][key[1]], *in2_cols[key[2]])
            if kind == "lru":
                out = []
                for i, n in enumerate(("l0_lru_wa", "l0_lru_wx")):
                    out.append(((0, P), (i * 256, 256), A[n].rearrange("(a two) i j -> (two i) a j", two=2)))
                for i, n in enumerate(("l0_cmp_w2_k", "l0_cmp_w2_v")):
                    out.append(((0, P), (512 + i * HD, HD), A[n]))
                return out
            if kind == "cmp":
                return [((0, P), (i * 2048, 2048), A[n].rearrange("(c p) n -> p c n", p=P))
                        for i, n in enumerate(("l0_cmp_w1_k", "l0_cmp_w1_v"))]
            if kind == "out":
                layer, half = key[1:]
                w = A[f"l{layer}_w_out"]
                if layer == 0 and half == 0:
                    return [((0, P), (0, 4096), w[0:512, :].rearrange("(c p) n -> p c n", p=P))]
                out = []
                for g in range(2):
                    o = 512 + g * 256 if layer == 0 else g * 512 + half * 256
                    out.append(((g * HD, g * HD + HD), (0, 4096),
                                w[o:o + 256, :].rearrange("(c d) n -> d c n", d=HD)))
                return out
            if kind == "wg" or kind == "wu":
                n = min(512, F - key[2] * 512)
                return cols(A[f"l{key[1]}_ffn_{kind}"], key[2] * 512, n)
            if kind == "wd":
                n = min(512, F - key[2] * 512)
                w = A[f"l{key[1]}_ffn_wd"][key[2] * 512:key[2] * 512 + n, :]
                return [((0, P), (0, n // P * D), w.rearrange("(c p) n -> p c n", p=P))]
            if kind == "mla":
                l = key[1]
                return [((0, P), (3072, C_END - C_ROPE), A["shape_tables"][:, C_ROPE:C_END]),
                        ((0, P), (0, 1536), A["w_uq_2"][l].rearrange("(c p) n -> p c n", p=P)),
                        ((0, P), (1536, 1024), A["w_ukv_2"][l]),
                        ((0, P), (2560, 512), A["w_sgu_2"][l].rearrange("h p q -> p h q"))]
            if kind == "tab":
                return [((0, P), (0, C_CAUSAL), A["shape_tables"][:, 0:C_CAUSAL])]
            if kind == "out2":
                w = A["w_out_2"][key[1]][key[2] * 512:key[2] * 512 + 512, :]
                return [((0, P), (0, 4096), w.rearrange("(c p) n -> p c n", p=P))]
            raise ValueError(key)

        def moe_source(layer, kind, group, s, j):
            name = ("w_gate_2", "w_up_2", "w_down_2")[kind]
            w = A[name][layer].rearrange("(g e) (s p) n -> g e s p n", e=GE, p=P)
            if kind < 2:
                return w[group, j, 2 * s:2 * s + 2].rearrange("s p n -> p s n")
            return w[group, j, s]

        @block.sync
        def _(sp):
            sp.dma_start(tab[:, :], A["shape_tables"][:, C_CAUSAL:C_ROPE]).then_inc(stream_loads, 16)
            sp.dma_start(tok_in[:, :, :], A["x"][0].rearrange("(t p) d -> p t d", p=P)).then_inc(stream_loads, 16)
            sp.dma_start(tok_in2[:, :, :], A["ctx_2"][0].rearrange("(t p) d -> p t d", p=P))\
                .then_inc(stream_loads, 16)
            for t, names in enumerate(VEC_NAMES):
                o = 0
                for n in names:
                    rows = VEC_ROWS[n]
                    a = A[n]
                    if len(a.shape) == 3:
                        a = a.rearrange("l h p -> (l h) p")
                    elif len(a.shape) == 2:
                        a = a.rearrange("a (r p) -> (a r) p", p=P)
                    else:
                        a = a.rearrange("(r p) -> r p", p=P)
                    sp.dma_start(vec_rows[o:o + rows, t, :], a).then_inc(loads, 16)
                    o += rows
            for n, (a, first, m) in HEAD_VECS.items():
                o = vcol[n] - 2 * P
                for copy in range(P // m):
                    sp.dma_start(vec_rows[o:o + 2, 2, copy * m:(copy + 1) * m], A[a][:, first:first + m])\
                        .then_inc(loads, 16)
            for i, n in enumerate(("l0_cmp_pe_k", "l0_cmp_pe_v")):
                for j in range(2):
                    sp.dma_start(pe_rows[:, i * P + j * HD:i * P + j * HD + HD], A[n]).then_inc(loads, 16)
            sp.dma_start(cmp_mask, A["shape_tables"][:, C_CMP:C_CMP + NT * 256].rearrange(
                "p (t n) -> p t n", t=NT)).then_inc(loads, 16)

            def load_rows(layer):
                sp.dma_start(sgu_gain, A["sgu_norm_2"][layer:layer + 1, :].to_broadcast([P, 256]))\
                    .then_inc(row_loads, 16)
                for h in range(MH):
                    lo = h % 2 * HD
                    sp.dma_start(sgu_bias[lo:lo + HD, h // 2, :],
                                 A["b_sgu_2"][layer, h:h + 1, :].to_broadcast([HD, P])).then_inc(row_loads, 16)

            k = 0
            while k < len(pieces):
                key = pieces[k]
                if key[0] == "moe":
                    layer, per = key[1], 12
                    with sp.Fori(0, NG) as g:
                        for m in range(per):
                            _, _, kind, _, s = pieces[k + m]
                            sp.wait_ge(slots_released, g * per + (k + m - SLOTS + 1))
                            for j in range(GE):
                                dst = slot(k + m)[:, j * 1024:(j + 1) * 1024]
                                if kind < 2:
                                    dst = dst.rearrange("p (s n) -> p s n", s=2)
                                sp.dma_start(dst, moe_source(layer, kind, g, s, j)).then_inc(
                                    slot_loaded[(k + m) % SLOTS], 16)
                    k += per * NG
                    continue
                if k >= SLOTS:
                    sp.wait_ge(slots_released, k - SLOTS + 1)
                for (p0, p1), (o, n), src in source(key):
                    dst = slot(k)[p0:p1, o:o + n]
                    if len(src.shape) == 3:
                        dst = dst.rearrange("p (a b) -> p a b", a=src.shape[1])
                    sp.dma_start(dst, src).then_inc(slot_loaded[k % SLOTS], 16)
                k += 1
                if key == ("mla", 0) \
                        and ("mla", 0) not in pieces[:k - 1]:
                    sp.wait_ge(ada_cols, 48)
                    for l in range(2):
                        sp.dma_start(v3(wrt, l * P, DC, NE),
                                     A["w_router_2"][l].rearrange("(c p) n -> p c n", p=P))\
                            .then_inc(row_loads, 16)
                    load_rows(0)
                if key == ("mla", 1) and pieces[k - 3][0] == "moe":
                    sp.wait_ge(slots_released, k - 2)
                    load_rows(1)
            sp.wait_ge(out_copied, DC // 2)
            sp.dma_start(A["out"][0].rearrange("(t p) d -> p t d", p=P), tok_in[:, :, :]).then_inc(stored, 16)
            sp.wait_ge(stored, 16)

        N_LOADS = 16 * (sum(len(n) for n in VEC_NAMES) + 6 + 4 + 1)
        LAYERS = 2

        def nsa_units():
            return [(qt, c, g) for qt in range(NT) for c in range(4) for g in range(2)]

        def dsa_units():
            return [(qt, cp, g) for qt in range(NT) for cp in range(4) for g in range(2)]

        def mla_units():
            return [(qt, h) for qt in range(NT) for h in range(MH)]

        @block.tensor
        def _(pe):
            n = {"dve": 0, "act": 0, "columns_read": 0, "jobs_read": 0, "piece": 0, "phase": 0, "ln": 0, "unit": 0, "ada": 0, "gu": 0,
                 "squares": 0, "h": 0, "turned": 0, "from_act": 0, "from_dve": 0}
            ada_log = []
            owed = []

            def mm(out, lhsT, rhs, start=True, stop=True, signal=None):
                ins = nc.tensor.matmul(out, lhsT, rhs, start=start, stop=stop, skip_group_check=True)
                if signal is not None:
                    ins.then_inc(signal, 1)
                elif owed:
                    owed.pop(0)
                    ins.then_inc(slots_released, 1)
                return ins

            def turn(out, in_, signal=None):
                k = in_.shape[0]
                ins = nc.tensor.transpose(out, in_, ident[0:k, 0:k])
                if signal is not None:
                    ins.then_inc(signal, 1)
                return ins

            def barrier():
                n["phase"] += 1
                pe.drain().then_inc(pe_phase, 1)
                pe.wait_ge(act_phase, n["phase"])
                pe.wait_ge(dve_phase, n["phase"])

            def from_dve():
                n["from_dve"] += 1
                pe.wait_ge(dve_made_for_pe, n["from_dve"])

            def from_act():
                n["from_act"] += 1
                pe.wait_ge(act_made_for_pe, n["from_act"])

            def bank_for_dve():
                k = n["dve"]
                n["dve"] += 1
                if k >= 2:
                    pe.wait_ge(dve_read, k - 1)
                return banks[k % 2]

            def bank_for_act():
                k = n["act"]
                n["act"] += 1
                if k >= 2:
                    pe.wait_ge(act_read, k - 1)
                if n["turned"] > n["columns_read"]:
                    pe.wait_ge(ada_read, n["turned"])
                    n["columns_read"] = n["turned"]
                return banks[2 + k % 2]

            def use(key):
                k = n["piece"]
                assert pieces[k] == key, (pieces[k], key)
                n["piece"] += 1
                pe.wait_ge(slot_loaded[k % SLOTS], landed[k])
                return slot(k)

            def release():
                owed.append(1)

            def settle():
                while owed:
                    owed.pop(0)
                    pe.drain().then_inc(slots_released, 1)

            def norm(sq, modulated=True):
                b = bank_for_dve()
                for c in range(DC):
                    n["squares"] += 1
                    pe.wait_ge(squares_ready, n["squares"])
                    mm(b[:, 0:T], ones[:, :], sq[:, c, :], start=(c == 0), stop=(c == DC - 1),
                       signal=pe_to_dve if c == DC - 1 else None)
                if modulated:
                    n["h"] += 1

            def wait_h(c):
                pe.wait_ge(h_ready, (n["h"] - 1) * DC + c + 1)

            def to_T(out, w, o, m, h=hT, signal=None):
                for c in range(DC):
                    mm(out, w[:, c, o:o + m], h[:, c, :], start=(c == 0), stop=(c == DC - 1),
                       signal=signal if c == DC - 1 else None)

            def to_T_halves(out, ws, offsets, signal=None):
                for c in range(DC):
                    for g in range(2):
                        mm(out[g * HD:(g + 1) * HD, :], ws[g][:, c, offsets[g]:offsets[g] + HD], hT[:, c, :],
                           start=(c == 0), stop=(c == DC - 1), signal=signal if c == DC - 1 and g else None)

            def to_tok(out, w, o, m, t, h=hT, signal=None):
                for c in range(DC):
                    mm(out, h[:, c, t * P:(t + 1) * P], w[:, c, o:o + m], start=(c == 0),
                       stop=(c == DC - 1), signal=signal if c == DC - 1 else None)

            def ada_columns():
                k = n["ada"] - 1
                matrix, s = ada_log[-1]
                lo, m = (0, 1) if matrix < 2 else (1, 2)
                pe.wait_ge(ada_copied, k + 1)
                if k >= 1:
                    pe.wait_ge(ada_read, k)
                for j in range(4):
                    mm(banks[3][:, j * m:(j + 1) * m], brow[:, (k % 2) * 512 + j * P:(k % 2) * 512 + (j + 1) * P],
                       selector[:, lo:lo + m], signal=ada_cols if j == 3 else None)

            def ada_pieces(keys, turn_last=True):
                for key in keys:
                    w = use(key).rearrange("p (c n) -> p c n", c=DC)
                    k = n["ada"]
                    if k >= 1:
                        pe.wait_ge(ada_copied, k)
                    if n["act"] > n["jobs_read"]:
                        pe.wait_ge(act_read, n["act"])
                        n["jobs_read"] = n["act"]
                    for c in range(DC):
                        j = c % 4
                        mm(banks[2][32 * j:32 * j + 32, :], csil[:, c, :], w[:, c, :], start=(c < 4),
                           stop=(c >= 4), signal=ada_rows if c == DC - 1 else None)
                    release()
                    if n["ada"] > n["turned"]:
                        ada_columns()
                        n["turned"] += 1
                    n["ada"] += 1
                    ada_log.append(key[1:])
                if turn_last and n["ada"] > n["turned"]:
                    ada_columns()
                    n["turned"] += 1

            def accumulate(out_bank0, lhs, rhs, first, last):
                for c in range(DC):
                    b = banks[out_bank0 + c // 2]
                    mm(b[:, (c % 2) * T:(c % 2 + 1) * T], lhs[:, c * P:(c + 1) * P], rhs,
                       start=first and c % 2 == 0, stop=last,
                       signal=acc_ready if last and c % 2 else None)

            def mixed():
                pe.wait_ge(dve_read, n["dve"])
                pe.wait_ge(exp_done, n["unit"])
                pe.wait_ge(turned_copied, n["unit"])

            def out_proj(keys, y):
                for half, key in enumerate(keys):
                    w = use(key).rearrange("p (c n) -> p c n", c=4)
                    for k in range(4):
                        accumulate(4, w[:, k, :], y[:, half * 4 + k, :], half == 0 and k == 0,
                                   half == 1 and k == 3)
                    release()

            def ffn(layer, extra):
                keys = ffn_pieces(layer, extra)
                steps = -(-F // 512)

                def down(f, wdp, k, rel):
                    pe.wait_ge(act_ready, f_base + f + 1)
                    accumulate(4, wdp[:, k, :], actT[:, f % 4, :], f == 0, f == FC - 1)
                    if rel:
                        release()
                f_base = n["gu"]
                at = 0
                for s in range(steps):
                    nf = min(4, FC - 4 * s)
                    wg = use(("wg", layer, s))[:, 0:DC * nf * P].rearrange("p (c n) -> p c n", c=DC)
                    wu = use(("wu", layer, s))[:, 0:DC * nf * P].rearrange("p (c n) -> p c n", c=DC)
                    for k in range(nf):
                        f = 4 * s + k
                        b = banks[(f_base + f) % 2]
                        if f >= 2:
                            pe.wait_ge(act_ready, f_base + f - 1)
                        elif f == 0:
                            pe.wait_ge(dve_read, n["dve"])
                        for c in range(DC):
                            if f == 0:
                                wait_h(c)
                            mm(b[:, 0:T], wg[:, c, k * P:(k + 1) * P], hT[:, c, :], start=(c == 0),
                               stop=(c == DC - 1))
                        for c in range(DC):
                            mm(b[:, T:2 * T], wu[:, c, k * P:(k + 1) * P], hT[:, c, :],
                               start=(c == 0), stop=(c == DC - 1),
                               signal=gu_ready if c == DC - 1 else None)
                        if k > 0:
                            if k == 1:
                                wd = use(("wd", layer, s))[:, 0:nf * D].rearrange("p (c n) -> p c n", c=nf)
                            down(f - 1, wd, k - 1, False)
                    release()
                    release()
                    down(4 * s + nf - 1, wd, nf - 1, True)
                    at += 3
                    mods_ = []
                    while at < len(keys) and keys[at][0] == "ada":
                        mods_.append(keys[at])
                        at += 1
                    ada_pieces(mods_, s == steps - 1)
                n["gu"] += FC
                settle()

            def attention(N, S, V, n_blocks, pt_, pr_, fill=()):
                u0 = n["unit"]
                for i in range(N + 3):
                    if i < N:
                        u = u0 + i
                        if u >= 2:
                            pe.wait_ge(exp_done, u - 1)
                        S(i, banks[4 + u % 2])
                    if 2 <= i < N + 2:
                        u = u0 + i - 2
                        pe.wait_ge(probs_ready, u + 1)
                        if u >= 2:
                            pe.wait_ge(turned_copied, u - 1)
                        nb = n_blocks(i - 2)
                        for b in range(nb):
                            turn(banks[6 + u % 2][:, b * P:(b + 1) * P],
                                 pr_[:, u % 2, b * P:(b + 1) * P], turned if b == nb - 1 else None)
                    if i >= 3:
                        u = u0 + i - 3
                        pe.wait_ge(turned_copied, u + 1)
                        V(i - 3, pt_[:, u % 2, :])
                    if fill and i % 2 == 1 and i // 2 < len(fill):
                        ada_pieces([fill[i // 2]], i // 2 == len(fill) - 1)
                n["unit"] += N

            pe.wait_ge(stream_loads, 48)
            for src in (tok_in, tok_in2):
                for c in range(DC):
                    b = bank_for_dve() if c % 2 == 0 else b
                    for t in range(NT):
                        turn(b[:, (c % 2) * T + t * P:(c % 2) * T + (t + 1) * P],
                             src[:, t, c * P:(c + 1) * P], pe_to_dve if c % 2 and t == 1 else None)
            pe.wait_ge(loads, N_LOADS)
            b = bank_for_dve()
            for t in range(3):
                rows = third_rows if t == 2 else sum(VEC_ROWS[m] for m in VEC_NAMES[t])
                turn(b[:, t * P:t * P + rows], vec_rows[0:rows, t, :])
            for i in range(2):
                turn(b[:, 384 + i * 32:416 + i * 32], pe_rows[:, i * P:(i + 1) * P],
                     pe_to_dve if i == 1 else None)
            from_dve()
            from_act()
            ada_pieces(ADA_AT["start"])

            norm(hT)
            w = use(("in0", 1)).rearrange("p (c n) -> p c n", c=DC)
            for c in range(DC):
                wait_h(c)
            for m in range(LC):
                b = bank_for_dve()
                to_T(b[:, 0:T], w, m * P, P, signal=pe_to_dve)
            release()
            w = use(("in0", 0)).rearrange("p (c n) -> p c n", c=DC)
            for m in range(LC):
                b = bank_for_act()
                to_T(b[:, 0:T], w, m * P, P, signal=pe_to_act)
            release()
            w = use(("in0", 2)).rearrange("p (c n) -> p c n", c=DC)
            for m in range(4):
                b = bank_for_act()
                to_T_halves(b[:, 0:T], (w, w), (m * HD, 256 + m * HD), pe_to_act)
            release()
            w = use(("in0", 3)).rearrange("p (c n) -> p c n", c=DC)
            for m in range(2):
                b = bank_for_dve()
                for g in range(2):
                    o = m * P + g * HD
                    to_T_halves(b[:, g * T:(g + 1) * T], (w, w), (o, o), pe_to_dve if g else None)
            b = bank_for_act()
            to_T(b[:, 0:T], w, 256, P, signal=pe_to_act)
            b = bank_for_act()
            for t in range(NT):
                to_tok(b[:, t * P:(t + 1) * P], w, 384, P, t, signal=pe_to_act if t else None)
            release()
            w = use(("in0", 4))[:, 0:DC * 280].rearrange("p (c n) -> p c n", c=DC)
            b = bank_for_act()
            to_T(b[:, 0:T], w, 0, P, signal=pe_to_act)
            b = bank_for_act()
            for t in range(NT):
                to_tok(b[:, t * P:(t + 1) * P], w, 128, P, t, signal=pe_to_act if t else None)
            b = bank_for_act()
            for t in range(NT):
                to_tok(b[:, t * 24:(t + 1) * 24], w, 256, 24, t, signal=pe_to_act if t else None)
            release()
            wl = use(("lru",))
            wax = wl[:, 0:512].rearrange("p (i a j) -> p i a j", i=2, a=LC)
            for m in range(LC):
                b = bank_for_act()
                from_dve()
                for i in range(2):
                    for h in range(2):
                        lo = h * HD
                        mm(b[lo:lo + HD, i * T:(i + 1) * T], wax[lo:lo + HD, i, m, :],
                           xc[lo:lo + HD, m, :], start=True, stop=True,
                           signal=pe_to_act if i and h else None)
            b = bank_for_act()
            w = use(("cmp",)).rearrange("p (i c n) -> p i c n", i=2, c=CMP_STRIDE)
            for kv in range(2):
                from_dve()
                for c in range(CMP_STRIDE):
                    mm(b[:, kv * 32:kv * 32 + 2 * NBLK], w[:, kv, c, :],
                       ft[kv][:, c].rearrange("p g b -> p (g b)"), start=(c == 0),
                       stop=(c == CMP_STRIDE - 1), signal=pe_to_act if kv and c == CMP_STRIDE - 1 else None)
            w2 = wl[:, 512:640].rearrange("p (i d) -> p i d", i=2)
            from_act()
            b = bank_for_dve()
            for g in range(2):
                mm(b[g * HD:(g + 1) * HD, 0:NBLK], w2[:, 0, :], h1[:, 0, g, :])
            for j in range(4):
                for g in range(2):
                    mm(b[32 * j:32 * j + NBLK, 64 + g * HD:64 + (g + 1) * HD],
                       h1[:, 1, g, :], w2[:, 1, :],
                       signal=pe_to_dve if j == 3 and g else None)
            for _ in range(2):
                release()
            from_dve()
            for t in range(NT):
                for g in range(2):
                    b = bank_for_dve()
                    mm(b[:, 0:P], ident, cmp_mask[:, t, 0:P], start=True, stop=False)
                    for c in range(4):
                        mm(b[:, c * 32:c * 32 + NBLK], q0[g * HD:(g + 1) * HD, c, t * P:(t + 1) * P],
                           kc[g * HD:(g + 1) * HD, 0:NBLK], start=False, stop=True,
                           signal=pe_to_dve if c == 3 else None)
            for t in range(NT):
                b = bank_for_dve()
                from_dve()
                for i in range(2):
                    turn(b[:, i * P:(i + 1) * P],
                         pc[:, t, 4 * i:4 * i + 4, :].rearrange("p a b -> p (a b)"),
                         pe_to_dve if i else None)
            from_dve()
            units = nsa_units()
            bank = [None]

            def S(i, b):
                qt, c, g = units[i]
                nk, lo = (qt + 1) * P, g * HD
                for s, kk in enumerate((ks0, kw0)):
                    mm(b[:, s * nk:(s + 1) * nk], q0[lo:lo + HD, c, qt * P:(qt + 1) * P],
                       kk[lo:lo + HD, 0:nk], start=(s == 0), stop=False)
                for s in range(2):
                    mm(b[:, (s + 1) * nk - P:(s + 1) * nk], ident, causal, start=False, stop=True,
                       signal=scores_ready if s else None)

            def V(i, ptu):
                qt, c, g = units[i]
                lo, nb = g * HD, qt + 1
                if g == 0:
                    bank[0] = bank_for_dve()
                o = bank[0][lo:lo + HD, 0:P]
                h = 4 * g + c
                mm(o, vc[32 * c:32 * c + NBLK, g, :],
                   pcT[32 * c:32 * c + NBLK, g, qt * P:(qt + 1) * P], start=True, stop=False)
                for s, vt in enumerate((vs0, vw0)):
                    for k in range(nb):
                        last = s == 1 and k == nb - 1
                        mm(o, vt[:, k, lo:lo + HD], ptu[:, (s * nb + k) * P:(s * nb + k + 1) * P],
                           start=False, stop=last, signal=pe_to_dve if last and g else None)

            ada_pieces(ADA_AT["lru"])
            attention(len(units), S, V, lambda i: 2 * (units[i][0] + 1), pt, pr, ADA_AT["attention0"])
            mixed()
            out_proj([("out", 0, 0), ("out", 0, 1)], yT)
            settle()
            norm(hT)
            ffn(0, ADA_AT["ffn0"])

            norm(hT)
            ada_pieces(ADA_AT["norm1"])
            for c in range(DC):
                wait_h(c)
            wq = [use(("in1", s)).rearrange("p (c n) -> p c n", c=DC) for s in range(2)]
            for m in range(8):
                b = bank_for_act() if m % 2 else bank_for_dve()
                to_T_halves(b[:, 0:T], wq, (m * HD, m * HD), pe_to_act if m % 2 else pe_to_dve)
            release()
            release()
            w = use(("in1", 2)).rearrange("p (c n) -> p c n", c=DC)
            w3 = use(("in1", 3))[:, 0:DC * 328].rearrange("p (c n) -> p c n", c=DC)
            b = bank_for_act()
            to_T(b[:, 0:T], w, 0, P, signal=pe_to_act)
            b = bank_for_dve()
            for t in range(NT):
                to_tok(b[:, t * P:(t + 1) * P], w, 128, P, t, signal=pe_to_dve if t else None)
            for m in range(4):
                b = bank_for_act() if m % 2 else bank_for_dve()
                sg = pe_to_act if m % 2 else pe_to_dve
                if m < 2:
                    to_T(b[:, 0:T], w, 256 + m * P, P, signal=sg)
                else:
                    to_T(b[:, 0:T], w3, (m - 2) * P, P, signal=sg)
            b = bank_for_dve()
            to_T_halves(b[:, 0:T], (w3, w3), (256, 256), pe_to_dve)
            b = bank_for_dve()
            for t in range(NT):
                to_tok(b[:, t * 8:(t + 1) * 8], w3, 320, 8, t, signal=pe_to_dve if t else None)
            release()
            release()
            barrier()
            for t in range(NT):
                for g in range(2):
                    for mp in range(2):
                        b = bank_for_act()
                        for i in range(2):
                            mm(b[:, i * T:(i + 1) * T],
                               qi[g * HD:(g + 1) * HD, 2 * mp + i, t * P:(t + 1) * P],
                               ki[g * HD:(g + 1) * HD, :], signal=pe_to_act if i else None)
            units1 = dsa_units()
            def S1(i, b):
                qt, cp, g = units1[i]
                nk, lo = (qt + 1) * P, g * HD
                if cp == 0 and g == 0:
                    from_dve()
                for s in range(2):
                    mm(b[:, s * nk:(s + 1) * nk], q1[lo:lo + HD, 2 * cp + s, qt * P:(qt + 1) * P],
                       k1[lo:lo + HD, 0:nk], start=(s == 0), stop=False)
                for s in range(2):
                    mm(b[:, s * nk:(s + 1) * nk], ident, sel[:, qt, 0:nk], start=False, stop=True,
                       signal=scores_ready if s else None)

            def V1(i, ptu):
                qt, cp, g = units1[i]
                nb, lo = qt + 1, g * HD
                if g == 0:
                    bank[0] = bank_for_dve()
                b = bank[0]
                for s in range(2):
                    for k in range(nb):
                        last = k == nb - 1
                        mm(b[lo:lo + HD, s * P:(s + 1) * P], v1[:, k, lo:lo + HD],
                           ptu[:, (s * nb + k) * P:(s * nb + k + 1) * P], start=(k == 0), stop=last,
                           signal=pe_to_dve if last and s and g else None)

            attention(len(units1), S1, V1, lambda i: 2 * (units1[i][0] + 1), pt1, pr1, ADA_AT["attention1"])
            mixed()
            out_proj([("out", 1, 0), ("out", 1, 1)], yT)
            settle()
            norm(hT)
            ffn(1, ADA_AT["ffn1"])
            norm(hT, False)

            def mixers(layer, stream):
                full_ = stream == 1 or layer == 0
                norm(hT)
                for c in range(DC):
                    wait_h(c)
                if full_:
                    w = use(("in2", layer, 1)).rearrange("p (c n) -> p c n", c=DC)
                    for c in range(2):
                        to_T(banks[4][:, c * T:(c + 1) * T], w, 256 + c * P, P)
                w2 = use(("in2", layer, 2))[:, 0:DC * 192].rearrange("p (c n) -> p c n", c=DC)
                to_T_halves(banks[5][:, T:2 * T], (w2, w2), (P, P))
                to_T(banks[5][:, 0:T], w2, 0, P, signal=pe_made_for_act)
                if full_:
                    b = bank_for_dve()
                    for t in range(NT):
                        to_tok(b[:, t * 256:(t + 1) * 256], w, 0, 256, t, signal=pe_to_dve if t else None)
                    release()
                release()
                from_act()
                b = banks[6]
                if full_:
                    for c in range(2):
                        mm(b[:, 0:T], ones[:, :], lsq[:, c, :], start=(c == 0), stop=(c == 1))
                mm(b[:, T:2 * T], ones[:, :], lsq[:, 2, :], signal=pe_made_for_dve)
                if full_:
                    w = use(("in2", layer, 0)).rearrange("p (c n) -> p c n", c=DC)
                    b = bank_for_act()
                    for c in range(2):
                        to_T(b[:, c * T:(c + 1) * T], w, c * P, P, signal=pe_to_act if c else None)
                    b = bank_for_act()
                    for t in range(NT):
                        to_tok(b[:, t * 256:(t + 1) * 256], w, 256, 256, t, signal=pe_to_act if t else None)
                    release()
                wm = use(("mla", layer))
                wuq = wm[:, 0:1536].rearrange("p (c n) -> p c n", c=2)
                wukv = wm[:, 1536:2560].rearrange("p (h w d) -> p h w d", h=MH, w=2)
                wsg = wm[:, 2560:3072].rearrange("p (h q) -> p h q", h=4)
                swap = wm[:, 3072 + 2 * T:3072 + 2 * T + P]
                if full_:
                    b = bank_for_dve()
                    for h in range(4):
                        turn(b[:, h * P:(h + 1) * P], wsg[:, h, :], pe_to_dve if h == 3 else None)
                from_dve()
                for h in range(MH):
                    mm(banks[6 + h % 2][:, h // 2 * T:(h // 2 + 1) * T], wukv[:, h, 0, :], cqT[:, 2, :],
                       signal=pe_made_for_act if h == MH - 1 else None)
                if stream:
                    b = bank_for_dve()
                    mm(b[:, 0:T], swap, krg, signal=pe_to_dve)
                for t in range(NT):
                    b = bank_for_act()
                    mm(b[:, :], cqT[:, 2, t * P:(t + 1) * P], wukv[:, :, 1, :], signal=pe_to_act)
                if full_:
                    for h in range(MH):
                        for c in range(2):
                            mm(banks[4 + h % 2][:, h // 2 * T:(h // 2 + 1) * T],
                               wuq[:, c, h * QKD:h * QKD + NOPE], cqT[:, c, :], start=(c == 0),
                               stop=(c == 1), signal=pe_made_for_act if c and h == MH - 1 else None)
                    b = bank_for_act()
                    for pair in range(2):
                        for c in range(2):
                            for g in range(2):
                                h = 2 * pair + g
                                mm(b[g * HD:(g + 1) * HD, pair * T:(pair + 1) * T],
                                   wuq[:, c, h * QKD + NOPE:(h + 1) * QKD], cqT[:, c, :], start=(c == 0),
                                   stop=(c == 1), signal=pe_to_act if c and h == MH - 1 else None)

                def head_sums(plain, rotated):
                    b = bank_for_dve()
                    for h in range(MH):
                        g, c = h % 2, h // 2
                        mm(b[32 * h:32 * h + 32, 0:T], ones[:, 0:32], plain[:, g, c, :], start=True, stop=False)
                    for h in range(MH):
                        g, c = h % 2, h // 2
                        mm(b[32 * h:32 * h + 32, 0:T], halves[:, 32 * g:32 * g + 32], rotated(c),
                           start=False, stop=True, signal=pe_to_dve if h == MH - 1 else None)

                def spread_keys_rms():
                    from_dve()
                    for g in range(2):
                        b = bank_for_dve()
                        for c in range(2):
                            h = 2 * c + g
                            mm(b[:, c * T:(c + 1) * T], ident[:, 32 * h:32 * h + 1].to_broadcast([P, P]),
                               rk, signal=pe_to_dve if c else None)

                from_act()
                head_sums(ksq, lambda c: lsq[:, 3, :])
                if not full_:
                    spread_keys_rms()
                    release()
                    settle()
                    return
                from_act()
                head_sums(qsq, lambda c: qrsq[:, c, :])
                tb = use(("tab",))
                dftn = tb[:, C_DFTN:C_DFTN + 1024].rearrange("p (t s n) -> p t s n", t=NT, s=2)
                dftd = tb[:, C_DFTD:C_DFTD + 256].rearrange("p (s n) -> p s n", s=2)
                for c in range(2):
                    b = bank_for_dve()
                    for s in range(2):
                        for t in range(NT):
                            mm(b[:, s * T:(s + 1) * T], fq[:, t, c * P:(c + 1) * P], dftn[:, t, s, :],
                               start=(t == 0), stop=(t == 1), signal=pe_to_dve if s and t else None)
                from_dve()
                b = bank_for_dve()
                for t in range(NT):
                    turn(b[:, t * P:(t + 1) * P], rq[:, t * P:(t + 1) * P], pe_to_dve if t else None)
                spread_keys_rms()
                from_dve()
                b = bank_for_dve()
                for c in range(2):
                    for t in range(NT):
                        for g in range(2):
                            h = 2 * c + g
                            mm(b[g * HD:(g + 1) * HD, c * T + t * P:c * T + (t + 1) * P],
                               vg[:, t, h * HD:(h + 1) * HD], wsT[:, h * P:(h + 1) * P],
                               signal=pe_to_dve if c and t and g else None)
                if stream:
                    b = bank_for_dve()
                    mm(b[:, :], swap, qraw.rearrange("p c t -> p (c t)"), signal=pe_to_dve)
                from_dve()
                for c in range(2):
                    b = bank_for_dve()
                    for s in range(2):
                        mm(b[:, 0:T], dftd[:, s, :], acs[:, s, c, :], start=(s == 0), stop=(s == 1),
                           signal=pe_to_dve if s else None)
                nk = 2 * T if stream else T
                units2 = mla_units()

                def S2(i, b):
                    qt, h = units2[i]
                    c, lo = h // 2, h % 2 * HD
                    mm(b[:, 0:nk], qTn[:, h, qt * P:(qt + 1) * P], kTn[:, h, 0:nk], start=True, stop=False)
                    mm(b[:, 0:nk], qTr[lo:lo + HD, c, qt * P:(qt + 1) * P], kTr[lo:lo + HD, c, 0:nk],
                       start=False, stop=True, signal=scores_ready)

                def V2(i, ptu):
                    qt, h = units2[i]
                    b = bank_for_dve()
                    nb = nk // P
                    for k in range(nb):
                        mm(b[:, 0:P], vv[:, k, h * P:(h + 1) * P], ptu[:, k * P:(k + 1) * P],
                           start=(k == 0), stop=(k == nb - 1), signal=pe_to_dve if k == nb - 1 else None)

                from_dve()
                release()
                release()
                attention(len(units2), S2, V2, lambda i: nk // P, pt2, pr2)
                mixed()
                out_proj([("out2", layer, 0), ("out2", layer, 1)], yT)
                settle()

            def route(layer, stream):
                norm(mhT)
                for c in range(DC):
                    wait_h(c)
                pe.wait_ge(row_loads, 32)
                wr = v3(wrt, layer * P, DC, NE)
                b = bank_for_dve()
                for t in range(NT):
                    to_tok(b[:, t * NE:(t + 1) * NE], wr, 0, NE, t, h=mhT, signal=pe_to_dve if t else None)
                for t in range(NT):
                    for half in range(2):
                        b = bank_for_act()
                        for c in range(4):
                            turn(b[:, c * P:(c + 1) * P], mxn[:, half * 4 + c, t * P:(t + 1) * P],
                                 pe_to_act if c == 3 else None)
                from_dve()
                b = bank_for_dve()
                for t in range(NT):
                    turn(b[0:NE, t * P:(t + 1) * P], small[:, 128 + t * NE:128 + (t + 1) * NE],
                         pe_to_dve if t else None)
                from_dve()
                b = bank_for_dve()
                for t in range(NT):
                    turn(b[:, t * NE:(t + 1) * NE], exs[2][:, t * P:(t + 1) * P],
                         pe_to_dve if t else None)
                from_dve()
                from_act()
                for c in range(DC):
                    b = bank_for_act() if c % 2 else bank_for_dve()
                    for t in range(NT):
                        mm(b[:, :], xtok[:, t, c * P:(c + 1) * P], pm[:, t, :], start=(t == 0),
                           stop=(t == 1), signal=(pe_to_act if c % 2 else pe_to_dve) if t else None)
                for half in range(2):
                    b = bank_for_dve()
                    for g in range(2):
                        for t in range(NT):
                            turn(b[:, g * T + t * P:g * T + (t + 1) * P],
                                 pg[:, t, (half * 2 + g) * P:(half * 2 + g + 1) * P],
                                 pe_to_dve if g and t else None)
                barrier()

            def experts(layer, streams):
                k0 = n["piece"]
                ns = len(streams)
                assert pieces[k0][0] == "moe"
                per = 12
                gain = [sum(16 * GE for m in range(per) if (k0 + m) % SLOTS == s) for s in range(SLOTS)]
                base = NG * layer
                base_s = 2 * NG * layer
                with pe.Fori(0, NG) as g:
                    def piece(m):
                        k = k0 + m
                        pe.wait_ge(slot_loaded[k % SLOTS], g * gain[k % SLOTS] + landed[k])
                        return slot(k)
                    pe.wait_ge(xs_ready, g + (base + 1))
                    for kind in range(2):
                        for s4 in range(4):
                            w = piece(kind * 4 + s4).rearrange("p (e s n) -> p e s n", e=GE, s=2)
                            for c2 in range(2):
                                c = 2 * s4 + c2
                                for i, s in enumerate(streams):
                                    b = banks[2 * s + kind]
                                    for j in range(GE):
                                        lastp = c2 == 1 and i == ns - 1 and j == GE - 1
                                        ins = nc.tensor.matmul(
                                            b[32 * j:32 * j + 32, :], xs[s][:, c, 32 * j:32 * j + 32],
                                            w[:, j, c2, :], start=(c == 0), stop=(c == DC - 1),
                                            skip_group_check=True)
                                        if lastp:
                                            ins.then_inc(slots_released, 1)
                    pe.drain().then_inc(gu_done, 1)
                    for i, s in enumerate(streams):
                        pe.wait_ge(hid_ready, g * ns + (base_s + i + 1))
                        for f in range(4):
                            ins = nc.tensor.transpose(banks[2 * s][:, f * P:(f + 1) * P],
                                                      hid[s][:, f * P:(f + 1) * P], ident)
                        ins.then_inc(hid_turned, 1)
                    pe.wait_ge(y_read, g + (base + 1))
                    for f in range(4):
                        w = piece(8 + f).rearrange("p (e n) -> p e n", e=GE)
                        for i, s in enumerate(streams):
                            if f == 0:
                                pe.wait_ge(hid_copied, g * ns + (base_s + i + 1))
                            for half in range(2):
                                for j in range(GE):
                                    lastp = half == 1 and i == ns - 1 and j == GE - 1
                                    ins = nc.tensor.matmul(
                                        banks[4 + 2 * s + half][32 * j:32 * j + 32, :],
                                        hidT[s][:, f, 32 * j:32 * j + 32],
                                        w[:, j, half * 512:(half + 1) * 512], start=(f == 0),
                                        stop=(f == 3), skip_group_check=True)
                                    if lastp:
                                        ins.then_inc(slots_released, 1)
                    pe.drain().then_inc(y_ready, 1)
                n["piece"] += per * NG
                barrier()
                for s in streams:
                    if s != streams[0]:
                        barrier()
                    for g in range(NG):
                        accumulate(4, ys[s][:, g, :], pgT[s][:, g, :], g == 0, g == NG - 1)
                barrier()

            for layer in range(LAYERS):
                mixers(layer, 0)
                mixers(layer, 1)
                for s in ((0, 1) if layer == 0 else (1,)):
                    route(layer, s)
                experts(layer, (0, 1) if layer == 0 else (1,))
            for c in range(DC):
                b = banks[c // 2]
                for t in range(NT):
                    turn(b[:, (c % 2) * T + t * P:(c % 2) * T + (t + 1) * P],
                         xT[:, c, t * P:(t + 1) * P], pe_to_dve if c % 2 and t else None)

        @block.scalar
        def _(act):
            n = {"act": 0, "phase": 0, "ln": 0, "chain": 0, "gu": 0, "unit": 0, "from_dve": 0,
                 "x": 0, "xn": 0, "ada": 0, "from_pe": 0}

            def barrier():
                n["phase"] += 1
                act.drain().then_inc(act_phase, 1)
                act.wait_ge(pe_phase, n["phase"])
                act.wait_ge(dve_phase, n["phase"])

            def link(ins):
                n["chain"] += 1
                ins.then_inc(act_chain, 1)
                act.wait_ge(act_chain, n["chain"])

            def job():
                k = n["act"]
                n["act"] += 1
                act.wait_ge(pe_to_act, k + 1)
                return banks[2 + k % 2]

            def from_dve():
                n["from_dve"] += 1
                act.wait_ge(dve_made_for_act, n["from_dve"])

            def preload(function):
                nc.scalar.activation(small[:, 118:119], ones[:, 0:1], function)

            def norm(src, dst, xn_, B, std_, sq, chunks=True, scale=None):
                k = n["ln"]
                n["ln"] += 1
                for c in range(DC):
                    if chunks:
                        n["x"] += 1
                        act.wait_ge(x_ready, n["x"])
                    nc.scalar.activation(sq[:, c, :], src[:, c, :], ACT.Square).then_inc(squares_ready, 1)
                preload(ACT.Sqrt)
                act.wait_ge(var_ready, k + 1)
                nc.scalar.activation(std_, std_, ACT.Sqrt).then_inc(std_ready, 1)
                for c in range(DC if B else 0):
                    n["xn"] += 1
                    act.wait_ge(xn_ready, n["xn"])
                    nc.scalar.activation(dst[:, c, :], xn_[:, c, :], ACT.Identity, bias=B(c),
                                         scale=scale(c) if scale else 1.0).then_inc(h_ready, 1)

            def ada_pieces(count):
                for _ in range(count):
                    k = n["ada"]
                    n["ada"] += 1
                    act.wait_ge(ada_rows, k + 1)
                    if k >= 2:
                        act.wait_ge(ada_cols, k - 1)
                    nc.scalar.copy(brow[:, (k % 2) * 512:(k % 2 + 1) * 512], banks[2][:, :])\
                        .then_inc(ada_copied, 1)

            def ffn(extra):
                at = ada_after(extra)
                preload(ACT.Silu)
                for f in range(FC):
                    k = n["gu"]
                    n["gu"] += 1
                    act.wait_ge(gu_ready, k + 1)
                    if f >= 2:
                        act.wait_ge(act_ready, k - 1)
                    nc.scalar.activation(sil[:, k % 2, :], banks[k % 2][:, 0:T], ACT.Silu)\
                        .then_inc(silu_ready, 1)
                    ada_pieces(at.get(f, 0))

            def attention(N, segs, pr_, pt_, scale, nb_of, sums, negs, fill=0):
                u0 = n["unit"]
                scale_of = scale if callable(scale) else lambda i: scale
                preload(ACT.Exp)
                for i in range(N + 2):
                    if i >= 2:
                        u = u0 + i - 2
                        nb = nb_of(i - 2)
                        act.wait_ge(turned, u + 1)
                        nc.scalar.copy(pt_[:, u % 2, 0:nb * P], banks[6 + u % 2][:, 0:nb * P])\
                            .then_inc(turned_copied, 1)
                    if i < N:
                        u = u0 + i
                        nb = nb_of(i)
                        nk = nb * P // segs
                        act.wait_ge(negmax_ready, u + 1)
                        for s in range(segs):
                            ins = nc.scalar.activation(
                                pr_[:, u % 2, s * nk:(s + 1) * nk], banks[4 + u % 2][:, s * nk:(s + 1) * nk],
                                ACT.Exp, bias=negs[:, (u % 2) * 2 + s:(u % 2) * 2 + s + 1],
                                scale=scale_of(i),
                                accum_out=sums[:, (u % 2) * 2 + s:(u % 2) * 2 + s + 1])
                        ins.then_inc(exp_done, 1)
                    if i % 2 == 1 and i // 2 < fill:
                        ada_pieces(1)
                n["unit"] += N

            negs, sums = small[:, 84:88], small[:, 88:92]
            rqs = small[:, 120:128]

            from_dve()
            for i, name in enumerate(("c", "c_2", "c_ctx_2")):
                ins = nc.scalar.activation(csil[:, :, i], vec(name, 0, 8), ACT.Silu)
            ins.then_inc(act_made_for_pe, 1)
            link(nc.scalar.activation(lam[:, 0:4], vec("l0_lru_lambda", 0, 4), ACT.Abs))
            link(nc.scalar.activation(lam[:, 4:8], lam[:, 0:4], ACT.Exp, scale=-1.0))
            nc.scalar.activation(lam[:, 8:12], lam[:, 4:8], ACT.Ln, bias=1.0).then_inc(act_made_for_dve, 1)
            ada_pieces(len(ADA_AT["start"]))

            from_dve()
            norm(xT, hT, xn, lambda c: mod(0, 0, c), std, hT, False)
            for m in range(LC):
                b = job()
                nc.scalar.activation(gg[:, m, :], b[:, 0:T], ACT.Gelu_apprx_tanh).then_inc(act_read, 1)
            for m in range(4):
                b = job()
                nc.scalar.copy(q0[:, m, :], b[:, 0:T]).then_inc(act_read, 1)
            b = job()
            nc.scalar.copy(ks0, b[:, 0:T]).then_inc(act_read, 1)
            b = job()
            nc.scalar.copy(vs0, b[:, 0:T].rearrange("p (a b) -> p a b", a=2)).then_inc(act_read, 1)
            b = job()
            nc.scalar.copy(kw0, b[:, 0:T]).then_inc(act_read, 1)
            b = job()
            nc.scalar.copy(vw0, b[:, 0:T].rearrange("p (a b) -> p a b", a=2)).then_inc(act_read, 1)
            b = job()
            nc.scalar.activation(gts.rearrange("p t h k -> p (t h k)"), b[:, 0:48], ACT.Sigmoid)\
                .then_inc(act_read, 1)
            for m in range(LC):
                b = job()
                nc.scalar.activation(rr[:, m, :], b[:, 0:T], ACT.Sigmoid, bias=vec("l0_lru_ba", m))
                nc.scalar.activation(ii[:, m, :], b[:, T:2 * T], ACT.Sigmoid, bias=vec("l0_lru_bx", m))\
                    .then_inc(act_read, 1)
            act.wait_ge(act_read, n["act"])
            for m in range(LC):
                nc.scalar.activation(aa[:, m, :], rr[:, m, :], ACT.Exp, scale=lam[:, 12 + m:13 + m])
                ins = nc.scalar.activation(th[:, m, :], rr[:, m, :], ACT.Tanh, scale=lam[:, 16 + m:17 + m])
            ins.then_inc(act_made_for_dve, 1)
            b = job()
            for kv in range(2):
                ins = nc.scalar.activation(h1[:, kv], b[:, kv * 32:kv * 32 + 2 * NBLK].rearrange(
                    "p (g b) -> p g b", g=2), ACT.Gelu_apprx_tanh)
            ins.then_inc(act_read, 1)
            act.drain().then_inc(act_made_for_pe, 1)
            from_dve()
            nc.scalar.activation(th, th, ACT.Sqrt).then_inc(act_made_for_dve, 1)
            for t in range(NT):
                from_dve()
                nc.scalar.activation(pc[:, t], pc[:, t], ACT.Exp, scale=HD ** -0.5).then_inc(act_made_for_dve, 1)
            units = nsa_units()
            ada_pieces(len(ADA_AT["lru"]))
            attention(len(units), 2, pr, pt, HD ** -0.5, lambda i: 2 * (units[i][0] + 1), sums, negs,
                      len(ADA_AT["attention0"]))
            norm(xT, hT, xn, lambda c: mod(0, 3, c), std, hT)
            ffn(ADA_AT["ffn0"])

            norm(xT, hT, xn, lambda c: mod(1, 0, c), std, hT)
            ada_pieces(len(ADA_AT["norm1"]))
            for m in range(1, 8, 2):
                b = job()
                nc.scalar.copy(q1[:, m, :], b[:, 0:T]).then_inc(act_read, 1)
            b = job()
            nc.scalar.copy(k1, b[:, 0:T]).then_inc(act_read, 1)
            for m in (1, 3):
                b = job()
                nc.scalar.copy(qi[:, m, :], b[:, 0:T]).then_inc(act_read, 1)
            barrier()
            for t in range(NT):
                for m in range(4):
                    b = job()
                    k = t * 4 + m
                    if k >= 2:
                        act.wait_ge(index_added, 2 * (k - 1))
                    nc.scalar.activation(rel[:, k % 2, :], b[:, :], ACT.Relu, scale=HD ** -0.5)\
                        .then_inc(act_read, 1)
                    act.drain().then_inc(act_made_for_dve, 1)
            units1 = dsa_units()
            attention(len(units1), 2, pr1, pt1, HD ** -0.5, lambda i: 2 * (units1[i][0] + 1), sums, negs,
                      len(ADA_AT["attention1"]))
            norm(xT, hT, xn, lambda c: mod(1, 3, c), std, hT)
            ffn(ADA_AT["ffn1"])
            norm(xT, xT, xn, None, std, hT)

            def mixers(layer, stream):
                full_ = stream == 1 or layer == 0
                src = xT if stream else cT
                cond = 0 if stream else 1

                def from_pe():
                    n["from_pe"] += 1
                    act.wait_ge(pe_made_for_act, n["from_pe"])

                from_dve()
                norm(src, hT, xn, lambda c: mod(2 + layer, 0, c, 1, cond), std, hT, False)
                from_pe()
                for k in range(2):
                    if full_ or k == 1:
                        nc.scalar.activation(lsq[:, 2 * k:2 * k + 2, :], banks[4 + k][:, :].rearrange(
                            "p (c t) -> p c t", c=2), ACT.Square)
                act.drain().then_inc(act_made_for_pe, 1)
                from_dve()
                nc.scalar.activation(lrs, lrs, ACT.Sqrt).then_inc(act_made_for_dve, 1)
                ms = small[:, 112:114]
                if full_:
                    b = job()
                    nc.scalar.activation(uT, b[:, :].rearrange("p (c t) -> p c t", c=2),
                                         ACT.Gelu_apprx_tanh).then_inc(act_read, 1)
                    b = job()
                    nc.scalar.activation(vg, b[:, :].rearrange("p (c t) -> p c t", c=2),
                                         ACT.Gelu_apprx_tanh).then_inc(act_read, 1)
                    act.wait_ge(act_read, n["act"])
                    for t in range(NT):
                        nc.scalar.activation(qsq[:, 0, t, :], vg[:, t, :], ACT.Square,
                                             accum_out=ms[:, t:t + 1])
                    act.drain().then_inc(act_made_for_dve, 1)
                from_pe()
                for g in range(2):
                    b = banks[6 + g][:, :].rearrange("p (c t) -> p c t", c=2)
                    nc.scalar.activation(ksq[:, g], b, ACT.Square)
                    nc.scalar.activation(kTn[:, g::2, T * stream:T * stream + T], b, ACT.Identity,
                                         scale=vec("k_nope", layer))
                act.drain().then_inc(act_made_for_pe, 1)
                for t in range(NT):
                    b = job()
                    nc.scalar.copy(vv[:, 2 * stream + t, :], b[:, :]).then_inc(act_read, 1)
                if full_:
                    from_pe()
                    for g in range(2):
                        b = banks[4 + g][:, :].rearrange("p (c t) -> p c t", c=2)
                        nc.scalar.activation(qsq[:, g], b, ACT.Square)
                        nc.scalar.activation(qTn[:, g::2, :], b, ACT.Identity, scale=vec("q_nope", layer))
                    b = job()
                    b = b[:, :].rearrange("p (c t) -> p c t", c=2)
                    nc.scalar.activation(qrsq, b, ACT.Square)
                    nc.scalar.activation(qraw if stream else qTr, b, ACT.Identity,
                                         scale=vec("q_rope", layer)).then_inc(act_read, 1)
                    act.drain().then_inc(act_made_for_pe, 1)
                from_dve()
                if full_:
                    nc.scalar.activation(ms, ms, ACT.Sqrt)
                nc.scalar.activation(rk, rk, ACT.Sqrt)
                act.drain().then_inc(act_made_for_dve, 1)
                if full_:
                    from_dve()
                    nc.scalar.activation(rqs, rqs, ACT.Sqrt).then_inc(act_made_for_dve, 1)
                    units2 = mla_units()
                    nk = 2 * T if stream else T
                    attention(len(units2), 1, pr2, pt2, lambda i: rqs[:, i:i + 1], lambda i: nk // P, sums,
                              negs)

            def route(layer, stream):
                src = xT if stream else cT
                cond = 0 if stream else 1
                from_dve()
                norm(src, mhT, mxn, lambda c: mod(2 + layer, 3, c, 1, cond), mstd, mhT, False,
                     lambda c: ac(8, c))
                for t in range(NT):
                    for half in range(2):
                        b = job()
                        nc.scalar.copy(xtok[:, t, half * 512:(half + 1) * 512], b[:, :]).then_inc(act_read, 1)
                act.drain().then_inc(act_made_for_pe, 1)
                from_dve()
                nc.scalar.activation(small[:, 128:128 + NT * NE], small[:, 128:128 + NT * NE], ACT.Exp)\
                    .then_inc(act_made_for_dve, 1)
                for c in range(1, DC, 2):
                    b = job()
                    nc.scalar.activation(xsT[stream][:, c, :], b[:, :], ACT.Identity, scale=ac(8, c),
                                         bias=mod(2 + layer, 3, c, 1, cond)).then_inc(act_read, 1)
                barrier()

            def experts(layer, streams):
                ns = len(streams)
                base = NG * layer
                base_s = 2 * NG * layer
                with act.Fori(0, NG) as g:
                    for i, s in enumerate(streams):
                        ins = nc.scalar.copy(xs[s], xsT[s][:, :, bass.ts(g, P)])
                    ins.then_inc(xs_ready, 1)
                    act.wait_ge(gu_done, g + (base + 1))
                    for i, s in enumerate(streams):
                        ins = nc.scalar.activation(hid[s], banks[2 * s][:, :], ACT.Silu)
                        ins.then_inc(hid_silu, 1)
                    for i, s in enumerate(streams):
                        act.wait_ge(hid_turned, g * ns + (base_s + i + 1))
                        nc.scalar.copy(hidT[s], banks[2 * s][:, :].rearrange("p (a b) -> p a b", a=4))\
                            .then_inc(hid_copied, 1)
                barrier()
                for s in streams[1:]:
                    barrier()
                barrier()

            for layer in range(LAYERS):
                mixers(layer, 0)
                mixers(layer, 1)
                for s in ((0, 1) if layer == 0 else (1,)):
                    route(layer, s)
                experts(layer, (0, 1) if layer == 0 else (1,))

        @block.vector
        def _(dve):
            n = {"dve": 0, "phase": 0, "ln": 0, "chain": 0, "gu": 0, "unit": 0, "from_act": 0, "acc": 0,
                 "ada": 0, "index": 0, "from_pe": 0}

            def barrier():
                n["phase"] += 1
                dve.drain().then_inc(dve_phase, 1)
                dve.wait_ge(pe_phase, n["phase"])
                dve.wait_ge(act_phase, n["phase"])

            def link(ins):
                n["chain"] += 1
                ins.then_inc(dve_chain, 1)
                dve.wait_ge(dve_chain, n["chain"])

            def job():
                k = n["dve"]
                n["dve"] += 1
                dve.wait_ge(pe_to_dve, k + 1)
                return banks[k % 2]

            def from_act():
                n["from_act"] += 1
                dve.wait_ge(act_made_for_dve, n["from_act"])

            tt, ts_, stt = nc.vector.tensor_tensor, nc.vector.tensor_scalar, nc.vector.scalar_tensor_tensor

            def bc(ap, axis, shape):
                return ap.unsqueeze(axis).to_broadcast(shape)

            def norm(src, dst, xn_, std_, A_=None):
                k = n["ln"]
                n["ln"] += 1
                b = job()
                ts_(std_, b[:, 0:T], 1.0 / D, EPS, ALU.mult, ALU.add).then_inc(var_ready, 1)
                dve.wait_ge(std_ready, k + 1)
                nc.vector.reciprocal(std_, std_).then_inc(dve_read, 1)
                dve.wait_ge(dve_read, n["dve"])
                for c in range(DC):
                    if A_ is None:
                        ins = tt(xn_[:, c, :], src[:, c, :], std_, ALU.mult)
                    else:
                        ins = stt(xn_[:, c, :], src[:, c, :], A_(c), std_, ALU.mult, ALU.mult)
                    if dst is not None:
                        ins.then_inc(xn_ready, 1)

            def residual(dst, gate, normed=True):
                for c in range(DC):
                    if c % 2 == 0:
                        n["acc"] += 1
                        dve.wait_ge(acc_ready, n["acc"])
                    ins = stt(dst[:, c, :], banks[4 + c // 2][:, (c % 2) * T:(c % 2 + 1) * T], gate(c),
                              dst[:, c, :], ALU.mult, ALU.add)
                    if normed:
                        ins.then_inc(x_ready, 1)

            def ada_pieces(keys):
                for _, matrix, s in keys:
                    n["ada"] += 1
                    dve.wait_ge(ada_cols, n["ada"])
                    if matrix < 2:
                        src, dst = banks[3][:, 0:4], mods[:, MODO[matrix] + 4 * s:MODO[matrix] + 4 * s + 4]
                        bias = vec(f"l{matrix}_mod_b", 4 * s, 4)
                    else:
                        src = banks[3][:, 0:8].rearrange("p (a b) -> p a b", b=2)
                        o = MODO[matrix] + 8 * s
                        dst = mods[:, o:o + 8].rearrange("p (a b) -> p a b", b=2)
                        bias = bc(vec("b_ada_2", (matrix - 2) * 48 + 4 * s, 4), 2, [P, 4, 2])
                    tt(dst, src, bias, ALU.add).then_inc(ada_read, 1)
                dve.wait_ge(ada_read, n["ada"])

            def scale_cols(i, matrix, seg, cond=0, gain=None):
                s = mod(matrix, seg, 0, 8, cond)
                if gain is None:
                    return ts_(ac(i, 0, 8), s, 1.0, None, ALU.add)
                return stt(ac(i, 0, 8), s, 1.0, vec(gain, 0, 8), ALU.add, ALU.mult)

            def ffn(extra):
                at, done = ada_after(extra), 0
                for f in range(FC):
                    k = n["gu"]
                    n["gu"] += 1
                    dve.wait_ge(silu_ready, k + 1)
                    tt(actT[:, f % 4, :], sil[:, k % 2, :], banks[k % 2][:, T:2 * T], ALU.mult)\
                        .then_inc(act_ready, 1)
                    if f in at:
                        upto = done + at[f]
                        end = upto if f == FC - 1 else upto - 1
                        ada_pieces(extra[n_ada[0]:end])
                        n_ada[0] = end
                        done = upto
                n_ada[0] = 0

            n_ada = [0]

            def attention(N, segs, pr_, scale, nb_of, sums, negs, gate, V, every, fill=()):
                u0 = n["unit"]
                rs = small[:, 94:98]
                for i in range(N + 3):
                    if i < N:
                        u = u0 + i
                        nk = nb_of(i) * P // segs
                        dve.wait_ge(scores_ready, u + 1)
                        ng = negs[:, (u % 2) * 2:(u % 2) * 2 + segs]
                        link(nc.vector.tensor_reduce(
                            ng, banks[4 + u % 2][:, 0:segs * nk].rearrange("p (s k) -> p s k", s=segs),
                            X, ALU.max))
                        if callable(scale):
                            ts_(ng, ng, scale(i), None, ALU.mult).then_inc(negmax_ready, 1)
                        else:
                            ts_(ng, ng, FLOOR, -scale, ALU.max, ALU.mult).then_inc(negmax_ready, 1)
                    if 1 <= i <= N:
                        u = u0 + i - 1
                        nk = nb_of(i - 1) * P // segs
                        dve.wait_ge(exp_done, u + 1)
                        sm = sums[:, (u % 2) * 2:(u % 2) * 2 + segs]
                        r = rs[:, (u % 2) * 2:(u % 2) * 2 + segs]
                        link(ts_(r, sm, 1e-30, None, ALU.max))
                        link(nc.vector.reciprocal(r, r))
                        if gate is not None:
                            link(tt(r, r, gate(i - 1), ALU.mult))
                        for s in range(segs):
                            p_ = pr_[:, u % 2, s * nk:(s + 1) * nk]
                            ins = ts_(p_, p_, r[:, s:s + 1], None, ALU.mult)
                        ins.then_inc(probs_ready, 1)
                    if i >= 3 and (i - 3) % every == every - 1:
                        b = job()
                        V(i - 3, b)
                    if fill and i % 2 == 1 and 1 <= i // 2 < len(fill):
                        ada_pieces([fill[i // 2 - 1]])
                        if i // 2 == len(fill) - 1:
                            ada_pieces([fill[-1]])
                n["unit"] += N

            negs, sums = small[:, 84:88], small[:, 88:92]
            rqs, neg_rqs = small[:, 120:128], small[:, 100:108]

            nc.vector.memset(halves[0:HD, 0:32], 1.0)
            nc.vector.memset(halves[0:HD, 32:64], 0.0)
            nc.vector.memset(halves[HD:P, 0:32], 0.0)
            nc.vector.memset(halves[HD:P, 32:64], 1.0)
            nc.vector.memset(csil_[:, :], 0.0)
            nc.vector.memset(ones[:, :], 1.0)
            dve.wait_ge(stream_loads, 48)
            nc.vector.tensor_reduce(selector[:, 0:3], ident.rearrange("p (j i) -> p i j", j=4)[:, 0:3, :],
                                    X, ALU.add)
            dve.drain().then_inc(dve_made_for_pe, 1)
            for dst in (xT, cT):
                for c in range(0, DC, 2):
                    b = job()
                    nc.vector.tensor_copy(dst[:, c:c + 2, :], b[:, :].rearrange("p (a b) -> p a b", a=2))\
                        .then_inc(dve_read, 1)
            b = job()
            for t in range(3):
                rows = third_rows if t == 2 else sum(VEC_ROWS[m] for m in VEC_NAMES[t])
                nc.vector.tensor_copy(vecs[:, t * P:t * P + rows], b[:, t * P:t * P + rows])
            nc.vector.tensor_copy(peT, b[:, 384:448]).then_inc(dve_read, 1)
            dve.drain().then_inc(dve_made_for_act, 1)
            from_act()
            link(ts_(lam[:, 12:16], vec("l0_lru_lambda", 0, 4), -1.0, 0.0, ALU.mult, ALU.max))
            e_, l_, s_ = lam[:, 4:8], lam[:, 8:12], lam[:, 12:16]
            w1, w2, w3 = small[:, 100:104], small[:, 104:108], small[:, 108:112]
            link(ts_(w1, e_, 1.0, None, ALU.add))
            link(ts_(w1, w1, 1.0, None, ALU.subtract))
            link(ts_(w2, w1, 0.0, None, ALU.is_equal))
            link(tt(w1, w1, w2, ALU.add))
            link(nc.vector.reciprocal(w1, w1))
            link(tt(w1, w1, e_, ALU.mult))
            link(tt(w1, w1, l_, ALU.mult))
            link(tt(w3, w2, e_, ALU.mult))
            link(tt(w1, w1, w3, ALU.add))
            link(tt(s_, s_, w1, ALU.add))
            link(ts_(lam[:, 16:20], s_, 8.0, None, ALU.mult))
            link(ts_(s_, s_, -8.0, None, ALU.mult))
            ada_pieces(ADA_AT["start"])
            link(scale_cols(0, 0, 1, gain="l0_norm_mix"))
            dve.drain().then_inc(dve_made_for_act, 1)

            norm(xT, hT, xn, std, lambda c: ac(0, c))
            link(nc.vector.memset(axp[:, :, 0:3], 0.0))
            for m in range(LC):
                b = job()
                nc.vector.tensor_copy(axp[:, m, 3:], b[:, 0:T]).then_inc(dve_read, 1)
                dve.wait_ge(dve_read, n["dve"])
                link(ts_(xc[:, m, :], axp[:, m, 0:T], vec("l0_conv_w", m), vec("l0_conv_b", m),
                         ALU.mult, ALU.add))
                for k in range(1, 4):
                    ins = stt(xc[:, m, :], axp[:, m, k:k + T], vec("l0_conv_w", 4 * k + m), xc[:, m, :],
                              ALU.mult, ALU.add)
                    if k < 3:
                        link(ins)
                ins.then_inc(dve_made_for_pe, 1)
            for kv in range(2):
                b = job()
                src = b[:, :].rearrange("p (g b l) -> p g l b", g=2, l=CMP_STRIDE)
                for odd in range(2):
                    lo = slice(odd * HD, (odd + 1) * HD)
                    for g in range(2):
                        for hf in range(2):
                            pos = peT[lo, kv * 32 + hf * 16 + odd:kv * 32 + hf * 16 + 16:2]
                            ins = tt(ft[kv][lo, 8 * hf:8 * hf + 8, g, :], src[lo, g, odd::2, hf:hf + NBLK],
                                     bc(pos, 2, [HD, 8, NBLK]), ALU.add)
                ins.then_inc(dve_read, 1)
                dve.drain().then_inc(dve_made_for_pe, 1)
            from_act()
            link(tt(rr, aa, aa, ALU.mult))
            stt(th, rr, 1.0, th, ALU.add, ALU.mult).then_inc(dve_made_for_act, 1)
            b = job()
            nc.vector.tensor_copy(kc[:, 0:NBLK], b[:, 0:NBLK])
            for j in range(4):
                ins = nc.vector.tensor_copy(vc[32 * j:32 * j + NBLK],
                                            b[32 * j:32 * j + NBLK, 64:192].rearrange("p (g d) -> p g d", g=2))
            ins.then_inc(dve_read, 1)
            dve.drain().then_inc(dve_made_for_pe, 1)
            from_act()
            nc.vector.memset(th[:, :, 0:1], 1.0)
            link(tt(ii, ii, xc, ALU.mult))
            dve.drain().then_inc(dve_chain, 1)
            n["chain"] += 1
            dve.wait_ge(dve_chain, n["chain"])
            link(tt(ii, ii, th, ALU.mult))
            for m in range(LC):
                ins = nc.vector.tensor_tensor_scan(xc[:, m, :], aa[:, m, :], ii[:, m, :], 0.0,
                                                   ALU.mult, ALU.add)
                link(ins)
            link(tt(yT[:, 0:4, :], xc, gg, ALU.mult))
            mx, sm8 = small[:, 100:108], small[:, 108:116]
            for t in range(NT):
                for g in range(2):
                    b = job()
                    s3 = b[:, 0:P].rearrange("p (h k) -> p h k", h=4)
                    mg = mx[:, 4 * g:4 * g + 4]
                    link(nc.vector.tensor_reduce(mg, s3, X, ALU.max))
                    link(ts_(mg, mg, FLOOR, None, ALU.max))
                    tt(pc[:, t, 4 * g:4 * g + 4, :], s3, bc(mg, 2, [P, 4, 32]), ALU.subtract)\
                        .then_inc(dve_read, 1)
                dve.drain().then_inc(dve_made_for_act, 1)
                from_act()
                link(nc.vector.tensor_reduce(sm8, pc[:, t], X, ALU.add))
                link(ts_(sm8, sm8, 1e-30, None, ALU.max))
                link(nc.vector.reciprocal(sm8, sm8))
                link(tt(sm8, sm8, gts[:, t, :, 0], ALU.mult))
                tt(pc[:, t], pc[:, t], bc(sm8, 2, [P, 8, 32]), ALU.mult).then_inc(dve_made_for_pe, 1)
            for t in range(NT):
                b = job()
                nc.vector.tensor_copy(pcT[:, :, t * P:(t + 1) * P],
                                      b[:, 0:256].rearrange("p (a b) -> p a b", a=2)).then_inc(dve_read, 1)
            dve.drain().then_inc(dve_made_for_pe, 1)
            units = nsa_units()

            def V0(i, b):
                qt, c, g = units[i]
                nc.vector.tensor_copy(yT[:, 4 + c, qt * P:(qt + 1) * P], b[:, 0:P]).then_inc(dve_read, 1)

            def gate0(i):
                qt, c, g = units[i]
                return gts[:, qt, 4 * g + c, 1:3]

            ada_pieces(ADA_AT["lru"])
            attention(len(units), 2, pr, HD ** -0.5, lambda i: 2 * (units[i][0] + 1), sums, negs, gate0,
                      V0, 2, ADA_AT["attention0"])
            link(scale_cols(1, 0, 4, gain="l0_norm_ffn"))
            residual(xT, lambda c: mod(0, 2, c))
            norm(xT, hT, xn, std, lambda c: ac(1, c))
            ffn(ADA_AT["ffn0"])
            link(scale_cols(2, 1, 1, gain="l1_norm_mix"))
            link(scale_cols(3, 1, 4, gain="l1_norm_ffn"))
            residual(xT, lambda c: mod(0, 5, c))

            norm(xT, hT, xn, std, lambda c: ac(2, c))
            ada_pieces(ADA_AT["norm1"])
            for m in range(0, 8, 2):
                b = job()
                nc.vector.tensor_copy(q1[:, m, :], b[:, 0:T]).then_inc(dve_read, 1)
            b = job()
            nc.vector.tensor_copy(v1, b[:, 0:T].rearrange("p (a b) -> p a b", a=2)).then_inc(dve_read, 1)
            for m in (0, 2):
                b = job()
                nc.vector.tensor_copy(qi[:, m, :], b[:, 0:T]).then_inc(dve_read, 1)
            b = job()
            nc.vector.tensor_copy(ki, b[:, 0:T]).then_inc(dve_read, 1)
            b = job()
            ts_(wi.rearrange("p t h -> p (t h)"), b[:, 0:16], IDX_HEADS ** -0.5, None, ALU.mult)\
                .then_inc(dve_read, 1)
            barrier()
            for t in range(NT):
                for m in range(4):
                    k = t * 4 + m
                    from_act()
                    for i in range(2):
                        g, mp = m // 2, m % 2
                        h = 4 * mp + 2 * i + g
                        r = rel[:, k % 2, i * T:(i + 1) * T]
                        if h == 0:
                            ins = ts_(idx[:, t, :], r, wi[:, t, h:h + 1], None, ALU.mult)
                        else:
                            ins = stt(idx[:, t, :], r, wi[:, t, h:h + 1], idx[:, t, :], ALU.mult, ALU.add)
                        n["index"] += 1
                        ins.then_inc(index_added, 1)
                        dve.wait_ge(index_added, n["index"])
                nk = (t + 1) * P
                link(tt(idx[:, t, nk - P:nk], idx[:, t, nk - P:nk], causal, ALU.add))
                m8 = small[:, 100:108]
                src = idx[:, t, 0:nk]
                wk = work[:, t, 0:nk]
                for r in range(TOPK // 8):
                    link(nc.vector.max(m8, src))
                    link(nc.vector.match_replace(wk, m8, src, TAKEN))
                    src = wk
                link(ts_(sel[:, t, 0:nk], wk, TAKEN / 2, NEG, ALU.is_gt, ALU.mult))
                tt(sel[:, t, nk - P:nk], sel[:, t, nk - P:nk], causal, ALU.add).then_inc(dve_made_for_pe, 1)
            units1 = dsa_units()

            def V1(i, b):
                qt, cp, g = units1[i]
                nc.vector.tensor_copy(yT[:, 2 * cp:2 * cp + 2, qt * P:(qt + 1) * P],
                                      b[:, 0:2 * P].rearrange("p (s t) -> p s t", s=2)).then_inc(dve_read, 1)

            attention(len(units1), 2, pr1, HD ** -0.5, lambda i: 2 * (units1[i][0] + 1), sums, negs, None,
                      V1, 2, ADA_AT["attention1"])
            residual(xT, lambda c: mod(1, 2, c))
            norm(xT, hT, xn, std, lambda c: ac(3, c))
            ffn(ADA_AT["ffn1"])
            residual(xT, lambda c: mod(1, 5, c))
            norm(xT, None, xT, std, lambda c: vec("final_norm", c))

            def mixers(layer, stream):
                full_ = stream == 1 or layer == 0
                src = xT if stream else cT
                cond = 0 if stream else 1
                link(scale_cols(4, 2 + layer, 1, cond))
                dve.drain().then_inc(dve_made_for_act, 1)
                norm(src, hT, xn, std, lambda c: ac(4, c))
                if full_:
                    b = job()
                    nc.vector.tensor_copy(fq, b[:, :].rearrange("p (t n) -> p t n", t=NT)).then_inc(dve_read, 1)
                n["from_pe"] += 1
                dve.wait_ge(pe_made_for_dve, n["from_pe"])
                if full_:
                    ts_(lrs[:, 0, :], banks[6][:, 0:T], 1.0 / 256, EPS, ALU.mult, ALU.add)
                else:
                    nc.vector.memset(lrs[:, 0, :], 1.0)
                ts_(lrs[:, 1, :], banks[6][:, T:2 * T], 1.0 / P, EPS, ALU.mult, ALU.add)
                dve.drain().then_inc(dve_made_for_act, 1)
                from_act()
                link(nc.vector.reciprocal(lrs, lrs))
                if full_:
                    for c in range(2):
                        stt(cqT[:, c, :], banks[4][:, c * T:(c + 1) * T], vec("q_lora_norm_2", 2 * layer + c),
                            lrs[:, 0, :], ALU.mult, ALU.mult)
                stt(cqT[:, 2, :], banks[5][:, 0:T], vec("kv_lora_norm_2", layer), lrs[:, 1, :],
                    ALU.mult, ALU.mult)
                ts_(krg, banks[5][:, T:2 * T], vec("k_rope", layer), None, ALU.mult)
                dve.drain().then_inc(dve_made_for_pe, 1)
                if full_:
                    b = job()
                    nc.vector.tensor_copy(wsT, b[:, :]).then_inc(dve_read, 1)
                rope = slot(index[("mla", layer)][stream])[:, 3072:3072 + 2 * T]
                cos, sin = rope[:, 0:T], rope[:, T:2 * T]
                if stream:
                    b = job()
                    tt(ra[:, 0, :], krg, cos, ALU.mult)
                    tt(rb[:, 0, :], b[:, 0:T], sin, ALU.mult).then_inc(dve_read, 1)
                    dve.drain().then_inc(dve_chain, 1)
                    n["chain"] += 1
                    dve.wait_ge(dve_chain, n["chain"])
                    tt(krg, ra[:, 0, :], rb[:, 0, :], ALU.add)
                ms = small[:, 112:114]
                if full_:
                    from_act()
                    ts_(ms, ms, 1.0 / 256, EPS, ALU.mult, ALU.add)
                b = job()
                ts_(rk, b[:, 0:T], 1.0 / QKD, EPS, ALU.mult, ALU.add).then_inc(dve_read, 1)
                dve.drain().then_inc(dve_made_for_act, 1)
                if full_:
                    b = job()
                    ts_(rq, b[:, 0:T], 1.0 / QKD, EPS, ALU.mult, ALU.add).then_inc(dve_read, 1)
                    dve.wait_ge(dve_read, n["dve"])
                    dve.drain().then_inc(dve_made_for_pe, 1)
                    for c in range(2):
                        b = job()
                        nc.vector.tensor_copy(acs[:, :, c, :], b[:, :].rearrange("p (s n) -> p s n", s=2))\
                            .then_inc(dve_read, 1)
                from_act()
                nc.vector.reciprocal(rk, rk).then_inc(dve_made_for_pe, 1)
                if full_:
                    link(nc.vector.reciprocal(ms, ms))
                    dve.wait_ge(row_loads, 16 * (2 + 5 * (layer + 1)))
                    for t in range(NT):
                        stt(vg[:, t, :], vg[:, t, :], ms[:, t:t + 1], sgu_gain, ALU.mult, ALU.mult)
                    dve.drain().then_inc(dve_made_for_pe, 1)
                    b = job()
                    nc.vector.tensor_copy(rqs.rearrange("p (t h) -> p t h", t=NT),
                                          b[:, 0:T].rearrange("p (t h r) -> p t h r", t=NT, h=MH)[:, :, :, 0])\
                        .then_inc(dve_read, 1)
                    dve.drain().then_inc(dve_made_for_act, 1)
                keys = slice(T * stream, T * stream + T)
                for g in range(2):
                    b = job()
                    spread = b[:, :].rearrange("p (c t) -> p c t", c=2)
                    tt(kTn[:, g::2, keys], kTn[:, g::2, keys], spread, ALU.mult)
                    half = slice(g * HD, (g + 1) * HD)
                    tt(kTr[half, :, keys], bc(krg[half], 1, [HD, 2, T]), spread[half], ALU.mult)\
                        .then_inc(dve_read, 1)
                if not full_:
                    return
                from_act()
                link(nc.vector.reciprocal(rqs, rqs))
                ts_(neg_rqs, rqs, -QKD ** -0.5, None, ALU.mult)
                link(ts_(rqs, rqs, QKD ** -0.5, None, ALU.mult))
                if stream:
                    link(tt(ra, qraw, bc(cos, 1, [P, 2, T]), ALU.mult))
                dve.drain().then_inc(dve_made_for_pe, 1)
                b = job()
                sg = qrsq.rearrange("p c (t q) -> p c t q", t=NT)
                for c in range(2):
                    ins = tt(sg[:, c], b[:, c * T:(c + 1) * T].rearrange("p (t q) -> p t q", t=NT),
                             bc(sgu_bias[:, c, :], 1, [P, NT, P]), ALU.add)
                ins.then_inc(dve_read, 1)
                dve.drain().then_inc(dve_chain, 1)
                n["chain"] += 1
                dve.wait_ge(dve_chain, n["chain"])
                tt(yT[:, 0:2, :], qrsq, uT, ALU.mult)
                if stream:
                    b = job()
                    bv = b[:, :].rearrange("p (c t) -> p c t", c=2)
                    tt(rb, bv, bc(sin, 1, [P, 2, T]), ALU.mult).then_inc(dve_read, 1)
                    dve.wait_ge(dve_read, n["dve"])
                    tt(qTr, ra, rb, ALU.add)
                dve.drain().then_inc(dve_made_for_pe, 1)
                for c in range(2):
                    b = job()
                    nc.vector.tensor_copy(yT[:, 2 + c, :], b[:, 0:T]).then_inc(dve_read, 1)
                units2 = mla_units()
                nk = 2 * T if stream else T

                def V2(i, b):
                    qt, h = units2[i]
                    nc.vector.tensor_copy(yT[:, 4 + h, qt * P:(qt + 1) * P], b[:, 0:P]).then_inc(dve_read, 1)

                attention(len(units2), 1, pr2, lambda i: neg_rqs[:, i:i + 1], lambda i: nk // P, sums, negs,
                          None, V2, 1)
                residual(src, lambda c: mod(2 + layer, 2, c, 1, cond), False)

            def route(layer, stream):
                src = xT if stream else cT
                cond = 0 if stream else 1
                link(scale_cols(8, 2 + layer, 4, cond))
                dve.drain().then_inc(dve_made_for_act, 1)
                norm(src, mhT, mxn, mstd)
                aff = small[:, 128:160].rearrange("p (t e) -> p t e", t=NT)
                place = small[:, 160:192].rearrange("p (t e) -> p t e", t=NT)
                m2 = small[:, 100:102]
                b = job()
                lg = b[:, 0:32].rearrange("p (t e) -> p t e", t=NT)
                link(nc.vector.tensor_reduce(m2, lg, X, ALU.max))
                tt(aff, lg, bc(m2, 2, [P, NT, NE]), ALU.subtract).then_inc(dve_read, 1)
                dve.drain().then_inc(dve_made_for_act, 1)
                from_act()
                link(nc.vector.tensor_reduce(m2, aff, X, ALU.add))
                link(nc.vector.reciprocal(m2, m2))
                tt(aff, aff, bc(m2, 2, [P, NT, NE]), ALU.mult).then_inc(dve_made_for_pe, 1)
                b = job()
                arow, wrow, prow = exs
                link(nc.vector.tensor_copy(arow, b[0:NE, 0:T]))
                nc.vector.memset(zrow, 0.0).then_inc(dve_read, 1)
                m8 = small[0:NE, 104:112]
                s_ = arow
                for r in range(CAP // 8):
                    link(nc.vector.max(m8, s_))
                    link(nc.vector.match_replace(wrow, m8, s_, -1.0))
                    s_ = wrow
                link(ts_(arow, wrow, 0.0, None, ALU.is_lt))
                link(nc.vector.tensor_tensor_scan(prow, arow, zrow, 0.0, ALU.add, ALU.add))
                tt(prow, prow, arow, ALU.mult).then_inc(dve_made_for_pe, 1)
                b = job()
                nc.vector.tensor_copy(small[:, 160:192], b[:, 0:32]).then_inc(dve_read, 1)
                dve.drain().then_inc(dve_chain, 1)
                n["chain"] += 1
                dve.wait_ge(dve_chain, n["chain"])
                for t in range(NT):
                    one = pm[:, t, :].rearrange("p (e s) -> p e s", e=NE)
                    wtd = pg[:, t, :].rearrange("p (e s) -> p e s", e=NE)
                    link(tt(one, bc(iota1, 1, [P, NE, CAP]), bc(place[:, t, :], 2, [P, NE, CAP]),
                            ALU.is_equal))
                    ins = tt(wtd, one, bc(aff[:, t, :], 2, [P, NE, CAP]), ALU.mult)
                ins.then_inc(dve_made_for_pe, 1)
                for c in range(0, DC, 2):
                    b = job()
                    ts_(xsT[stream][:, c, :], b[:, :], ac(8, c), mod(2 + layer, 3, c, 1, cond),
                        ALU.mult, ALU.add).then_inc(dve_read, 1)
                for half in range(2):
                    b = job()
                    nc.vector.tensor_copy(pgT[stream][:, 2 * half:2 * half + 2, :],
                                          b[:, :].rearrange("p (g t) -> p g t", g=2)).then_inc(dve_read, 1)
                barrier()

            def experts(layer, streams):
                ns = len(streams)
                base = NG * layer
                base_s = 2 * NG * layer
                if layer == 0:
                    dve.drain().then_inc(y_read, 1)
                with dve.Fori(0, NG) as g:
                    for i, s in enumerate(streams):
                        dve.wait_ge(hid_silu, g * ns + (base_s + i + 1))
                        tt(hid[s], hid[s], banks[2 * s + 1][:, :], ALU.mult).then_inc(hid_ready, 1)
                    dve.wait_ge(y_ready, g + (base + 1))
                    for s in streams:
                        for half in range(2):
                            ins = nc.vector.tensor_copy(
                                ys[s].rearrange("p g d -> p (g d)")[:, bass.ds(g * D + half * 512, 512)],
                                banks[4 + 2 * s + half][:, :])
                    ins.then_inc(y_read, 1)
                barrier()
                for s in streams:
                    if s != streams[0]:
                        barrier()
                    residual((cT, xT)[s], lambda c: mod(2 + layer, 5, c, 1, 1 - s), False)
                barrier()

            for layer in range(LAYERS):
                mixers(layer, 0)
                mixers(layer, 1)
                for s in ((0, 1) if layer == 0 else (1,)):
                    route(layer, s)
                experts(layer, (0, 1) if layer == 0 else (1,))
            for c in range(0, DC, 2):
                job()
                b = banks[c // 2]
                nc.vector.tensor_copy(
                    tok_in[:, :, c * P:(c + 2) * P].rearrange("p t (c q) -> p c t q", c=2),
                    b[:, :].rearrange("p (c t q) -> p c t q", c=2, t=NT)).then_inc(out_copied, 1)


INS = ["x", "c", "l0_norm_mix", "l0_norm_ffn", "l0_mod_w", "l0_mod_b", "l0_w_in", "l0_conv_w",
       "l0_conv_b", "l0_lru_wa", "l0_lru_ba", "l0_lru_wx", "l0_lru_bx", "l0_lru_lambda",
       "l0_cmp_pe_k", "l0_cmp_w1_k", "l0_cmp_w2_k", "l0_cmp_pe_v", "l0_cmp_w1_v", "l0_cmp_w2_v",
       "l0_w_out", "l0_ffn_wg", "l0_ffn_wu", "l0_ffn_wd", "l1_norm_mix", "l1_norm_ffn", "l1_mod_w",
       "l1_mod_b", "l1_w_in", "l1_w_out", "l1_ffn_wg", "l1_ffn_wu", "l1_ffn_wd", "final_norm", "c_2",
       "ctx_2", "c_ctx_2", "w_ada_2", "b_ada_2", "w_in_2", "sgu_norm_2", "w_sgu_2", "b_sgu_2",
       "q_lora_norm_2", "w_uq_2", "kv_lora_norm_2", "w_ukv_2", "q_norm_2", "k_norm_2", "w_out_2",
       "w_router_2", "w_gate_2", "w_up_2", "w_down_2"]


def shape_tables():
    tab = np.zeros((P, C_END), np.float64)
    n = np.arange(T)
    ang = 2 * np.pi * (np.outer(n, n) % T) / T
    dft = np.stack([np.cos(ang), np.sin(ang)], 1) / np.sqrt(T)
    tab[:, C_DFTN:C_DFTN + 1024] = dft.reshape(NT, P, 2 * T).transpose(1, 0, 2).reshape(P, -1)
    d = np.arange(64)
    angd = 2 * np.pi * (np.outer(d, d) % 64) / 64
    for g in range(2):
        o = g * 64
        tab[o:o + 64, C_DFTD + o:C_DFTD + o + 64] = np.cos(angd) / 8
        tab[o:o + 64, C_DFTD + P + o:C_DFTD + P + o + 64] = -np.sin(angd) / 8
    q = np.arange(P)
    tab[:, C_CAUSAL:C_CAUSAL + P] = np.where(q[None, :] > q[:, None], NEG, 0.0)
    blk = np.arange(32)
    for t in range(NT):
        seen = (blk[None, :] * CMP_STRIDE + CMP_LEN - 1 <= (t * P + q)[:, None]) & (blk[None, :] < NBLK)
        tab[:, C_CMP + t * 256:C_CMP + (t + 1) * 256] = np.tile(np.where(seen, 0.0, NEG), (1, 8))
    tab[:, C_IDENT:C_IDENT + P] = np.eye(P)
    tab[:, C_IOTA:C_IOTA + CAP] = np.arange(1, CAP + 1)
    freqs = (np.float32(10000.0) ** (-np.arange(16, dtype=np.float32) / np.float32(16))).astype(np.float32)
    tok = np.arange(T)
    for head in range(2):
        for rc, pos in enumerate((tok // 64, tok % 64)):
            a = (freqs[:, None] * pos[None, :].astype(np.float32)).astype(np.float64)
            for hf in range(2):
                o = head * 64 + rc * 32 + hf * 16
                tab[o:o + 16, C_ROPE:C_ROPE + T] = np.cos(a)
                tab[o:o + 16, C_ROPE + T:C_ROPE + 2 * T] = np.sin(a) * (1 if hf else -1)
    tab[np.arange(P), C_ROPE + 2 * T + (np.arange(P) ^ 16)] = 1
    return tab.astype(np.float32)


def kernel(**inputs):
    import concourse.bacc as bacc
    from concourse.bass_utils import run_bass_kernel_spmd

    nc = bacc.Bacc("TRN2", target_bir_lowering=False, num_devices=1)
    arrays, aps = {}, {}
    for name in INS:
        a = np.ascontiguousarray(inputs[name])
        arrays[f"in_{name}"] = a
        aps[name] = nc.dram_tensor(f"in_{name}", a.shape, mybir.dt.from_np(a.dtype), kind="ExternalInput").ap()
    table = shape_tables()
    arrays["shape_tables"] = table
    aps["shape_tables"] = nc.dram_tensor("shape_tables", table.shape, F32, kind="ExternalInput").ap()
    aps["out"] = nc.dram_tensor("out", (1, T, D), F32, kind="ExternalOutput").ap()
    program(nc, aps)
    r = run_bass_kernel_spmd(nc, [arrays], core_ids=[0])
    return r.results[0]["out"]
```
